# Optimizing a Trainium2 kernel written in Bass

```python
import jax, jax.numpy as jnp
from jax import lax
import numpy as np

D_MODEL = 1024
BATCH = 1
SEQ = 512
DEPTH = 2

GRID_W = 64
CTX_LEN = 256
N_BRANCH = 3
MIX_W = 512
HEAD_DIM = 64
N_HEADS = MIX_W // HEAD_DIM
CONV_WIDTH = 3
D_DECAY_LORA = 64
D_AAA_LORA = 64
D_GATE_LORA = 128
NA_ROWS = 8
NA_COLS = 16
D_FF = -(-(8 * D_MODEL) // (3 * 256)) * 256
ROPE_THETA = 10000.0
EPS = 1e-6
LN_X_EPS = 64e-5
NEG_INF = -1e30

C_CONV = 3 * MIX_W
C_RWKV = 3 * MIX_W + D_DECAY_LORA + D_AAA_LORA
C_ATTN = 3 * MIX_W
C_GATE = N_BRANCH * D_MODEL
D_IN = C_CONV + C_RWKV + D_GATE_LORA + C_ATTN + C_GATE
IN_SPLITS = [C_CONV, C_CONV + C_RWKV, C_CONV + C_RWKV + D_GATE_LORA, C_CONV + C_RWKV + D_GATE_LORA + C_ATTN]
RWKV_SPLITS = [MIX_W, 2 * MIX_W, 3 * MIX_W, 3 * MIX_W + D_DECAY_LORA]

kernel_name = 'hybrid_conv_rwkv7_natten_dit'

def rms_norm(x, g):
    xf = x.astype(jnp.float32)
    y = xf * lax.rsqrt(jnp.mean(xf * xf, axis=-1, keepdims=True) + EPS)
    return (y * g.astype(jnp.float32)).astype(x.dtype)

def heads(t):
    return t.reshape(t.shape[:-1] + (N_HEADS, HEAD_DIM))

def shift_seq(z, offset):
    if offset == 1:
        return jnp.pad(z[:, :-1], ((0, 0), (1, 0), (0, 0)))
    return jnp.pad(z[:, 1:], ((0, 0), (0, 1), (0, 0)))

def short_conv_mixer(u, conv_w):
    b_gate, c_gate, h = jnp.split(u, 3, axis=-1)
    z = c_gate * h
    zc = conv_w[0] * shift_seq(z, 1) + conv_w[1] * z + conv_w[2] * shift_seq(z, -1)
    return b_gate * zc

def rwkv_scan_inputs(z, mu, w0, w2, a0, a2, k_k, k_a):
    f32 = jnp.float32
    per_dir = []
    for d, offset in enumerate((1, -1)):
        zd = z + mu[d] * (shift_seq(z, offset) - z)
        r, k, v, lw, la = jnp.split(zd, RWKV_SPLITS, axis=-1)
        w_log = -jax.nn.softplus(-(w0[d] + jnp.tanh(lw) @ w2[d])) - 0.5
        decay = jnp.exp(-jnp.exp(w_log.astype(f32)))
        a = jax.nn.sigmoid(a0[d] + la @ a2[d])
        kk = heads(k * k_k).astype(f32)
        kk = kk * lax.rsqrt(jnp.maximum(jnp.sum(kk * kk, axis=-1, keepdims=True), 1e-24))
        k = k * (1.0 + (a - 1.0) * k_a)
        seqs = [heads(t).astype(f32) for t in (r, decay, k, v)] + [-kk, kk * heads(a).astype(f32)]
        if d == 1:
            seqs = [jnp.flip(t, axis=1) for t in seqs]
        per_dir.append(seqs)
    return [jnp.stack(pair, axis=0).transpose(2, 0, 1, 3, 4) for pair in zip(*per_dir)]

def wkv_scan(state0, xs, emit):
    def step(S, inp):
        r, w, k, v, a, b = inp
        sa = jnp.einsum('dbhij,dbhj->dbhi', S, a)
        S = S * w[..., None, :] + sa[..., :, None] * b[..., None, :] + v[..., :, None] * k[..., None, :]
        y = jnp.einsum('dbhij,dbhj->dbhi', S, r) if emit else None
        return S, y
    return lax.scan(step, state0, tuple(xs))

def merge_dirs(t):
    return t[:, 0] + jnp.flip(t[:, 1], axis=0)

def rwkv_readout(ys, xs, lg, r_k, g2, lnx_g, lnx_b):
    f32 = jnp.float32
    r, k, v = xs[0], xs[2], xs[3]
    y = merge_dirs(ys)
    bonus = merge_dirs(jnp.sum(r * k * r_k.astype(f32), axis=-1, keepdims=True) * v)
    mean = jnp.mean(y, axis=-1, keepdims=True)
    var = jnp.mean(jnp.square(y - mean), axis=-1, keepdims=True)
    y = (y - mean) * lax.rsqrt(var + LN_X_EPS) * heads(lnx_g).astype(f32) + heads(lnx_b).astype(f32) + bonus
    T, B = y.shape[0], y.shape[1]
    y = y.transpose(1, 0, 2, 3).reshape(B, T, MIX_W).astype(lg.dtype)
    return y * (jax.nn.sigmoid(lg) @ g2)

def axial_rope(x, row, col):
    def rotate(xp, pos):
        half = xp.shape[-1] // 2
        freqs = ROPE_THETA ** (-jnp.arange(half, dtype=jnp.float32) / half)
        ang = pos.astype(jnp.float32)[:, None] * freqs
        cos, sin = jnp.cos(ang)[None, :, None, :], jnp.sin(ang)[None, :, None, :]
        x1, x2 = jnp.split(xp.astype(jnp.float32), 2, axis=-1)
        return jnp.concatenate([x1 * cos - x2 * sin, x1 * sin + x2 * cos], axis=-1)
    rd = HEAD_DIM // 2
    return jnp.concatenate([rotate(x[..., :rd], row), rotate(x[..., rd:], col)], axis=-1).astype(x.dtype)

def neighbourhood_attention(q, k, v, k_ctx, v_ctx, rpb):
    f32 = jnp.float32
    B, T = q.shape[0], q.shape[1]
    rows = T // GRID_W
    kh = min(NA_ROWS, rows)
    band = kh * GRID_W
    scale = HEAD_DIM ** -0.5
    t = jnp.arange(T)
    q_rot = axial_rope(q, t // GRID_W, t % GRID_W).transpose(0, 2, 1, 3)
    k_rot = axial_rope(k, t // GRID_W, t % GRID_W).transpose(0, 2, 1, 3)
    q_pl = q.transpose(0, 2, 1, 3)
    v_l = v.transpose(0, 2, 1, 3)
    kc = k_ctx.transpose(0, 2, 1, 3)
    vc = v_ctx.transpose(0, 2, 1, 3)
    key_col = jnp.arange(band) % GRID_W
    q_col = jnp.arange(GRID_W)
    col_start = jnp.clip(q_col - NA_COLS // 2, 0, GRID_W - NA_COLS)
    in_win = (key_col[None, :] >= col_start[:, None]) & (key_col[None, :] < col_start[:, None] + NA_COLS)
    dc = jnp.clip(key_col[None, :] - q_col[:, None] + NA_COLS - 1, 0, 2 * NA_COLS - 2)

    def row_block(i):
        row_start = jnp.clip(i - kh // 2, 0, rows - kh)
        qi = lax.dynamic_slice_in_dim(q_rot, i * GRID_W, GRID_W, axis=2)
        qpi = lax.dynamic_slice_in_dim(q_pl, i * GRID_W, GRID_W, axis=2)
        kb = lax.dynamic_slice_in_dim(k_rot, row_start * GRID_W, band, axis=2)
        vb = lax.dynamic_slice_in_dim(v_l, row_start * GRID_W, band, axis=2)
        dr = jnp.broadcast_to(row_start + jnp.arange(band) // GRID_W - i + NA_ROWS - 1, (GRID_W, band))
        bias = rpb[:, dr, dc].astype(f32)
        s_lat = jnp.einsum('bhqd,bhkd->bhqk', qi, kb).astype(f32) * scale + bias
        s_lat = jnp.where(in_win, s_lat, NEG_INF)
        s_ctx = jnp.einsum('bhqd,bhkd->bhqk', qpi, kc).astype(f32) * scale
        p = jax.nn.softmax(jnp.concatenate([s_lat, s_ctx], axis=-1), axis=-1).astype(v.dtype)
        return (jnp.einsum('bhqk,bhkd->bhqd', p[..., :band], vb)
                + jnp.einsum('bhqk,bhkd->bhqd', p[..., band:], vc))

    out = lax.map(row_block, jnp.arange(rows))
    return out.transpose(1, 0, 3, 2, 4).reshape(B, T, MIX_W)

def context_attention(q, k, v):
    s = jnp.einsum('blhd,bmhd->bhlm', q, k).astype(jnp.float32) * HEAD_DIM ** -0.5
    p = jax.nn.softmax(s, axis=-1).astype(v.dtype)
    out = jnp.einsum('bhlm,bmhd->blhd', p, v)
    return out.reshape(out.shape[0], out.shape[1], MIX_W)

def merge_branches(gate_u, branches, w_up, w_o):
    gates = jax.nn.sigmoid(gate_u.reshape(gate_u.shape[:-1] + (N_BRANCH, D_MODEL)))
    proj = jnp.einsum('btnm,nmd->btnd', jnp.stack(branches, axis=-2), w_up)
    return jnp.sum(gates * proj, axis=-2) @ w_o

def swiglu(h, w_in, w_out):
    a, b = jnp.split(h @ w_in, 2, axis=-1)
    return (jax.nn.silu(a) * b) @ w_out

def token_mixing(hx, hc, w_in, conv_w, rwkv_mu, rwkv_w0, rwkv_w2, rwkv_a0, rwkv_a2, rwkv_kk, rwkv_ka,
                 rwkv_rk, rwkv_g2, lnx_g, lnx_b, na_rpb, w_up, w_o, with_ctx_out):
    conv_x, rz_x, lg_x, att_x, gate_x = jnp.split(hx @ w_in, IN_SPLITS, axis=-1)
    conv_c, rz_c, lg_c, att_c, gate_c = jnp.split(hc @ w_in, IN_SPLITS, axis=-1)
    a_x = short_conv_mixer(conv_x, conv_w)
    B = hx.shape[0]
    state0 = jnp.zeros((2, B, N_HEADS, HEAD_DIM, HEAD_DIM), jnp.float32)
    xs_c = rwkv_scan_inputs(rz_c, rwkv_mu, rwkv_w0, rwkv_w2, rwkv_a0, rwkv_a2, rwkv_kk, rwkv_ka)
    state_c, ys_c = wkv_scan(state0, xs_c, with_ctx_out)
    xs_x = rwkv_scan_inputs(rz_x, rwkv_mu, rwkv_w0, rwkv_w2, rwkv_a0, rwkv_a2, rwkv_kk, rwkv_ka)
    _, ys_x = wkv_scan(state_c, xs_x, True)
    b_x = rwkv_readout(ys_x, xs_x, lg_x, rwkv_rk, rwkv_g2, lnx_g, lnx_b)
    q_x, k_x, v_x = [heads(t) for t in jnp.split(att_x, 3, axis=-1)]
    q_c, k_c, v_c = [heads(t) for t in jnp.split(att_c, 3, axis=-1)]
    c_x = neighbourhood_attention(q_x, k_x, v_x, k_c, v_c, na_rpb)
    y_x = merge_branches(gate_x, (a_x, b_x, c_x), w_up, w_o)
    if not with_ctx_out:
        return y_x, None
    a_c = short_conv_mixer(conv_c, conv_w)
    b_c = rwkv_readout(ys_c, xs_c, lg_c, rwkv_rk, rwkv_g2, lnx_g, lnx_b)
    c_c = context_attention(q_c, k_c, v_c)
    y_c = merge_branches(gate_c, (a_c, b_c, c_c), w_up, w_o)
    return y_x, y_c

def setup_inputs(seed: int = 0) -> dict:
    key = jax.random.key(seed)
    ks = jax.random.split(key, 26)
    f32 = jnp.float32
    def nrm(k, shape, s):
        return s * jax.random.normal(k, shape, f32)
    return {
        'x': nrm(ks[0], (BATCH, SEQ, D_MODEL), 1.0),
        'c': nrm(ks[1], (BATCH, D_MODEL), 1.0),
        'ctx': nrm(ks[2], (BATCH, CTX_LEN, D_MODEL), 1.0),
        'c_ctx': nrm(ks[3], (D_MODEL,), 1.0),
        'w_ada': nrm(ks[4], (DEPTH, D_MODEL, 6 * D_MODEL), D_MODEL ** -0.5),
        'b_ada': nrm(ks[5], (DEPTH, 6 * D_MODEL), 0.01),
        'norm_g': 1.0 + nrm(ks[6], (DEPTH, 4, D_MODEL), 0.05),
        'w_in': nrm(ks[7], (DEPTH, D_MODEL, D_IN), D_MODEL ** -0.5),
        'conv_w': nrm(ks[8], (DEPTH, CONV_WIDTH, MIX_W), CONV_WIDTH ** -0.5),
        'rwkv_mu': jax.random.uniform(ks[9], (DEPTH, 2, C_RWKV), f32, 0.0, 1.0),
        'rwkv_w0': jax.random.uniform(ks[10], (DEPTH, 2, MIX_W), f32, -6.0, 0.0),
        'rwkv_w2': nrm(ks[11], (DEPTH, 2, D_DECAY_LORA, MIX_W), 0.1 * D_DECAY_LORA ** -0.5),
        'rwkv_a0': nrm(ks[12], (DEPTH, 2, MIX_W), 0.1),
        'rwkv_a2': nrm(ks[13], (DEPTH, 2, D_AAA_LORA, MIX_W), 0.5 * D_AAA_LORA ** -0.5),
        'rwkv_kk': 0.85 + nrm(ks[14], (DEPTH, MIX_W), 0.05),
        'rwkv_ka': 1.0 + nrm(ks[15], (DEPTH, MIX_W), 0.05),
        'rwkv_rk': nrm(ks[16], (DEPTH, N_HEADS, HEAD_DIM), 0.1),
        'rwkv_g2': nrm(ks[17], (DEPTH, D_GATE_LORA, MIX_W), D_GATE_LORA ** -0.5),
        'lnx_g': 1.0 + nrm(ks[18], (DEPTH, MIX_W), 0.05),
        'lnx_b': nrm(ks[19], (DEPTH, MIX_W), 0.01),
        'na_rpb': nrm(ks[20], (DEPTH, N_HEADS, 2 * NA_ROWS - 1, 2 * NA_COLS - 1), 0.1),
        'w_up': nrm(ks[21], (DEPTH, N_BRANCH, MIX_W, D_MODEL), MIX_W ** -0.5),
        'w_o': nrm(ks[22], (DEPTH, D_MODEL, D_MODEL), D_MODEL ** -0.5),
        'w_ffn_in': nrm(ks[23], (DEPTH, D_MODEL, 2 * D_FF), D_MODEL ** -0.5),
        'w_ffn_out': nrm(ks[24], (DEPTH, D_FF, D_MODEL), D_FF ** -0.5),
    }

def reference(x, c, ctx, c_ctx, w_ada, b_ada, norm_g, w_in, conv_w, rwkv_mu, rwkv_w0, rwkv_w2, rwkv_a0,
              rwkv_a2, rwkv_kk, rwkv_ka, rwkv_rk, rwkv_g2, lnx_g, lnx_b, na_rpb, w_up, w_o, w_ffn_in, w_ffn_out):
    for l in range(DEPTH):
        with_ctx_out = l < DEPTH - 1
        mod_x = (jax.nn.silu(c) @ w_ada[l] + b_ada[l])[:, None, :]
        mod_c = jax.nn.silu(c_ctx) @ w_ada[l] + b_ada[l]
        sh1, sc1, gate1, sh2, sc2, gate2 = jnp.split(mod_x, 6, axis=-1)
        csh1, csc1, cgate1, csh2, csc2, cgate2 = jnp.split(mod_c, 6, axis=-1)
        hx = rms_norm(x, norm_g[l, 0]) * (1.0 + sc1) + sh1
        hc = rms_norm(ctx, norm_g[l, 0]) * (1.0 + csc1) + csh1
        y_x, y_c = token_mixing(hx, hc, w_in[l], conv_w[l], rwkv_mu[l], rwkv_w0[l], rwkv_w2[l], rwkv_a0[l],
                                rwkv_a2[l], rwkv_kk[l], rwkv_ka[l], rwkv_rk[l], rwkv_g2[l], lnx_g[l], lnx_b[l],
                                na_rpb[l], w_up[l], w_o[l], with_ctx_out)
        x = x + gate1 * rms_norm(y_x, norm_g[l, 1])
        hx = rms_norm(x, norm_g[l, 2]) * (1.0 + sc2) + sh2
        x = x + gate2 * rms_norm(swiglu(hx, w_ffn_in[l], w_ffn_out[l]), norm_g[l, 3])
        if with_ctx_out:
            ctx = ctx + cgate1 * rms_norm(y_c, norm_g[l, 1])
            hc = rms_norm(ctx, norm_g[l, 2]) * (1.0 + csc2) + csh2
            ctx = ctx + cgate2 * rms_norm(swiglu(hc, w_ffn_in[l], w_ffn_out[l]), norm_g[l, 3])
    return x


_drawn_inputs = setup_inputs


def setup_inputs(seed=0):
    import zlib

    import numpy as np

    out = dict(_drawn_inputs(seed))
    spreads = {}
    factors = {'rwkv_w2': 8.0, 'rwkv_a0': 5.367, 'lnx_g': 6.225, 'lnx_b': 46.086, 'na_rpb': 24.054}
    for name, (base, spread) in spreads.items():
        noise = np.random.default_rng([zlib.crc32(name.encode()), seed]).standard_normal(out[name].shape)
        drawn = base * np.exp(spread * noise) if base else spread * noise
        out[name] = __import__('jax').numpy.asarray(drawn.astype(out[name].dtype))
    for name, factor in factors.items():
        out[name] = (out[name] * factor).astype(out[name].dtype)
    return out
```

```python
import math
from contextlib import ExitStack

import numpy as np
import concourse.bass as bass
from concourse import mybir

D, SEQ, CTX, DEPTH, MIX, HD, FF = 1024, 512, 256, 2, 512, 64, 2816
P = 128
T = CTX + SEQ
GW, GR = 64, SEQ // 64
NROW, NCOL = 8, 16
KD, KM, NJ = D // P, MIX // P, FF // P
HP = MIX // P
CHUNK = 64
NBLK = T // P
SEGS = [(0, CTX), (CTX, T)]
DSEG = [[(0, CTX), (CTX, T)], [(SEQ, T), (0, SEQ)]]
QCOLS = 16
KCOLS = 32
KEY0 = [0, 8, 24, 32]
VCOL0 = [0, 16, 8, 24, 40, 32, 48]
VARIANT = [0, 1, 1, 2]
RPB = (2 * NROW - 1) * (2 * NCOL - 1)
RPB_PAD = 16
BX = 48
DECAY = math.exp(-0.5)
EPS, LN_EPS = 1e-6, 64e-5
V_NG, V_CW, V_MU, V_MUL, V_W0, V_A0 = 0, 32, 44, 68, 70, 78
V_KK, V_KA, V_RK, V_LG, V_LB, V_BA = 86, 90, 94, 98, 102, 106
NV = V_BA + 48


def constants():
    i = np.arange(P)
    same = (i[:, None] // HD == i[None, :] // HD)
    eye = np.eye(P, dtype=np.float32)
    perm = np.zeros((P, P), np.float32)
    perm[i, (i // 32) * 32 + (i + 16) % 32] = 1.0
    glob = np.concatenate([eye, np.full((P, P), 1.0 / D), same, perm], 1).astype(np.float32)
    s, t = i[:, None], i[None, :]
    chunk = s // CHUNK == t // CHUNK
    gram = [np.concatenate([chunk & (s < t), chunk & (s <= t)], 1), np.concatenate([chunk & (s > t), chunk & (s >= t)], 1)]
    merge = []
    for m in (1, 2, 4, 8, 16, 32):
        low = (s // (2 * m) == t // (2 * m)) & (s // m > t // m)
        merge.append(low)
    lows = np.concatenate(merge, 1)
    ups = np.concatenate([x.T for x in merge], 1)
    tok = np.arange(T)
    resets = [np.broadcast_to(tok % CHUNK != 0, (P, T)), np.broadcast_to(tok % CHUNK != CHUNK - 1, (P, T))]
    rwkv = np.concatenate(gram + [lows, ups] + resets, 1).astype(np.float32)
    tt = np.arange(SEQ)
    freq = 10000.0 ** (-np.arange(16, dtype=np.float32) / 16)
    pos = np.where((i % HD < 32)[:, None], (tt // GW)[None, :], (tt % GW)[None, :]).astype(np.float32)
    ang = pos * freq[i % 16][:, None].astype(np.float32)
    sign = np.where(i % 32 < 16, -1.0, 1.0)[:, None]
    neg = []
    for g in (0, 1, 3):
        qc = QCOLS * g + 15 - i // GR
        kc = KEY0[g] + np.arange(KCOLS * GR) // GR
        start = np.clip(qc - NCOL // 2, 0, GW - NCOL)
        win = (kc[None, :] >= start[:, None]) & (kc[None, :] < start[:, None] + NCOL)
        neg.append(np.where(win, 0.0, -1e30))
    attn = np.concatenate([np.cos(ang), np.sin(ang) * sign] + neg, 1).astype(np.float32)
    return glob, rwkv, attn


class Count:

    def __init__(self, sem, passes=1, per=1, primed=0):
        self.sem, self.passes, self.per, self.primed = sem, passes, per, primed
        self.total = primed + passes * per

    def ready(self, use, i, k=1):
        return i * self.per + (use * self.total + self.primed + k)

    def free(self, use, i, k=1):
        return i * self.per + (use * self.total + k)


def program(nc, a, debug=None):
    F = mybir.dt.float32
    ALU = mybir.AluOpType
    ACT = mybir.ActivationFunctionType
    AX = mybir.AxisListType.X
    ctx = ExitStack()
    with ctx:
        def sb(name, n):
            return ctx.enter_context(nc.sbuf_tensor(name, [P, n], F))

        def sem(name):
            return ctx.enter_context(nc.semaphore(name))

        glob = sb("glob", 4 * P)
        IDENT, MEAN_D, SAME, PERM = [glob[:, j * P:(j + 1) * P] for j in range(4)]
        vec = sb("vec", NV)
        cin = sb("cin", KD * 2)
        mod = sb("mod", 48 * 2)
        der = sb("der", 4 * KD * 2)
        one = sb("one", 4)
        resid = sb("resid", KD * T)
        hx = sb("hx", KD * T)
        slots = [sb(f"slot{s}", 18 * P) for s in range(2)]
        NA_ = 9216 + 25600
        arena = sb("arena", NA_)
        bank = [ctx.enter_context(nc.psum_tensor(f"bank{i}", [P, 512], F)) for i in range(8)]

        RES = resid[:, :].rearrange("p (k t) -> p k t", k=KD)
        HX = hx[:, :].rearrange("p (k t) -> p k t", k=KD)
        CIN = cin[:, :].rearrange("p (k s) -> p k s", s=2)
        MOD = mod[:, :].rearrange("p (j s) -> p j s", s=2)
        DER = der[:, :].rearrange("p (n k s) -> p n k s", n=4, s=2)

        class Carve:

            def __init__(self, at):
                self.at = at

            def __call__(self, n):
                self.at += n
                assert self.at <= NA_, self.at
                return arena[:, self.at - n:self.at]

        BR = arena[:, 0:3 * HP * T].rearrange("p (n k t) -> p n k t", n=3, k=HP)
        WS0 = 3 * HP * T

        norm_ws = Carve(NA_ - 5 * T)
        NSQ = [norm_ws(T), norm_ws(T)]
        NRS = norm_ws(T)
        NTMP = [norm_ws(T), norm_ws(T)]

        s_load = sem("loaded_constants")
        s_wload = sem("loaded_layer_tables")
        s_out = sem("output_stored")
        phase_end = sem("engines_at_phase_end")
        slab_full = [sem("slab_full_0"), sem("slab_full_1")]
        slab_used = sem("slab_used")
        silu_done = sem("silu_done")
        ada_prod = Count(sem("ada_products"), 12)
        ada_copy = Count(sem("ada_copied"), 12, primed=1)
        ada_scales = sem("ada_scales")
        sq_made = Count(sem("squares_made"), 8)
        sq_used = Count(sem("squares_used"), 8)
        rs_made = sem("rms_made")
        ap_scaled = Count(sem("norm_scaled"), 4, 2)
        ap_shift = Count(sem("norm_shifted"), 4, 2, primed=2)

        segs_of = lambda l, all_tokens=False: [0, 1] if (l == 0 or all_tokens) else [1]
        nbar = {}
        PHASES = 10
        TOTAL_BARRIERS = PHASES * DEPTH

        def phase_barrier(e, name):
            nbar[name] = nbar.get(name, 0) + 1
            e.drain().then_inc(phase_end, 1)
            e.wait_ge(phase_end, 4 * nbar[name])

        LOADS = []
        LOADS.append(("w_ada", 12, 16 * P))
        LOADS.append(("w_conv", 4, 12 * P))
        LOADS.append(("w_lora", 1, 8 * P))
        LOADS.append(("w_heads", HP, 14 * P))
        LOADS.append(("w_att", 3, 16 * P))
        LOADS.append(("w_merge", KD, 18 * P))
        LOADS.append(("w_out", 2, 16 * P))
        LOADS.append(("w_ffn_in", NJ // 2, 16 * P))
        LOADS.append(("w_ffn_out", KD, 11 * P))
        first_pass, n = {}, 0
        for l in range(DEPTH):
            for name, passes, _ in LOADS:
                first_pass[l, name] = n
                n += passes

        def wait_slab(pe, l, name, i, s):
            pe.wait_ge(slab_full[s], i * 16 + (first_pass[l, name] + 1) * 16)

        def block(n_in_slab, idx):
            s, j = divmod(idx, n_in_slab)
            return slots[s][:, j * P:(j + 1) * P]

        def products(outs, blocks, rhs, segs):
            for s in segs:
                for k, w in enumerate(blocks):
                    last = nc.tensor.matmul(outs[s], w, rhs(k, s), start=(k == 0), stop=(k == len(blocks) - 1))
            return last

        def hx_rhs(k, s):
            return HX[:, k, SEGS[s][0]:SEGS[s][1]]

        def pair(i, width=(CTX, SEQ)):
            return [bank[i][:, 0:width[0]], bank[i + 1][:, 0:width[1]]]

        def sync_program(sp):
            for l in range(DEPTH):
                for name, passes, cols in LOADS:
                    with sp.Fori(0, passes) as i:
                        for s in range(2):
                            sp.wait_ge(slab_used, i * 2 + (2 * first_pass[l, name] + s + 1))
                            sp.dma_start(slots[s][:, 0:cols], a[name][l, bass.ds(i * 2 + s, 1), :, :].rearrange("a p n -> p (a n)"))\
                              .then_inc(slab_full[s], 16)

        def ada_pe(pe, l):
            if l == 0:
                pe.wait_ge(silu_done, 1)
            with pe.Fori(0, 12) as i:
                pe.wait_ge(ada_copy.sem, ada_copy.free(l, i))
                for s in range(2):
                    wait_slab(pe, l, "w_ada", i, s)
                    for t in range(2):
                        for k in range(KD):
                            last = nc.tensor.matmul(bank[0][:, 4 * s + 2 * t:4 * s + 2 * t + 2], slots[s][:, (t * KD + k) * P:(t * KD + k + 1) * P],
                                                    CIN[:, k, :], start=(k == 0), stop=(k == KD - 1))
                    last.then_inc(slab_used, 1)
                nc.tensor.drain().then_inc(ada_prod.sem, 1)

        def ada_dve(dve, l):
            dve.wait_ge(s_wload, 16 * (l + 1))
            dve.sem_inc(ada_copy.sem, 1)
            with dve.Fori(0, 12) as i:
                dve.wait_ge(ada_prod.sem, ada_prod.ready(l, i))
                nc.vector.tensor_tensor(MOD[:, bass.ds(i * 4, 4), :], bank[0][:, 0:8].rearrange("p (j s) -> p j s", s=2),
                                        vec[:, bass.ds(i * 4 + V_BA, 4)].unsqueeze(2).to_broadcast([P, 4, 2]), ALU.add)\
                         .then_inc(ada_copy.sem, 1)
            dve.drain()
            for n, (part, is_scale) in enumerate([(1, True), (2, False), (4, True), (5, False)]):
                g = vec[:, V_NG + n * KD:V_NG + (n + 1) * KD].unsqueeze(2).to_broadcast([P, KD, 2])
                nc.vector.scalar_tensor_tensor(out=DER[:, n], in0=MOD[:, part * KD:(part + 1) * KD, :], scalar=1.0 if is_scale else 0.0,
                                               in1=g, op0=ALU.add, op1=ALU.mult)
            dve.drain()

        def stats_act(act, use, src, segs):
            lo, hi = SEGS[segs[0]][0], T
            for k in range(KD):
                if k >= 2:
                    act.wait_ge(sq_used.sem, sq_used.ready(use, k - 2))
                nc.scalar.activation(NSQ[k % 2][:, lo:hi], src(k)[:, lo:hi], ACT.Square).then_inc(sq_made.sem, 1)
            act.wait_ge(sq_used.sem, sq_used.ready(use, KD - 1))
            for s in segs:
                nc.scalar.activation(NRS[:, SEGS[s][0]:SEGS[s][1]], pair(0)[s], ACT.Ln, bias=one[:, 0:1])
            act.drain()
            nc.scalar.activation(NRS[:, lo:hi], NRS[:, lo:hi], ACT.Exp, scale=-0.5).then_inc(rs_made, 1)

        def stats_pe(pe, use, segs):
            for k in range(KD):
                pe.wait_ge(sq_made.sem, sq_made.ready(use, k))
                for s in segs:
                    last = nc.tensor.matmul(pair(0)[s], MEAN_D, NSQ[k % 2][:, SEGS[s][0]:SEGS[s][1]], start=(k == 0), stop=(k == KD - 1))
                last.then_inc(sq_used.sem, 1)

        def norm_dve(dve, use, half, segs):
            lo = SEGS[segs[0]][0]
            dve.wait_ge(rs_made, 2 * use + 1)
            with dve.Fori(0, KD // 2) as i:
                for b in range(2):
                    dve.wait_ge(ap_shift.sem, ap_shift.free(use, i, b + 1))
                    nc.vector.tensor_tensor(NTMP[b][:, lo:T], RES[:, bass.ds(i * 2 + b, 1), lo:T].rearrange("p a t -> p (a t)"), NRS[:, lo:T], ALU.mult)\
                      .then_inc(ap_scaled.sem, 1)

        def norm_act(act, use, half, segs):
            act.sem_inc(ap_shift.sem, 2)
            with act.Fori(0, KD // 2) as i:
                for b in range(2):
                    act.wait_ge(ap_scaled.sem, ap_scaled.ready(use, i, b + 1))
                    for s in segs:
                        gain = der[:, bass.ds((i * 2 + b) * 2 + (half * 2 * KD * 2 + s), 1)]
                        shift = mod[:, bass.ds((i * 2 + b) * 2 + (half * 3 * KD * 2 + s), 1)]
                        last = nc.scalar.activation(HX[:, bass.ds(i * 2 + b, 1), SEGS[s][0]:SEGS[s][1]].rearrange("p a t -> p (a t)"),
                                                    NTMP[b][:, SEGS[s][0]:SEGS[s][1]], ACT.Identity, bias=shift, scale=gain)
                    last.then_inc(ap_shift.sem, 1)

        def add_dve(dve, use, half, segs, Y):
            lo = SEGS[segs[0]][0]
            dve.wait_ge(rs_made, 2 * use + 2)
            with dve.Fori(0, KD) as k:
                nc.vector.tensor_tensor(NTMP[0][:, lo:T], Y[:, bass.ds(k, 1), lo:T].rearrange("p a t -> p (a t)"), NRS[:, lo:T], ALU.mult)
                dve.drain()
                for s in segs:
                    x = RES[:, bass.ds(k, 1), SEGS[s][0]:SEGS[s][1]].rearrange("p a t -> p (a t)")
                    nc.vector.scalar_tensor_tensor(out=x, in0=NTMP[0][:, SEGS[s][0]:SEGS[s][1]],
                                                   scalar=der[:, bass.ds(k * 2 + ((half * 2 + 1) * KD * 2 + s), 1)], in1=x, op0=ALU.mult, op1=ALU.add)
                dve.drain()

        conv_prod = Count(sem("conv_products"), HP, 3)
        cg_copied = Count(sem("conv_c_gate_copied"), HP, 1, primed=1)
        z_made = Count(sem("conv_z_made"), HP, 1, primed=1)
        conv_made = Count(sem("conv_made"), HP, 1, primed=1)
        cw = Carve(WS0)
        ZP = cw(T + 3)
        CG, CA = cw(T), cw(T)
        ZSEG = [(1, 1 + CTX), (2 + CTX, 2 + T)]

        def conv_pe(pe, l):
            segs = segs_of(l)
            with pe.Fori(0, HP) as i:
                for t, (b, freed) in enumerate([(4, z_made), (2, cg_copied), (0, conv_made)]):
                    for s in sorted({t * KD // 12, (t * KD + KD - 1) // 12}) if t != 1 else [1]:
                        wait_slab(pe, l, "w_conv", i, s)
                    pe.wait_ge(freed.sem, freed.free(l, i))
                    last = products(pair(b), [block(12, t * KD + k) for k in range(KD)], hx_rhs, segs)
                    last.then_inc(conv_prod.sem, 1)
                nc.tensor.drain().then_inc(slab_used, 2)

        def conv_act(act, l):
            act.sem_inc(cg_copied.sem, 1)
            with act.Fori(0, HP) as i:
                act.wait_ge(conv_prod.sem, conv_prod.ready(l, i, 2))
                act.wait_ge(z_made.sem, z_made.free(l, i))
                for s in segs_of(l):
                    last = nc.scalar.activation(CG[:, SEGS[s][0]:SEGS[s][1]], pair(2)[s], ACT.Copy)
                last.then_inc(cg_copied.sem, 1)

        def conv_dve(dve, l):
            nc.vector.memset(ZP, 0.0)
            dve.drain()
            dve.sem_inc(z_made.sem, 1)
            dve.sem_inc(conv_made.sem, 1)
            with dve.Fori(0, HP) as i:
                dve.wait_ge(cg_copied.sem, cg_copied.ready(l, i))
                dve.wait_ge(conv_prod.sem, conv_prod.ready(l, i, 2))
                for s in segs_of(l):
                    last = nc.vector.tensor_tensor(ZP[:, ZSEG[s][0]:ZSEG[s][1]], pair(4)[s], CG[:, SEGS[s][0]:SEGS[s][1]], ALU.mult)
                last.then_inc(z_made.sem, 1)
                dve.drain()
                w = [vec[:, bass.ds(i + (V_CW + j * HP), 1)] for j in range(3)]
                for s in segs_of(l):
                    (c0, c1), (z0, z1) = SEGS[s], ZSEG[s]
                    nc.vector.tensor_scalar(CA[:, c0:c1], ZP[:, z0:z1], w[1], None, ALU.mult)
                dve.drain()
                for j, off in ((0, -1), (2, 1)):
                    for s in segs_of(l):
                        (c0, c1), (z0, z1) = SEGS[s], ZSEG[s]
                        nc.vector.scalar_tensor_tensor(out=CA[:, c0:c1], in0=ZP[:, z0 + off:z1 + off], scalar=w[j], in1=CA[:, c0:c1], op0=ALU.mult, op1=ALU.add)
                    dve.drain()
                dve.wait_ge(conv_prod.sem, conv_prod.ready(l, i, 3))
                for s in segs_of(l):
                    c0, c1 = SEGS[s]
                    last = nc.vector.tensor_tensor(BR[:, 0, bass.ds(i, 1), c0:c1].rearrange("p a t -> p (a t)"), pair(0)[s], CA[:, c0:c1], ALU.mult)
                last.then_inc(conv_made.sem, 1)

        rw = Carve(2 * HP * T)
        RC = rw(2 * 256 + 2 * 6 * P + 2 * T)
        GMASK = [RC[:, 0:256], RC[:, 256:512]]
        LOWER = [RC[:, 512 + j * P:512 + (j + 1) * P] for j in range(6)]
        UPPER = [RC[:, 512 + (6 + j) * P:512 + (7 + j) * P] for j in range(6)]
        KEEP = [RC[:, 512 + 12 * P:512 + 12 * P + T], RC[:, 512 + 12 * P + T:512 + 12 * P + 2 * T]]
        RW_N = 512 + 12 * P + 2 * T
        ZL = rw(T + 3)
        LD = rw(2 * T).rearrange("p (d t) -> p d t", d=2)
        SG, GT, BONUS = rw(T), rw(T), rw(T)
        DD = [rw(NBLK * 5 * P).rearrange("p (b o t) -> p b o t", b=NBLK, o=5) for _ in range(2)]
        YD = rw(2 * T).rearrange("p (d t) -> p d t", d=2)
        DC = rw(2 * 2 * NBLK).rearrange("p (d c) -> p d c", d=2)
        ARZ = [rw(512).rearrange("p (h o t) -> p h o t", h=2, o=2) for _ in range(2)]
        BKC = [rw(512).rearrange("p (c o t) -> p c o t", c=2, o=2) for _ in range(2)]
        alias = rw.at
        ZR = [rw(T + 3) for _ in range(3)]
        TMP = [rw(T) for _ in range(8)]
        end_a = rw.at
        rw.at = alias
        STG = [rw(640).rearrange("p (o t) -> p o t", o=5) for _ in range(2)]
        VT = [rw(P) for _ in range(2)]
        NAK = [[rw(512).rearrange("p (h o t) -> p h o t", h=2, o=2) for _ in range(2)] for _ in range(2)]
        XX = [rw(512).rearrange("p (x h t) -> p x h t", x=2, h=2) for _ in range(2)]
        T1 = [rw(256).rearrange("p (h t) -> p h t", h=2) for _ in range(2)]
        WR = [rw(256).rearrange("p (h o j) -> p h o j", h=2, o=2) for _ in range(2)]
        ZQ = [rw(256).rearrange("p (o h j) -> p o h j", o=2, h=2) for _ in range(2)]
        GS = [rw(P) for _ in range(2)]
        MH = [rw(256).rearrange("p (c t) -> p c t", c=2) for _ in range(2)]
        HDD = [rw(256).rearrange("p (c t) -> p c t", c=2) for _ in range(2)]
        ST = [rw(P) for _ in range(2)]
        DCS = [rw(2) for _ in range(2)]

        rw_tables = sem("rwkv_tables_loaded")
        lora_prod = sem("lora_products")
        lora_copy = sem("lora_copied")
        lora_mix = sem("lora_mixed")
        lora_act = sem("lora_activated")
        hp_prod = Count(sem("head_products"), HP, 4)
        hp_copy = Count(sem("head_copied"), HP, 2)
        pre_prod = Count(sem("prep_products"), HP, 2 * 3)
        pre_act = Count(sem("prep_activations"), HP, 2 * 4)
        pre_dve = Count(sem("prep_vector"), HP, 2 * 4)
        NPE, NDV, NAC = 16, 15, 5
        blk_pe = [Count(sem(f"block_products_{n}"), HP * NBLK, NPE) for n in ("fwd", "bwd")]
        blk_dve = [Count(sem(f"block_vector_{n}"), HP * NBLK, NDV, primed=1) for n in ("fwd", "bwd")]
        blk_act = [Count(sem(f"block_copies_{n}"), HP * NBLK, NAC) for n in ("fwd", "bwd")]
        post_dve = Count(sem("readout_vector"), HP, 2)
        post_pe = Count(sem("readout_products"), HP, 2)
        post_act = Count(sem("readout_activations"), HP, 2)

        def lora_pe(pe, l):
            for t in range(2):
                wait_slab(pe, l, "w_lora", 0, t)
                products(pair(2 * t), [slots[t][:, k * P:(k + 1) * P] for k in range(KD)], hx_rhs, [0, 1]).then_inc(lora_prod, 1)
            nc.tensor.drain().then_inc(slab_used, 2)

        def lora_act_(act, l):
            act.wait_ge(lora_mix, 3 * l + 1)
            act.wait_ge(lora_prod, 2 * l + 1)
            for s in range(2):
                nc.scalar.activation(ZL[:, ZSEG[s][0]:ZSEG[s][1]], pair(0)[s], ACT.Copy)
            act.drain().then_inc(lora_copy, 1)
            act.wait_ge(lora_prod, 2 * l + 2)
            for s in range(2):
                nc.scalar.activation(SG[:, SEGS[s][0]:SEGS[s][1]], pair(2)[s], ACT.Sigmoid)
            for d in range(2):
                act.wait_ge(lora_mix, 3 * l + 2 + d)
                last = nc.scalar.activation(LD[0:64, d, :], LD[0:64, d, :], ACT.Tanh)
            last.then_inc(lora_act, 1)

        def mix_ops(dve, Z, mu, d, out):
            off = -1 if d == 0 else 1
            for s in range(2):
                (z0, z1), (o0, o1) = ZSEG[s], DSEG[d][s]
                nc.vector.tensor_tensor(out[:, o0:o1], Z[:, z0 + off:z1 + off], Z[:, z0:z1], ALU.subtract)
            dve.drain()
            for s in range(2):
                (z0, z1), (o0, o1) = ZSEG[s], DSEG[d][s]
                last = nc.vector.scalar_tensor_tensor(out=out[:, o0:o1], in0=out[:, o0:o1], scalar=mu, in1=Z[:, z0:z1], op0=ALU.mult, op1=ALU.add)
            return last

        def lora_dve(dve, l):
            for z in [ZL] + ARZ_FLAT:
                nc.vector.memset(z, 0.0)
            dve.drain().then_inc(lora_mix, 1)
            dve.wait_ge(lora_copy, l + 1)
            for d in range(2):
                mix_ops(dve, ZL, vec[:, V_MUL + d:V_MUL + d + 1], d, LD[:, d, :]).then_inc(lora_mix, 1)
            nc.vector.tensor_scalar(OMKA, vec[:, V_KA:V_KA + HP], -1.0, 1.0, ALU.mult, ALU.add)

        ARZ_FLAT = [x.rearrange("p h o t -> p (h o t)") for x in ARZ + BKC]
        omka = sb("omka", HP)
        OMKA = omka[:, :]

        def blocked(x):
            return x.rearrange("p (b t) -> p b t", b=NBLK)

        def heads_pe(pe, l, hp):
            wait_slab(pe, l, "w_heads", hp, 0)
            for t in range(3):
                if t == 1:
                    wait_slab(pe, l, "w_heads", hp, 1)
                products(pair(2 * t), [block(14, t * KD + k) for k in range(KD)], hx_rhs, [0, 1]).then_inc(hp_prod.sem, 1)
            products(pair(6), [block(14, 26)], lambda k, s: SG[:, SEGS[s][0]:SEGS[s][1]], [0, 1]).then_inc(hp_prod.sem, 1)
            pe.wait_ge(hp_copy.sem, hp_copy.ready(l, hp, 1))
            for d in range(2):
                if d == 1:
                    pe.wait_ge(pre_act.sem, pre_act.ready(l, hp, 2 + 1))
                w = block(14, 24 + d)
                for rows, b in ((slice(0, 64), 0), (slice(64, 128), 2)):
                    for s in range(2):
                        o0, o1 = DSEG[d][s]
                        last = nc.tensor.matmul(pair(b)[s], w[rows], LD[rows, d, o0:o1], start=True, stop=True)
                last.then_inc(pre_prod.sem, 1)
                pe.wait_ge(pre_act.sem, pre_act.ready(l, hp, 4 * d + 2))
                for s in range(2):
                    o0, o1 = DSEG[d][s]
                    last = nc.tensor.matmul(pair(4)[s], SAME, TMP[6][:, o0:o1], start=True, stop=True)
                last.then_inc(pre_prod.sem, 1)
                pe.wait_ge(pre_dve.sem, pre_dve.ready(l, hp, 4 * d + 3))
                pe.wait_ge(hp_copy.sem, hp_copy.ready(l, hp, 2))
                for s in range(2):
                    o0, o1 = DSEG[d][s]
                    last = nc.tensor.matmul(pair(6)[s], SAME, TMP[6][:, o0:o1], start=True, stop=True)
                last.then_inc(pre_prod.sem, 1)
            nc.tensor.drain().then_inc(slab_used, 2)

        def heads_act(act, l, hp):
            act.wait_ge(zr_clear.sem, zr_clear.ready(l, hp))
            for t in range(3):
                act.wait_ge(hp_prod.sem, hp_prod.ready(l, hp, t + 1))
                for s in range(2):
                    nc.scalar.activation(ZR[t][:, ZSEG[s][0]:ZSEG[s][1]], pair(2 * t)[s], ACT.Copy)
            act.drain().then_inc(hp_copy.sem, 1)
            act.wait_ge(hp_prod.sem, hp_prod.ready(l, hp, 4))
            for s in range(2):
                nc.scalar.activation(GT[:, SEGS[s][0]:SEGS[s][1]], pair(6)[s], ACT.Copy)
            act.drain().then_inc(hp_copy.sem, 1)
            for d in range(2):
                act.wait_ge(pre_prod.sem, pre_prod.ready(l, hp, 3 * d + 1))
                if d == 1:
                    act.wait_ge(pre_dve.sem, pre_dve.ready(l, hp, 4))
                for s in range(2):
                    o0, o1 = DSEG[d][s]
                    nc.scalar.activation(TMP[3][:, o0:o1], pair(0)[s], ACT.Sigmoid, bias=vec[:, bass.ds(hp + (V_W0 + d * HP), 1)])
                    nc.scalar.activation(TMP[5][:, o0:o1], pair(2)[s], ACT.Sigmoid, bias=vec[:, bass.ds(hp + (V_A0 + d * HP), 1)])
                act.drain().then_inc(pre_act.sem, 1)
                act.wait_ge(pre_dve.sem, pre_dve.ready(l, hp, 4 * d + 1))
                nc.scalar.activation(TMP[6], TMP[7], ACT.Square).then_inc(pre_act.sem, 1)
                act.wait_ge(pre_dve.sem, pre_dve.ready(l, hp, 4 * d + 2))
                nc.scalar.activation(TMP[6], TMP[6], ACT.Ln)
                act.drain()
                nc.scalar.activation(TMP[6], TMP[6], ACT.Exp, scale=-0.5)
                nc.scalar.activation(E3, E3, ACT.Exp, scale=-DECAY)
                nc.scalar.activation(E2, TMP[4], ACT.Exp, scale=DECAY)
                act.drain()
                nc.scalar.activation(TMP[4], TMP[4], ACT.Exp, scale=-DECAY).then_inc(pre_act.sem, 1)
                act.drain()
                last_tok = TMP[4].rearrange("p (c t) -> p c t", t=CHUNK)[:, :, CHUNK - 1 if d == 0 else 0]
                nc.scalar.activation(DC[:, d, :], last_tok, ACT.Copy).then_inc(pre_act.sem, 1)

        E2, E3 = YD[:, 0, :], YD[:, 1, :]
        zr_clear = Count(sem("head_pads_cleared"), HP, 1)

        def heads_dve(dve, l, hp):
            mu = lambda d, o: vec[:, bass.ds(hp + (V_MU + (d * 3 + o) * HP), 1)]
            for z in ZR:
                nc.vector.memset(z, 0.0)
            dve.drain().then_inc(zr_clear.sem, 1)
            dve.wait_ge(hp_copy.sem, hp_copy.ready(l, hp, 1))
            for d in range(2):
                if d == 1:
                    dve.wait_ge(pre_act.sem, pre_act.ready(l, hp, 4))
                for o in range(3):
                    mix_ops(dve, ZR[o], mu(d, o), d, TMP[o])
                dve.drain()
                nc.vector.tensor_scalar(TMP[7], TMP[1], vec[:, bass.ds(hp + V_KK, 1)], None, ALU.mult).then_inc(pre_dve.sem, 1)
                nc.vector.tensor_copy(DD[d][:, :, 4, :], blocked(TMP[2]))
                dve.wait_ge(pre_act.sem, pre_act.ready(l, hp, 4 * d + 1))
                sl = slice(None) if d == 0 else slice(None, None, -1)
                nc.vector.tensor_tensor_scan(TMP[4][:, sl], KEEP[d][:, sl], TMP[3][:, sl], 0.0, ALU.mult, ALU.add)
                dve.drain()
                nc.vector.tensor_tensor(E3, TMP[4], TMP[3], ALU.subtract)
                dve.wait_ge(pre_prod.sem, pre_prod.ready(l, hp, 3 * d + 2))
                for s in range(2):
                    o0, o1 = DSEG[d][s]
                    nc.vector.tensor_scalar(TMP[6][:, o0:o1], pair(4)[s], 1e-24, None, ALU.max)
                dve.drain().then_inc(pre_dve.sem, 1)
                nc.vector.tensor_scalar(TMP[3], TMP[5], vec[:, bass.ds(hp + V_KA, 1)], omka[:, bass.ds(hp, 1)], ALU.mult, ALU.add)
                dve.drain()
                nc.vector.tensor_tensor(TMP[1], TMP[1], TMP[3], ALU.mult)
                dve.wait_ge(pre_act.sem, pre_act.ready(l, hp, 4 * d + 3))
                nc.vector.tensor_tensor(TMP[7], TMP[7], TMP[6], ALU.mult)
                dve.drain()
                nc.vector.scalar_tensor_tensor(out=TMP[6], in0=TMP[0], scalar=vec[:, bass.ds(hp + V_RK, 1)], in1=TMP[1], op0=ALU.mult, op1=ALU.mult)\
                  .then_inc(pre_dve.sem, 1)
                nc.vector.tensor_tensor(DD[d][:, :, 3, :], blocked(TMP[1]), blocked(E2), ALU.mult)
                nc.vector.tensor_tensor(DD[d][:, :, 1, :], blocked(TMP[0]), blocked(TMP[4]), ALU.mult)
                nc.vector.scalar_tensor_tensor(out=DD[d][:, :, 0, :], in0=blocked(TMP[7]), scalar=-1.0, in1=blocked(E3), op0=ALU.mult, op1=ALU.mult)
                nc.vector.tensor_tensor(TMP[5], TMP[7], TMP[5], ALU.mult)
                dve.drain()
                nc.vector.tensor_tensor(DD[d][:, :, 2, :], blocked(TMP[5]), blocked(E2), ALU.mult)
                dve.wait_ge(pre_prod.sem, pre_prod.ready(l, hp, 3 * d + 3))
                for s in range(2):
                    (o0, o1), (c0, c1) = DSEG[d][s], SEGS[s]
                    dst = BONUS[:, c0:c1] if d == 0 else TMP[6][:, c0:c1]
                    nc.vector.tensor_tensor(dst, pair(6)[s], TMP[2][:, o0:o1], ALU.mult)
                dve.drain()
                if d == 1:
                    nc.vector.tensor_tensor(BONUS, BONUS, TMP[6], ALU.add)
                dve.drain().then_inc(pre_dve.sem, 1)
            for d in range(2):
                nc.vector.memset(ST[d], 0.0)

        def at_block(d, n):
            return n if d == 0 else (NBLK - 1) - n

        def block_pe(pe, l, it):
            b = lambda d, j: bank[4 * d + j]
            n = [0]

            def step(d, last, k):
                last.then_inc(blk_pe[d].sem, 1)

            def on_dve(d, k):
                pe.wait_ge(blk_dve[d].sem, blk_dve[d].ready(l, it, k))

            def on_act(d, k):
                pe.wait_ge(blk_act[d].sem, blk_act[d].ready(l, it, k))

            for d in range(2):
                on_act(d, 1)
                on_dve(d, 0)
                for j, o in enumerate((0, 2, 3, 4)):
                    nc.tensor.transpose(b(d, 0)[:, j * P:(j + 1) * P], STG[d][:, o, :], IDENT)
                rhs = ARZ[d].rearrange("p h o t -> p (h o t)")
                nc.tensor.matmul(b(d, 1)[:, :], STG[d][:, 2, :], rhs, start=True, stop=True)
                step(d, nc.tensor.matmul(b(d, 2)[:, :], STG[d][:, 3, :], rhs, start=True, stop=True), 1)
            for d in range(2):
                on_dve(d, 1)
                on_act(d, 2)
                for h in range(2):
                    nc.tensor.matmul(b(d, 3)[:, h * P:(h + 1) * P], NAK[d][0][:, h, 0, :], IDENT, start=True, stop=True)
                    last = nc.tensor.matmul(b(d, 0)[:, h * P:(h + 1) * P], NAK[d][1][:, h, 0, :], VT[d], start=True, stop=True)
                step(d, last, 2)
            for m in range(1, 6):
                for d in range(2):
                    on_dve(d, 2 * m)
                    for h in range(2):
                        last = nc.tensor.matmul(b(d, 1)[:, h * P:(h + 1) * P], NAK[d][0][:, h, 0, :], XX[d][:, 0, h, :], start=True, stop=True)
                    step(d, last, 2 * m + 1)
                for d in range(2):
                    on_dve(d, 2 * m + 1)
                    for h in range(2):
                        if m < 5:
                            nc.tensor.matmul(b(d, 2)[:, h * P:(h + 1) * P], XX[d][:, 1, h, :], T1[d][:, h, :], start=True, stop=True)
                        last = nc.tensor.matmul(b(d, 2)[:, (2 + h) * P:(3 + h) * P], T1[d][:, h, :], XX[d][:, 1, h, :], start=True, stop=True)
                    step(d, last, 2 * m + 2)
            for d in range(2):
                on_dve(d, 12)
                on_act(d, 3)
                for h in range(2):
                    last = nc.tensor.matmul(b(d, 3)[:, h * P:(h + 1) * P], XX[d][:, 1, h, :], WR[d][:, h].rearrange("p o j -> p (o j)"), start=True, stop=True)
                step(d, last, 13)
            for d in range(2):
                on_act(d, 4)
                for h in range(2):
                    rows = slice(h * HD, (h + 1) * HD)
                    nc.tensor.matmul(b(d, 0)[rows, 0:P], ZQ[d][:, 0, h, :], NAK[d][0][:, h, 1, :], start=True, stop=True)
                    nc.tensor.matmul(b(d, 1)[rows, 0:P], ZQ[d][:, 1, h, :], NAK[d][0][:, h, 1, :], start=True, stop=False, skip_group_check=True)
                    nc.tensor.matmul(b(d, 1)[rows, 0:P], VT[d][:, rows], NAK[d][1][:, h, 1, :], start=False, stop=False, skip_group_check=True)
                z = ZQ[d][:, 0].rearrange("p h j -> p (h j)")
                q = ZQ[d][:, 1].rearrange("p h j -> p (h j)")
                for c in range(2):
                    nc.tensor.matmul(b(d, 2)[:, c * P:(c + 1) * P], z, BKC[d][:, c, 0, :], start=True, stop=True)
                for c in range(2):
                    nc.tensor.matmul(b(d, 3)[:, c * P:(c + 1) * P], BKC[d][:, c, 0, :], q, start=True, stop=False)
                    last = nc.tensor.matmul(b(d, 3)[:, c * P:(c + 1) * P], BKC[d][:, c, 1, :], VT[d], start=False, stop=True)
                step(d, last, 14)
            for j in range(2):
                for d in range(2):
                    c = j if d == 0 else 1 - j
                    cols = slice(c * CHUNK, (c + 1) * CHUNK)
                    on_dve(d, 13 + j)
                    nc.tensor.matmul(b(d, 1)[:, cols], ST[d], GS[d][:, cols], start=False, stop=(j == 1), skip_group_check=True)
                    step(d, nc.tensor.matmul(b(d, 2)[:, j * P:(j + 1) * P], MH[d][:, c, :], ST[d], start=True, stop=True), 15 + j)

        def block_act(act, l, it, n):
            b = lambda d, j: bank[4 * d + j]
            for d in range(2):
                blk = at_block(d, n)
                act.wait_ge(blk_dve[d].sem, blk_dve[d].ready(l, it, 0))
                nc.scalar.activation(DCS[d], DC[:, d, bass.ds(blk * 2, 2)], ACT.Copy)
                nc.scalar.activation(STG[d].rearrange("p o t -> p (o t)"), DD[d][:, bass.ds(blk, 1)].rearrange("p a o t -> p (a o t)"), ACT.Copy)
                act.drain()
                for h in range(2):
                    rows = slice(h * HD, (h + 1) * HD)
                    nc.scalar.activation(ARZ[d][rows, h].rearrange("p o t -> p (o t)"), STG[d][rows, 0:2, :].rearrange("p o t -> p (o t)"), ACT.Copy)
                act.drain().then_inc(blk_act[d].sem, 1)
            for d in range(2):
                act.wait_ge(blk_pe[d].sem, blk_pe[d].ready(l, it, 1))
                nc.scalar.activation(WR[d][:, :, 0, :], b(d, 0)[:, 0:P].rearrange("p (h j) -> p h j", h=2), ACT.Copy)
                nc.scalar.activation(VT[d], b(d, 0)[:, 3 * P:4 * P], ACT.Copy)
                for c in range(2):
                    rows = slice(c * CHUNK, (c + 1) * CHUNK)
                    last = nc.scalar.activation(BKC[d][rows, c].rearrange("p o t -> p (o t)"), b(d, 0)[rows, P:3 * P], ACT.Copy)
                last.then_inc(blk_act[d].sem, 1)
            for d in range(2):
                act.wait_ge(blk_pe[d].sem, blk_pe[d].ready(l, it, 2))
                for h in range(2):
                    last = nc.scalar.activation(WR[d][:, h, 1, :], b(d, 0)[:, h * (P + HD):h * (P + HD) + HD], ACT.Copy)
                last.then_inc(blk_act[d].sem, 1)
            for d in range(2):
                act.wait_ge(blk_pe[d].sem, blk_pe[d].ready(l, it, 13))
                nc.scalar.activation(ZQ[d].rearrange("p o h j -> p h o j"), b(d, 3)[:, 0:256].rearrange("p (h o j) -> p h o j", h=2, o=2), ACT.Copy)\
                  .then_inc(blk_act[d].sem, 1)
            for d in range(2):
                act.wait_ge(blk_pe[d].sem, blk_pe[d].ready(l, it, 16))
                nc.scalar.activation(YD[:, d, bass.ds(at_block(d, n) * P, P)], b(d, 1)[:, 0:P], ACT.Copy).then_inc(blk_act[d].sem, 1)

        def block_dve(dve, l, it):
            b = lambda d, j: bank[4 * d + j]

            def bc(x, n):
                return x.unsqueeze(1).to_broadcast([P, n] + list(x.shape[1:]))

            def on_pe(d, k):
                dve.wait_ge(blk_pe[d].sem, blk_pe[d].ready(l, it, k))

            for d in range(2):
                on_pe(d, 1)
                for j in range(2):
                    last = nc.vector.tensor_tensor(NAK[d][j].rearrange("p h o t -> p h (o t)"), b(d, 1 + j)[:, :].rearrange("p (h t) -> p h t", h=2), bc(GMASK[d], 2), ALU.mult)
                last.then_inc(blk_dve[d].sem, 1)
            for d in range(2):
                on_pe(d, 2)
                low, up = (LOWER, UPPER) if d == 0 else (UPPER, LOWER)
                nc.vector.tensor_tensor(XX[d][:, 0], b(d, 3)[:, 0:256].rearrange("p (h t) -> p h t", h=2), bc(low[0], 2), ALU.mult)
                nc.vector.tensor_tensor(XX[d][:, 1], NAK[d][0][:, :, 0, :], bc(up[0], 2), ALU.mult)
                dve.drain()
                xx = XX[d].rearrange("p x h t -> p (x h) t")
                nc.vector.tensor_tensor(xx, xx, bc(IDENT, 4), ALU.add).then_inc(blk_dve[d].sem, 1)
            for m in range(1, 6):
                for d in range(2):
                    on_pe(d, 2 * m + 1)
                    low = LOWER if d == 0 else UPPER
                    nc.vector.tensor_tensor(T1[d], b(d, 1)[:, 0:256].rearrange("p (h t) -> p h t", h=2), bc(low[m], 2), ALU.mult).then_inc(blk_dve[d].sem, 1)
                for d in range(2):
                    on_pe(d, 2 * m + 2)
                    if m < 5:
                        x, ps = XX[d].rearrange("p x h t -> p (x h t)"), b(d, 2)[:, :]
                    else:
                        x, ps = XX[d][:, 1].rearrange("p h t -> p (h t)"), b(d, 2)[:, 256:512]
                    nc.vector.tensor_tensor(x, x, ps, ALU.add).then_inc(blk_dve[d].sem, 1)
            for d in range(2):
                on_pe(d, 14)
                nc.vector.tensor_tensor(GS[d], STG[d][:, 1, :], b(d, 0)[:, 0:P], ALU.add)
                nc.vector.tensor_tensor(MH[d], b(d, 2)[:, 0:256].rearrange("p (c t) -> p c t", c=2), bc(SAME, 2), ALU.mult)
                for c in range(2):
                    nc.vector.scalar_tensor_tensor(out=HDD[d][:, c, :], in0=b(d, 3)[:, c * P:(c + 1) * P], scalar=DCS[d][:, c:c + 1], in1=SAME, op0=ALU.mult, op1=ALU.mult)
                dve.drain()
                nc.vector.tensor_tensor(MH[d], MH[d], bc(IDENT, 2), ALU.add).then_inc(blk_dve[d].sem, 1)
            for j in range(2):
                for d in range(2):
                    c = j if d == 0 else 1 - j
                    on_pe(d, 15 + j)
                    nc.vector.scalar_tensor_tensor(out=ST[d], in0=b(d, 2)[:, j * P:(j + 1) * P], scalar=DCS[d][:, c:c + 1], in1=HDD[d][:, c, :], op0=ALU.mult, op1=ALU.add)\
                      .then_inc(blk_dve[d].sem, 1)

        def readout_pe(pe, l, hp):
            for j, src in enumerate((TMP[0], TMP[2])):
                pe.wait_ge(*( (post_dve.sem, post_dve.ready(l, hp, 1)) if j == 0 else (post_act.sem, post_act.ready(l, hp, 1)) ))
                for s in range(2):
                    last = nc.tensor.matmul(pair(2 * j)[s], SAME, src[:, SEGS[s][0]:SEGS[s][1]], start=True, stop=True)
                last.then_inc(post_pe.sem, 1)

        def readout_act(act, l, hp):
            act.wait_ge(post_dve.sem, post_dve.ready(l, hp, 2))
            nc.scalar.activation(TMP[2], TMP[1], ACT.Square).then_inc(post_act.sem, 1)
            act.wait_ge(post_pe.sem, post_pe.ready(l, hp, 2))
            for s in range(2):
                nc.scalar.activation(TMP[3][:, SEGS[s][0]:SEGS[s][1]], pair(2)[s], ACT.Ln, scale=1.0 / HD, bias=one[:, 1:2])
            act.drain()
            nc.scalar.activation(TMP[3], TMP[3], ACT.Exp, scale=-0.5).then_inc(post_act.sem, 1)

        def readout_dve(dve, l, hp, it_last):
            for d in range(2):
                dve.wait_ge(blk_act[d].sem, blk_act[d].ready(l, it_last, NAC))
            for s in range(2):
                (c0, c1), (o0, o1) = SEGS[s], DSEG[1][s]
                nc.vector.tensor_tensor(TMP[0][:, c0:c1], YD[:, 0, c0:c1], YD[:, 1, o0:o1], ALU.add)
            dve.drain().then_inc(post_dve.sem, 1)
            dve.wait_ge(post_pe.sem, post_pe.ready(l, hp, 1))
            for s in range(2):
                c0, c1 = SEGS[s]
                nc.vector.scalar_tensor_tensor(out=TMP[1][:, c0:c1], in0=pair(0)[s], scalar=-1.0 / HD, in1=TMP[0][:, c0:c1], op0=ALU.mult, op1=ALU.add)
            dve.drain().then_inc(post_dve.sem, 1)
            dve.wait_ge(post_act.sem, post_act.ready(l, hp, 2))
            nc.vector.tensor_tensor(TMP[1], TMP[1], TMP[3], ALU.mult)
            dve.drain()
            nc.vector.tensor_scalar(TMP[1], TMP[1], vec[:, bass.ds(hp + V_LG, 1)], vec[:, bass.ds(hp + V_LB, 1)], ALU.mult, ALU.add)
            dve.drain()
            nc.vector.tensor_tensor(TMP[1], TMP[1], BONUS, ALU.add)
            dve.drain()
            nc.vector.tensor_tensor(BR[:, 1, bass.ds(hp, 1), :].rearrange("p a t -> p (a t)"), TMP[1], GT, ALU.mult)
            dve.drain()

        def rwkv_pe(pe, l):
            lora_pe(pe, l)
            pe.wait_ge(lora_act, l + 1)
            pe.wait_ge(rw_tables, 16 * (l + 1))
            with pe.Fori(0, HP) as hp:
                heads_pe(pe, l, hp)
                phase_barrier_in(pe, l, hp, 0)
                with pe.Fori(0, NBLK) as n:
                    block_pe(pe, l, hp * NBLK + n)
                phase_barrier_in(pe, l, hp, 1)
                readout_pe(pe, l, hp)
                phase_barrier_in(pe, l, hp, 2)

        def rwkv_act(act, l):
            lora_act_(act, l)
            with act.Fori(0, HP) as hp:
                heads_act(act, l, hp)
                phase_barrier_in(act, l, hp, 0)
                with act.Fori(0, NBLK) as n:
                    block_act(act, l, hp * NBLK + n, n)
                phase_barrier_in(act, l, hp, 1)
                readout_act(act, l, hp)
                phase_barrier_in(act, l, hp, 2)

        def rwkv_dve(dve, l):
            lora_dve(dve, l)
            for d in range(2):
                dve.sem_inc(blk_dve[d].sem, 1)
            dve.wait_ge(rw_tables, 16 * (l + 1))
            with dve.Fori(0, HP) as hp:
                heads_dve(dve, l, hp)
                phase_barrier_in(dve, l, hp, 0)
                with dve.Fori(0, NBLK) as n:
                    block_dve(dve, l, hp * NBLK + n)
                phase_barrier_in(dve, l, hp, 1)
                readout_dve(dve, l, hp, hp * NBLK + (NBLK - 1))
                phase_barrier_in(dve, l, hp, 2)

        head_stage = Count(sem("engines_at_head_stage"), HP, 9)

        stages_entered = sem("head_stages_entered")

        def phase_barrier_in(e, l, hp, j):
            e.drain().then_inc(head_stage.sem, 1)
            e.wait_ge(head_stage.sem, head_stage.ready(l, hp, 3 * (j + 1)))
            e.sem_inc(stages_entered, 1)

        at = Carve(WS0)
        AC = at(2 * SEQ + 3 * 256)
        COS, SIN = AC[:, 0:SEQ], AC[:, SEQ:2 * SEQ]
        NEG = [AC[:, 2 * SEQ + j * 256:2 * SEQ + (j + 1) * 256] for j in range(3)]
        QKV = at(12 * T).rearrange("p (j t) -> p j t", j=12)
        QZ = at(2 * 2 * SEQ).rearrange("p (e o q) -> p e o q", e=2, o=2)
        QC = at(2 * CTX).rearrange("p (e q) -> p e q", e=2)
        KR = at(SEQ)
        VS = at(T)
        VA = at(9 * P).rearrange("p (j c) -> p j c", j=9)
        RT = [at(SEQ), at(SEQ)]
        BIAS = at(2 * GR * BX).rearrange("p (e r x) -> p e r x", e=2, r=GR)
        BN = at(2 * 3 * 256).rearrange("p (e v c r) -> p e v c r", e=2, v=3, c=KCOLS)
        SX = [at(512) for _ in range(2)]
        PX = [at(512) for _ in range(2)]
        PT = [at(512) for _ in range(2)]
        SM = [at(4) for _ in range(2)]

        at_tables = sem("attention_tables_loaded")
        bias_load = sem("bias_loaded")
        att_prod = Count(sem("qkv_products"), 3, 4)
        att_copy = Count(sem("qkv_copied"), 3, 4, primed=4)
        a_clear = sem("attention_cleared")
        a_bias = Count(sem("bias_masked"), HP, 1)
        a_biased = Count(sem("bias_used"), HP, 1, primed=1)
        a_stage = Count(sem("attention_staged"), HP, 1)
        a_swap = Count(sem("attention_swapped"), HP, 3)
        a_rot = Count(sem("attention_rotated"), HP, 3)

        def units(l):
            u = [(g, e, True) for g in range(4) for e in range(2)]
            if l == 0:
                u += [(g, e, False) for g in range(2) for e in range(2)]
            return u

        NU = [12, 8]
        u_score = [Count(sem(f"scores_{l}"), HP, NU[l]) for l in range(2)]
        u_prob = [Count(sem(f"probabilities_{l}"), HP, NU[l]) for l in range(2)]
        u_tr = [Count(sem(f"transposed_{l}"), HP, NU[l]) for l in range(2)]
        u_trc = [Count(sem(f"transposed_copied_{l}"), HP, NU[l]) for l in range(2)]
        u_out = [Count(sem(f"attended_{l}"), HP, NU[l]) for l in range(2)]
        u_ctx = [Count(sem(f"context_scores_copied_{l}"), HP, NU[l]) for l in range(2)]
        u_max = [Count(sem(f"maximum_{l}"), HP, NU[l]) for l in range(2)]
        u_exp = [Count(sem(f"exponentials_{l}"), HP, NU[l]) for l in range(2)]
        u_oc = [Count(sem(f"attended_copied_{l}"), HP, NU[l] // 2) for l in range(2)]

        def qkv_pe(pe, l):
            with pe.Fori(0, 3) as i:
                for t in range(4):
                    if t % 2 == 0:
                        wait_slab(pe, l, "w_att", i, t // 2)
                    pe.wait_ge(att_copy.sem, att_copy.free(l, i, t + 1))
                    products(pair(2 * t), [block(16, t * KD + k) for k in range(KD)], hx_rhs, [0, 1]).then_inc(att_prod.sem, 1)
                nc.tensor.drain().then_inc(slab_used, 2)

        def qkv_act(act, l):
            act.sem_inc(att_copy.sem, 4)
            with act.Fori(0, 3) as i:
                for t in range(4):
                    act.wait_ge(att_prod.sem, att_prod.ready(l, i, t + 1))
                    for s in range(2):
                        last = nc.scalar.activation(QKV[:, bass.ds(i * 4 + t, 1), SEGS[s][0]:SEGS[s][1]].rearrange("p a t -> p (a t)"), pair(2 * t)[s], ACT.Copy)
                    last.then_inc(att_copy.sem, 1)

        def col_major(x, reverse=False):
            if reverse:
                x = x[:, ::-1]
            return x.rearrange("p (c r) -> p r c", r=GR)

        def tokens(x):
            return x.rearrange("p (r c) -> p r c", r=GR)

        def q_of(j0, hp, s=1):
            return QKV[:, bass.ds(hp + j0 * HP, 1), SEGS[s][0]:SEGS[s][1]].rearrange("p a t -> p (a t)")

        SB = [4, 5, 6, 7]

        def attn_pe(pe, l):
            pe.wait_ge(at_tables, 16 * (l + 1))
            with pe.Fori(0, HP) as hp:
                pe.wait_ge(a_biased.sem, a_biased.free(l, hp))
                for j in range(2):
                    nc.tensor.matmul(bank[j][:, :], PERM, q_of(j, hp), start=True, stop=True).then_inc(a_swap.sem, 1)
                pe.wait_ge(a_stage.sem, a_stage.ready(l, hp))
                for j in range(9):
                    src = VS[:, (j - 7) * P:(j - 6) * P] if j >= 7 else VS[:, CTX + VCOL0[j] * GR:CTX + VCOL0[j] * GR + P]
                    last = nc.tensor.transpose(bank[2 + j // 4][:, (j % 4) * P:(j % 4 + 1) * P], src, IDENT)
                last.then_inc(a_swap.sem, 1)
                pe.wait_ge(a_rot.sem, a_rot.ready(l, hp, 3))
                us = units(l)

                def scores(u):
                    g, e, lat = us[u]
                    sc = bank[u % 2]
                    if u >= 2:
                        pe.wait_ge(u_prob[l].sem, u_prob[l].ready(0, hp, u - 1))
                    if lat:
                        k0 = KEY0[3 - g] * GR
                        nc.tensor.matmul(sc[:, 0:256], QZ[:, e, 0, g * P:(g + 1) * P], KR[:, k0:k0 + 256], start=True, stop=True)
                        last = nc.tensor.matmul(sc[:, 256:512], QZ[:, e, 1, g * P:(g + 1) * P], q_of(1, hp, 0), start=True, stop=True)
                    else:
                        last = nc.tensor.matmul(sc[:, 256:512], QC[:, e, g * P:(g + 1) * P], q_of(1, hp, 0), start=True, stop=True)
                    last.then_inc(u_score[l].sem, 1)

                scores(0)
                scores(1)
                for u, (g, e, lat) in enumerate(us):
                    pe.wait_ge(u_prob[l].sem, u_prob[l].ready(0, hp, u + 1))
                    tb = bank[2 + u % 2]
                    if u >= 2:
                        pe.wait_ge(u_trc[l].sem, u_trc[l].ready(0, hp, u - 1))
                    kts = range(4) if lat else range(2, 4)
                    for kt in kts:
                        last = nc.tensor.transpose(tb[:, kt * P:(kt + 1) * P], PX[u % 2][:, kt * P:(kt + 1) * P], IDENT)
                    last.then_inc(u_tr[l].sem, 1)
                    if u + 2 < len(us):
                        scores(u + 2)
                    pe.wait_ge(u_trc[l].sem, u_trc[l].ready(0, hp, u + 1))
                    if e == 0 and u >= 4:
                        pe.wait_ge(u_oc[l].sem, u_oc[l].ready(0, hp, u // 2 - 1))
                    ob = bank[4 + (u // 2) % 2]
                    rows = slice(e * HD, (e + 1) * HD)
                    k0 = KEY0[3 - g] if lat else 0
                    for kt in kts:
                        v = VA[:, 5 + kt, rows] if kt >= 2 else VA[:, VCOL0.index(k0 + 16 * kt), rows]
                        last = nc.tensor.matmul(ob[rows, 0:P], v, PT[u % 2][:, kt * P:(kt + 1) * P], start=(kt == kts[0]), stop=(kt == 3))
                    last.then_inc(u_out[l].sem, 1)
                nc.tensor.drain()

        def attn_act(act, l):
            act.wait_ge(a_clear, l + 1)
            with act.Fori(0, HP) as hp:
                nc.scalar.activation(VS[:, 0:CTX], q_of(2, hp, 0), ACT.Copy)
                nc.scalar.activation(col_major(VS[:, CTX:T]), tokens(q_of(2, hp)), ACT.Copy)
                for e in range(2):
                    rows = slice(e * HD, (e + 1) * HD)
                    nc.scalar.activation(col_major(QZ[rows, e, 1, :], True), tokens(q_of(0, hp)[rows]), ACT.Copy)
                    if l == 0:
                        nc.scalar.activation(QC[rows, e, :], q_of(0, hp, 0)[rows], ACT.Copy)
                act.drain().then_inc(a_stage.sem, 1)
                us = units(l)

                def probabilities(u):
                    g, e, lat = us[u]
                    act.wait_ge(u_score[l].sem, u_score[l].ready(0, hp, u + 1))
                    if u >= 2:
                        act.wait_ge(u_prob[l].sem, u_prob[l].ready(0, hp, u - 1))
                    nc.scalar.activation(SX[u % 2][:, 256:512], bank[u % 2][:, 256:512], ACT.Copy, scale=HD ** -0.5).then_inc(u_ctx[l].sem, 1)
                    act.wait_ge(u_max[l].sem, u_max[l].ready(0, hp, u + 1))
                    lo = 0 if lat else 256
                    nc.scalar.activation(SX[u % 2][:, lo:512], SX[u % 2][:, lo:512], ACT.Exp, bias=SM[u % 2][:, 0:1], accum_out=SM[u % 2][:, 1:2])\
                      .then_inc(u_exp[l].sem, 1)

                probabilities(0)
                for u, (g, e, lat) in enumerate(us):
                    if u + 1 < len(us):
                        probabilities(u + 1)
                    act.wait_ge(u_tr[l].sem, u_tr[l].ready(0, hp, u + 1))
                    if u >= 2:
                        act.wait_ge(u_out[l].sem, u_out[l].ready(0, hp, u - 1))
                    lo = 0 if lat else 256
                    nc.scalar.activation(PT[u % 2][:, lo:512], bank[2 + u % 2][:, lo:512], ACT.Copy).then_inc(u_trc[l].sem, 1)
                act.drain()

        def attn_dve(dve, l):
            for z in (QZ.rearrange("p e o q -> p (e o q)"), QC.rearrange("p e q -> p (e q)")):
                nc.vector.memset(z, 0.0)
            dve.drain().then_inc(a_clear, 1)
            dve.wait_ge(at_tables, 16 * (l + 1))
            dve.sem_inc(a_biased.sem, 1)
            with dve.Fori(0, HP) as hp:
                for j in range(2):
                    nc.vector.tensor_tensor(RT[0], q_of(j, hp), COS, ALU.mult)
                    dve.wait_ge(a_swap.sem, a_swap.ready(l, hp, j + 1))
                    nc.vector.tensor_tensor(RT[1], bank[j][:, :], SIN, ALU.mult)
                    dve.drain()
                    if j == 0:
                        for e in range(2):
                            rows = slice(e * HD, (e + 1) * HD)
                            nc.vector.tensor_tensor(col_major(QZ[rows, e, 0, :], True), tokens(RT[0][rows]), tokens(RT[1][rows]), ALU.add)
                    else:
                        nc.vector.tensor_tensor(col_major(KR), tokens(RT[0]), tokens(RT[1]), ALU.add)
                    dve.drain().then_inc(a_rot.sem, 1)
                dve.wait_ge(a_swap.sem, a_swap.ready(l, hp, 3))
                for j in range(3):
                    n = min(4, 9 - 4 * j)
                    last = nc.vector.tensor_copy(VA[:, 4 * j:4 * j + n, :].rearrange("p j c -> p (j c)"), bank[2 + j][:, 0:n * P])
                last.then_inc(a_rot.sem, 1)
                dve.wait_ge(a_bias.sem, a_bias.ready(l, hp))
                us = units(l)
                for u, (g, e, lat) in enumerate(us):
                    x = SX[u % 2]
                    lo = 0 if lat else 256
                    dve.wait_ge(u_ctx[l].sem, u_ctx[l].ready(0, hp, u + 1))
                    if lat:
                        nc.vector.scalar_tensor_tensor(out=x[:, 0:256], in0=bank[u % 2][:, 0:256], scalar=HD ** -0.5,
                                                       in1=BN[:, e, VARIANT[3 - g]].rearrange("p c r -> p (c r)"), op0=ALU.mult, op1=ALU.add)
                        dve.drain()
                    nc.vector.reduce_max(SM[u % 2][:, 2:3], x[:, lo:512], AX)
                    dve.drain()
                    nc.vector.tensor_scalar(SM[u % 2][:, 0:1], SM[u % 2][:, 2:3], -1.0, None, ALU.mult).then_inc(u_max[l].sem, 1)
                    if u >= 1:
                        finish(dve, l, hp, us, u - 1)
                finish(dve, l, hp, us, len(us) - 1)
                dve.drain().then_inc(a_biased.sem, 1)

        def finish(dve, l, hp, us, u):
            g, e, lat = us[u]
            lo = 0 if lat else 256
            dve.wait_ge(u_exp[l].sem, u_exp[l].ready(0, hp, u + 1))
            nc.vector.reciprocal(SM[u % 2][:, 3:4], SM[u % 2][:, 1:2])
            dve.drain()
            if u >= 2:
                dve.wait_ge(u_tr[l].sem, u_tr[l].ready(0, hp, u - 1))
            nc.vector.tensor_scalar(PX[u % 2][:, lo:512], SX[u % 2][:, lo:512], SM[u % 2][:, 3:4], None, ALU.mult).then_inc(u_prob[l].sem, 1)
            if u % 2 == 1 and u >= 3:
                copy_out(dve, l, hp, us, u - 2)
            if u == len(us) - 1:
                copy_out(dve, l, hp, us, u)

        def copy_out(dve, l, hp, us, u):
            g, e, lat = us[u]
            dve.wait_ge(u_out[l].sem, u_out[l].ready(0, hp, u + 1))
            ob = bank[4 + (u // 2) % 2][:, 0:P]
            if lat:
                g0 = 3 - g
                dst = BR[:, 2, bass.ds(hp, 1), CTX:T].rearrange("p a (r c) -> p (a r) c", r=GR)[:, :, g0 * QCOLS:(g0 + 1) * QCOLS]
                src = ob[:, ::-1].rearrange("p (c r) -> p r c", r=GR)
            else:
                dst = BR[:, 2, bass.ds(hp, 1), g * P:(g + 1) * P].rearrange("p a t -> p (a t)")
                src = ob
            nc.vector.tensor_copy(dst, src).then_inc(u_oc[l].sem, 1)

        def attn_pool(pool, l):
            with pool.Fori(0, HP) as hp:
                pool.wait_ge(a_biased.sem, a_biased.free(l, hp))
                for e in range(2):
                    for x in range(QCOLS):
                        off = a["rpb"][l, bass.ds(hp * (2 * RPB) + (RPB_PAD - 16 + e * RPB + x), 31 * (2 * GR - 1) + 17)]
                        src = bias_window(off)
                        pool.dma_start(BIAS[x * GR:(x + 1) * GR, e], src).then_inc(bias_load, 16)
                pool.wait_ge(bias_load, (hp + 1) * (2 * QCOLS * 16) + l * HP * 2 * QCOLS * 16)
                for e in range(2):
                    for v, shift in enumerate((16, 8, 0)):
                        nc.gpsimd.tensor_tensor(BN[:, e, v], BIAS[:, e, :, shift:shift + KCOLS].rearrange("p r x -> p x r"),
                                                NEG[v].rearrange("p (c r) -> p c r", c=KCOLS), ALU.add)
                pool.drain().then_inc(a_bias.sem, 1)

        def bias_window(ap):
            rows = ap[0:31 * (2 * GR - 1) + 17]
            return bass.AP(tensor=rows.tensor, offset=rows.offset, ap=[[31, GR], [31, GR], [1, BX]])

        mg = Carve(WS0)
        MG = mg(KD * T).rearrange("p (k t) -> p k t", k=KD)
        GATE = [mg(T), mg(T)]
        MT = mg(T)
        m_prod = Count(sem("merge_products"), KD, 3)
        m_gate = Count(sem("merge_gates"), KD, 3)
        m_used = Count(sem("merge_used"), KD, 3, primed=3)

        def merge_pe(pe, l):
            segs = segs_of(l)
            with pe.Fori(0, KD) as i:
                wait_slab(pe, l, "w_merge", i, 0)
                for n in range(3):
                    if n == 1:
                        wait_slab(pe, l, "w_merge", i, 1)
                    b = 4 * (n % 2)
                    if n == 0:
                        pe.wait_ge(m_used.sem, m_used.free(l, i, 3))
                    elif n == 1:
                        pe.wait_ge(m_used.sem, m_used.free(l, i, 2))
                    else:
                        pe.wait_ge(m_used.sem, m_used.ready(l, i, 1))
                    products(pair(b), [block(18, n * 12 + k) for k in range(KD)], hx_rhs, segs)
                    products(pair(b + 2), [block(18, n * 12 + KD + k) for k in range(KM)],
                             lambda k, s: BR[:, n, k, SEGS[s][0]:SEGS[s][1]], segs).then_inc(m_prod.sem, 1)
                nc.tensor.drain().then_inc(slab_used, 2)

        def merge_act(act, l):
            with act.Fori(0, KD) as i:
                for n in range(3):
                    act.wait_ge(m_prod.sem, m_prod.ready(l, i, n + 1))
                    if n == 2:
                        act.wait_ge(m_used.sem, m_used.ready(l, i, 1))
                    else:
                        act.wait_ge(m_used.sem, m_used.free(l, i, 3 if n == 0 else 2))
                    for s in segs_of(l):
                        last = nc.scalar.activation(GATE[n % 2][:, SEGS[s][0]:SEGS[s][1]], pair(4 * (n % 2))[s], ACT.Sigmoid)
                    last.then_inc(m_gate.sem, 1)

        def merge_dve(dve, l):
            dve.sem_inc(m_used.sem, 3)
            with dve.Fori(0, KD) as i:
                for n in range(3):
                    dve.wait_ge(m_gate.sem, m_gate.ready(l, i, n + 1))
                    dst = [MG[:, bass.ds(i, 1), c0:c1].rearrange("p a t -> p (a t)") for c0, c1 in SEGS]
                    for s in segs_of(l):
                        c0, c1 = SEGS[s]
                        last = nc.vector.tensor_tensor(dst[s] if n == 0 else MT[:, c0:c1], pair(4 * (n % 2) + 2)[s], GATE[n % 2][:, c0:c1], ALU.mult)
                    last.then_inc(m_used.sem, 1)
                    if n:
                        dve.drain()
                        for s in segs_of(l):
                            c0, c1 = SEGS[s]
                            nc.vector.tensor_tensor(dst[s], dst[s], MT[:, c0:c1], ALU.add)
                        dve.drain()

        Y = arena[:, 0:KD * T].rearrange("p (k t) -> p k t", k=KD)
        o_prod = Count(sem("out_products"), 2, 4)
        o_copy = Count(sem("out_copied"), 2, 4, primed=4)

        def out_pe(pe, l):
            with pe.Fori(0, 2) as i:
                for t in range(4):
                    if t % 2 == 0:
                        wait_slab(pe, l, "w_out", i, t // 2)
                    pe.wait_ge(o_copy.sem, o_copy.free(l, i, t + 1))
                    products(pair(2 * t), [block(16, t * KD + k) for k in range(KD)], lambda k, s: MG[:, k, SEGS[s][0]:SEGS[s][1]], segs_of(l))\
                        .then_inc(o_prod.sem, 1)
                nc.tensor.drain().then_inc(slab_used, 2)

        def out_act(act, l):
            act.sem_inc(o_copy.sem, 4)
            with act.Fori(0, 2) as i:
                for t in range(4):
                    act.wait_ge(o_prod.sem, o_prod.ready(l, i, t + 1))
                    for s in segs_of(l):
                        last = nc.scalar.activation(Y[:, bass.ds(i * 4 + t, 1), SEGS[s][0]:SEGS[s][1]].rearrange("p a t -> p (a t)"), pair(2 * t)[s], ACT.Copy)
                    last.then_inc(o_copy.sem, 1)

        MID = arena[:, KD * T:KD * T + NJ * T].rearrange("p (j t) -> p j t", j=NJ)
        SL = [NSQ[0], NSQ[1]]
        f_prod = Count(sem("ffn_products"), NJ // 2, 2)
        f_silu = Count(sem("ffn_silu"), NJ // 2, 2)
        f_mid = Count(sem("ffn_mid"), NJ // 2, 2, primed=2)
        g_prod = Count(sem("ffn_out_products"), KD, 1)
        g_copy = Count(sem("ffn_out_copied"), KD, 1, primed=1)

        def ffn_pe(pe, l):
            segs = segs_of(l)
            with pe.Fori(0, NJ // 2) as i:
                for t in range(2):
                    wait_slab(pe, l, "w_ffn_in", i, t)
                    pe.wait_ge(f_mid.sem, f_mid.free(l, i, t + 1))
                    products(pair(4 * t), [slots[t][:, k * P:(k + 1) * P] for k in range(KD)], hx_rhs, segs)
                    products(pair(4 * t + 2), [slots[t][:, (KD + k) * P:(KD + k + 1) * P] for k in range(KD)], hx_rhs, segs).then_inc(f_prod.sem, 1)
                nc.tensor.drain().then_inc(slab_used, 2)
            pe.wait_ge(f_mid.sem, f_mid.ready(l, NJ // 2 - 1, 2))
            with pe.Fori(0, KD) as i:
                for s in range(2):
                    wait_slab(pe, l, "w_ffn_out", i, s)
                pe.wait_ge(g_copy.sem, g_copy.free(l, i))
                products(pair(0), [block(11, j) for j in range(NJ)], lambda j, s: MID[:, j, SEGS[s][0]:SEGS[s][1]], segs).then_inc(g_prod.sem, 1)
                nc.tensor.drain().then_inc(slab_used, 2)

        def ffn_act(act, l):
            with act.Fori(0, NJ // 2) as i:
                for t in range(2):
                    act.wait_ge(f_prod.sem, f_prod.ready(l, i, t + 1))
                    act.wait_ge(f_mid.sem, f_mid.free(l, i, t + 1))
                    for s in segs_of(l):
                        last = nc.scalar.activation(SL[t][:, SEGS[s][0]:SEGS[s][1]], pair(4 * t)[s], ACT.Silu)
                    last.then_inc(f_silu.sem, 1)
            act.sem_inc(g_copy.sem, 1)
            with act.Fori(0, KD) as i:
                act.wait_ge(g_prod.sem, g_prod.ready(l, i))
                for s in segs_of(l):
                    last = nc.scalar.activation(Y[:, bass.ds(i, 1), SEGS[s][0]:SEGS[s][1]].rearrange("p a t -> p (a t)"), pair(0)[s], ACT.Copy)
                last.then_inc(g_copy.sem, 1)

        def ffn_dve(dve, l):
            dve.sem_inc(f_mid.sem, 2)
            with dve.Fori(0, NJ // 2) as i:
                for t in range(2):
                    dve.wait_ge(f_silu.sem, f_silu.ready(l, i, t + 1))
                    for s in segs_of(l):
                        c0, c1 = SEGS[s]
                        last = nc.vector.tensor_tensor(MID[:, bass.ds(i * 2 + t, 1), c0:c1].rearrange("p a t -> p (a t)"), pair(4 * t + 2)[s], SL[t][:, c0:c1], ALU.mult)
                    last.then_inc(f_mid.sem, 1)

        blk = ctx.enter_context(nc.Block())
        res_src = lambda k: RES[:, k, :]
        y_src = lambda k: Y[:, k, :]

        @blk.sync
        def _(sp):
            sync_program(sp)
            sp.wait_ge(phase_end, 4 * TOTAL_BARRIERS)
            sp.dma_start(a["out"].rearrange("p (k t) -> p k t", k=KD), RES[:, :, CTX:T]).then_inc(s_out, 16)
            sp.wait_ge(s_out, 16)

        @blk.tensor
        def _(pe):
            pe.sem_inc(slab_used, 2)
            pe.wait_ge(s_load, 16 * 3)
            for l in range(DEPTH):
                ada_pe(pe, l); phase_barrier(pe, "pe")
                stats_pe(pe, 4 * l, [0, 1]); phase_barrier(pe, "pe")
                conv_pe(pe, l); phase_barrier(pe, "pe")
                rwkv_pe(pe, l); phase_barrier(pe, "pe")
                qkv_pe(pe, l); phase_barrier(pe, "pe")
                attn_pe(pe, l); phase_barrier(pe, "pe")
                merge_pe(pe, l); phase_barrier(pe, "pe")
                out_pe(pe, l)
                pe.wait_ge(o_copy.sem, o_copy.ready(l, 1, 4))
                stats_pe(pe, 4 * l + 1, segs_of(l)); phase_barrier(pe, "pe")
                stats_pe(pe, 4 * l + 2, segs_of(l)); phase_barrier(pe, "pe")
                ffn_pe(pe, l)
                pe.wait_ge(g_copy.sem, g_copy.ready(l, KD - 1))
                stats_pe(pe, 4 * l + 3, segs_of(l)); phase_barrier(pe, "pe")

        @blk.scalar
        def _(act):
            act.wait_ge(s_load, 16 * 3)
            nc.scalar.activation(cin[:, :], cin[:, :], ACT.Silu).then_inc(silu_done, 1)
            for l in range(DEPTH):
                phase_barrier(act, "act")
                stats_act(act, 4 * l, res_src, [0, 1])
                norm_act(act, 2 * l, 0, [0, 1]); phase_barrier(act, "act")
                conv_act(act, l); phase_barrier(act, "act")
                rwkv_act(act, l); phase_barrier(act, "act")
                qkv_act(act, l); phase_barrier(act, "act")
                attn_act(act, l); phase_barrier(act, "act")
                merge_act(act, l); phase_barrier(act, "act")
                out_act(act, l)
                act.drain()
                stats_act(act, 4 * l + 1, y_src, segs_of(l)); phase_barrier(act, "act")
                stats_act(act, 4 * l + 2, res_src, segs_of(l))
                norm_act(act, 2 * l + 1, 1, segs_of(l)); phase_barrier(act, "act")
                ffn_act(act, l)
                act.drain()
                stats_act(act, 4 * l + 3, y_src, segs_of(l)); phase_barrier(act, "act")

        @blk.vector
        def _(dve):
            nc.vector.memset(one[:, 0:1], EPS)
            nc.vector.memset(one[:, 1:4], LN_EPS)
            dve.wait_ge(s_load, 16 * 3)
            for l in range(DEPTH):
                ada_dve(dve, l); phase_barrier(dve, "dve")
                norm_dve(dve, 2 * l, 0, [0, 1]); phase_barrier(dve, "dve")
                conv_dve(dve, l); phase_barrier(dve, "dve")
                rwkv_dve(dve, l); phase_barrier(dve, "dve")
                phase_barrier(dve, "dve")
                attn_dve(dve, l); phase_barrier(dve, "dve")
                merge_dve(dve, l); phase_barrier(dve, "dve")
                add_dve(dve, 2 * l, 0, segs_of(l), Y); phase_barrier(dve, "dve")
                norm_dve(dve, 2 * l + 1, 1, segs_of(l)); phase_barrier(dve, "dve")
                ffn_dve(dve, l)
                add_dve(dve, 2 * l + 1, 1, segs_of(l), Y); phase_barrier(dve, "dve")

        @blk.gpsimd
        def _(pool):
            pool.dma_start(glob[:, :], a["glob"]).then_inc(s_load, 16)
            pool.dma_start(cin[:, :], a["cin"]).then_inc(s_load, 16)
            pool.dma_start(resid[:, :], a["x"]).then_inc(s_load, 16)
            for l in range(DEPTH):
                if l:
                    pass
                pool.dma_start(vec[:, :], a["vec"][l, :, :]).then_inc(s_wload, 16)
                for k in range(3):
                    phase_barrier(pool, "pool")
                pool.dma_start(RC, a["rwkv_tables"]).then_inc(rw_tables, 16)
                for k in range(2):
                    phase_barrier(pool, "pool")
                pool.dma_start(AC, a["attn_tables"]).then_inc(at_tables, 16)
                pool.wait_ge(at_tables, 16 * (l + 1))
                attn_pool(pool, l)
                for k in range(5):
                    phase_barrier(pool, "pool")


def arrays():
    return {
        "glob": (P, 4 * P), "rwkv_tables": (P, 512 + 12 * P + 2 * T), "attn_tables": (P, 2 * SEQ + 768),
        "x": (P, KD * T), "cin": (P, KD * 2), "vec": (DEPTH, P, NV), "rpb": (DEPTH, 2 * RPB_PAD + 8 * RPB),
        "w_ada": (DEPTH, 24, P, 16 * P), "w_conv": (DEPTH, 8, P, 12 * P), "w_lora": (DEPTH, 2, P, 8 * P),
        "w_heads": (DEPTH, 8, P, 14 * P), "w_att": (DEPTH, 6, P, 16 * P), "w_merge": (DEPTH, 16, P, 18 * P),
        "w_out": (DEPTH, 4, P, 16 * P), "w_ffn_in": (DEPTH, 22, P, 16 * P), "w_ffn_out": (DEPTH, 16, P, 11 * P),
    }


def layout(x, c, ctx, c_ctx, w_ada, b_ada, norm_g, w_in, conv_w, rwkv_mu, rwkv_w0, rwkv_w2, rwkv_a0, rwkv_a2,
           rwkv_kk, rwkv_ka, rwkv_rk, rwkv_g2, lnx_g, lnx_b, na_rpb, w_up, w_o, w_ffn_in, w_ffn_out):
    out = dict(zip(("glob", "rwkv_tables", "attn_tables"), constants()))

    def chan(v):
        v = np.asarray(v)
        return np.moveaxis(v.reshape(v.shape[:-1] + (-1, P)), -1, 0).reshape(P, -1)

    tok = np.concatenate([ctx[0], x[0]], 0)
    out["x"] = np.ascontiguousarray(tok.T.reshape(KD, P, T).transpose(1, 0, 2)).reshape(P, KD * T)
    out["cin"] = np.stack([c_ctx.reshape(KD, P).T, c[0].reshape(KD, P).T], 2).reshape(P, KD * 2)
    zero = np.zeros((P, P), np.float32)
    vecs, rpbs = [], []
    streams = {k: [] for k in arrays() if k.startswith("w_")}
    for l in range(DEPTH):
        mu = rwkv_mu[l]
        vecs.append(np.concatenate([
            chan(norm_g[l]), chan(conv_w[l]), chan(mu[:, 0:3 * MIX].reshape(2, 3, MIX)), chan(mu[:, 3 * MIX:]),
            chan(rwkv_w0[l]), chan(rwkv_a0[l]), chan(rwkv_kk[l]), chan(rwkv_ka[l]), chan(rwkv_rk[l].reshape(MIX)),
            chan(lnx_g[l]), chan(lnx_b[l]), chan(b_ada[l])], 1))
        rpbs.append(np.pad(na_rpb[l].reshape(-1), RPB_PAD))

        def blocks(w):
            k, n = w.shape
            return w.reshape(k // P, P, n // P, P).transpose(2, 0, 1, 3)

        def slabs(name, bl):
            n, cols = arrays()[name][1], arrays()[name][3] // P
            bl = np.asarray(bl).reshape(n, cols, P, P)
            streams[name].append(bl.transpose(0, 2, 1, 3).reshape(n, P, cols * P))

        ada, win = blocks(w_ada[l]), blocks(w_in[l])
        slabs("w_ada", ada)
        cv, rk, lo, lg, qt, gt = win[0:12], win[12:24], win[24:25], win[25:26], win[26:38], win[38:62]
        slabs("w_conv", [b for i in range(HP) for t in (2, 1, 0) for b in cv[t * HP + i]])
        slabs("w_lora", [b for t in (lo[0], lg[0]) for b in t])
        w2a2 = np.concatenate([rwkv_w2[l], rwkv_a2[l]], 1)
        heads = []
        for i in range(HP):
            cs = slice(i * P, (i + 1) * P)
            heads += [b for t in range(3) for b in rk[t * HP + i]] + [np.zeros((P, P), np.float32)] * 0
            heads += [w2a2[0][:, cs], w2a2[1][:, cs], rwkv_g2[l][:, cs], zero]
        slabs("w_heads", heads)
        slabs("w_att", qt)
        up = [blocks(w_up[l, n]) for n in range(3)]
        slabs("w_merge", [b for i in range(KD) for n in range(3) for b in list(gt[n * KD + i]) + list(up[n][i])])
        slabs("w_out", blocks(w_o[l]))
        fi = blocks(w_ffn_in[l])
        slabs("w_ffn_in", [b for j in range(NJ) for t in (j, NJ + j) for b in fi[t]])
        slabs("w_ffn_out", blocks(w_ffn_out[l]))
    out["vec"] = np.stack(vecs)
    out["rpb"] = np.stack(rpbs)
    for k, v in streams.items():
        out[k] = np.stack(v)
    for k, shape in arrays().items():
        assert out[k].shape == shape, (k, out[k].shape, shape)
        out[k] = np.ascontiguousarray(out[k])
    return out


def build(nc):
    F = mybir.dt.float32
    a = {}
    for name, shape in arrays().items():
        a[name] = nc.dram_tensor("in_" + name, list(shape), F, kind="ExternalInput").ap()
    a["out"] = nc.dram_tensor("out", [P, KD * SEQ], F, kind="ExternalOutput").ap()
    return a


def kernel(**inputs):
    import concourse.bacc as bacc
    from concourse.bass_utils import run_bass_kernel_spmd

    nc = bacc.Bacc("TRN2", target_bir_lowering=False, num_devices=1)
    a = build(nc)
    program(nc, a)
    got = run_bass_kernel_spmd(nc, [{"in_" + k: v for k, v in layout(**{k: np.asarray(v) for k, v in inputs.items()}).items()}], core_ids=[0])
    y = got.results[0]["out"].reshape(P, KD, SEQ)
    return np.ascontiguousarray(y.transpose(2, 1, 0).reshape(1, SEQ, D))
```

```python
import math
from contextlib import ExitStack

import numpy as np
import concourse.bass as bass
from concourse import mybir

D, SEQ, CTX, DEPTH, MIX, HD, FF = 1024, 512, 256, 2, 512, 64, 2816
P = 128
T = CTX + SEQ
GW, GR = 64, SEQ // 64
NROW, NCOL = 8, 16
KD, KM, NJ = D // P, MIX // P, FF // P
HP = MIX // P
CHUNK = 64
NBLK = T // P
SEGS = [(0, CTX), (CTX, T)]
DSEG = [[(0, CTX), (CTX, T)], [(SEQ, T), (0, SEQ)]]
QCOLS = 16
KCOLS = 32
KEY0 = [0, 8, 24, 32]
VCOL0 = [0, 16, 8, 24, 40, 32, 48]
VARIANT = [0, 1, 1, 2]
RPB = (2 * NROW - 1) * (2 * NCOL - 1)
RPB_PAD = 16
BX = 48
DECAY = math.exp(-0.5)
EPS, LN_EPS = 1e-6, 64e-5
V_NG, V_CW, V_MU, V_MUL, V_W0, V_A0 = 0, 32, 44, 68, 70, 78
V_KK, V_KA, V_RK, V_LG, V_LB = 86, 90, 94, 98, 102
NV = V_LB + HP
NADA = 6 * KD


def constants():
    i = np.arange(P)
    same = (i[:, None] // HD == i[None, :] // HD)
    eye = np.eye(P, dtype=np.float32)
    perm = np.zeros((P, P), np.float32)
    perm[i, (i // 32) * 32 + (i + 16) % 32] = 1.0
    glob = np.concatenate([eye, np.full((P, P), 1.0 / D), same, perm], 1).astype(np.float32)
    s, t = i[:, None], i[None, :]
    chunk = s // CHUNK == t // CHUNK
    gram = [np.concatenate([chunk & (s < t), chunk & (s <= t)], 1), np.concatenate([chunk & (s > t), chunk & (s >= t)], 1)]
    merge = []
    for m in (1, 2, 4, 8, 16, 32):
        low = (s // (2 * m) == t // (2 * m)) & (s // m > t // m)
        merge.append(low)
    lows = np.concatenate(merge, 1)
    ups = np.concatenate([x.T for x in merge], 1)
    tok = np.arange(T)
    resets = [np.broadcast_to(tok % CHUNK != 0, (P, T)), np.broadcast_to(tok % CHUNK != CHUNK - 1, (P, T))]
    rwkv = np.concatenate(gram + [lows, ups] + resets, 1).astype(np.float32)
    tt = np.arange(SEQ)
    freq = 10000.0 ** (-np.arange(16, dtype=np.float32) / 16)
    pos = np.where((i % HD < 32)[:, None], (tt // GW)[None, :], (tt % GW)[None, :]).astype(np.float32)
    ang = pos * freq[i % 16][:, None].astype(np.float32)
    sign = np.where(i % 32 < 16, -1.0, 1.0)[:, None]
    neg = []
    for g in (0, 1, 3):
        qc = QCOLS * g + 15 - i // GR
        kc = KEY0[g] + np.arange(KCOLS * GR) // GR
        start = np.clip(qc - NCOL // 2, 0, GW - NCOL)
        win = (kc[None, :] >= start[:, None]) & (kc[None, :] < start[:, None] + NCOL)
        neg.append(np.where(win, 0.0, -1e30))
    attn = np.concatenate([np.cos(ang), np.sin(ang) * sign] + neg, 1).astype(np.float32)
    return glob, rwkv, attn


class Count:

    def __init__(self, sem, passes=1, per=1, primed=0):
        self.sem, self.passes, self.per, self.primed = sem, passes, per, primed
        self.total = primed + passes * per

    def ready(self, use, i, k=1):
        return i * self.per + (use * self.total + self.primed + k)

    def free(self, use, i, k=1):
        return i * self.per + (use * self.total + k)


def program(nc, a, debug=None):
    F = mybir.dt.float32
    ALU = mybir.AluOpType
    ACT = mybir.ActivationFunctionType
    AX = mybir.AxisListType.X
    ctx = ExitStack()
    with ctx:
        def sb(name, n):
            return ctx.enter_context(nc.sbuf_tensor(name, [P, n], F))

        def sem(name):
            return ctx.enter_context(nc.semaphore(name))

        side_dram, gates_dram = a["side_dram"], a["gates_dram"]

        glob = sb("glob", 4 * P)
        IDENT, MEAN_D, SAME, PERM = [glob[:, j * P:(j + 1) * P] for j in range(4)]
        vec = sb("vec", NV)
        cin = sb("cin", KD * 2)
        bada = sb("bada", DEPTH * NADA)
        mods = [sb(f"mod{l}", NADA * 2) for l in range(DEPTH)]
        ders = [sb(f"der{l}", 4 * KD * 2) for l in range(DEPTH)]
        one = sb("one", 4)
        resid = sb("resid", KD * T)
        hx = sb("hx", KD * T)
        slots = [sb(f"slot{s}", 8 * P) for s in range(4)]
        NA_ = 9216 + 25984
        arena = sb("arena", NA_)
        bank = [ctx.enter_context(nc.psum_tensor(f"bank{i}", [P, 512], F)) for i in range(8)]

        RES = resid[:, :].rearrange("p (k t) -> p k t", k=KD)
        HX = hx[:, :].rearrange("p (k t) -> p k t", k=KD)
        CIN = cin[:, :].rearrange("p (k s) -> p k s", s=2)
        MOD = [x[:, :].rearrange("p (j s) -> p j s", s=2) for x in mods]
        DER = [x[:, :].rearrange("p (n k s) -> p n k s", n=4, s=2) for x in ders]

        class Carve:

            def __init__(self, at):
                self.at = at

            def __call__(self, n):
                self.at += n
                assert self.at <= NA_, self.at
                return arena[:, self.at - n:self.at]

        BR = arena[:, 0:3 * HP * T].rearrange("p (n k t) -> p n k t", n=3, k=HP)
        WS0 = 3 * HP * T

        norm_ws = Carve(NA_ - 5 * T)
        NSQ = [norm_ws(T), norm_ws(T)]
        NRS = norm_ws(T)
        NTMP = [norm_ws(T), norm_ws(T)]

        s_load = sem("loaded_constants")
        s_wload = sem("loaded_layer_tables")
        s_out = sem("output_stored")
        phase_end = sem("engines_at_phase_end")
        slab_full = [sem(f"slab_full_{s}") for s in range(4)]
        slab_used = [sem(f"slab_used_{s}") for s in range(4)]
        silu_done = sem("silu_done")
        ada_prod = Count(sem("ada_products"), 4)
        ada_copy = Count(sem("ada_copied"), 4, primed=1)
        late_prod = Count(sem("late_ada_products"), HP, 2)
        late_copy = Count(sem("late_ada_copied"), HP, 2, primed=1)
        sq_made = Count(sem("squares_made"), 8)
        sq_used = Count(sem("squares_used"), 8)
        rs_made = sem("rms_made")
        ap_scaled = Count(sem("norm_scaled"), 4, 2)
        ap_shift = Count(sem("norm_shifted"), 4, 2, primed=2)

        segs_of = lambda l, all_tokens=False: [0, 1] if (l == 0 or all_tokens) else [1]
        nbar = {}
        PHASES = 9
        TOTAL_BARRIERS = PHASES * DEPTH

        def phase_barrier(e, name):
            nbar[name] = nbar.get(name, 0) + 1
            e.drain().then_inc(phase_end, 1)
            e.wait_ge(phase_end, 4 * nbar[name])

        STREAM = []
        for l in range(DEPTH):
            if l == 0:
                STREAM.append(((l, "ada"), 4, (1, 1, 1, 1)))
            STREAM.append(((l, "lora"), 1, (1, 1, 0, 0)))
            STREAM.append(((l, "rwkv"), HP, (3 + NBLK, 3 + NBLK, 3 + NBLK, 1) if l == 0 else (3 + NBLK, 3, 3, 1)))
            if l == 0:
                STREAM.append(((l, "late_ada"), HP, (2, 2, 2, 2)))
            STREAM.append(((l, "merge"), KD // 2, (2, 2, 2, 0)))
            STREAM.append(((l, "out"), 2, (1, 1, 1, 1)))
            STREAM.append(((l, "ffn_in"), NJ // 2, (1, 1, 1, 1)))
            STREAM.append(((l, "ffn_out"), KD, (1, 1, 1, 0)))
        before, sofar = {}, [0] * 4
        for key, passes, uses in STREAM:
            before[key] = (list(sofar), uses)
            sofar = [n + passes * u for n, u in zip(sofar, uses)]

        def nth(l, phase, s, i, k):
            base, uses = before[l, phase]
            return i * uses[s] + (base[s] + k)

        def wait_slab(pe, l, phase, s, i, k=0):
            pe.wait_ge(slab_full[s], nth(l, phase, s, i, k) * 16 + 16)

        def block(s, j):
            return slots[s][:, j * P:(j + 1) * P]

        def products(outs, blocks, rhs, segs, done_before=None):
            for s in segs:
                for k, w in enumerate(blocks):
                    last = nc.tensor.matmul(outs[s], w, rhs(k, s), start=(k == 0), stop=(k == len(blocks) - 1))
                    if done_before is not None:
                        last.then_inc(done_before, 1)
                        done_before = None
            return last

        def slot_blocks(s, n=KD):
            return [block(s, k) for k in range(n)]

        def hx_rhs(k, s):
            return HX[:, k, SEGS[s][0]:SEGS[s][1]]

        def pair(i, width=(CTX, SEQ)):
            return [bank[i][:, 0:width[0]], bank[i + 1][:, 0:width[1]]]

        def sync_program(sp):
            def load(l, phase, s, i, k, src, cols=8 * P):
                sp.wait_ge(slab_used[s], nth(l, phase, s, i, k) + 1)
                sp.dma_start(slots[s][:, 0:cols], src.rearrange("a p n -> p (a n)")).then_inc(slab_full[s], 16)

            def tile(name, l, j):
                return a[name][l, bass.ds(j, 1), :, :]

            for l in range(DEPTH):
                if l == 0:
                    with sp.Fori(0, 4) as i:
                        for s in range(4):
                            load(l, "ada", s, i, 0, tile("w_ada", l, i * 4 + s))
                for s in range(2):
                    load(l, "lora", s, 0, 0, a["w_lora"][l, s:s + 1, :, :])
                with sp.Fori(0, HP) as hp:
                    for s in range(4):
                        load(l, "rwkv", s, hp, 0, tile("w_heads", l, hp * 4 + s))
                    for g in range(6):
                        load(l, "rwkv", g % 3, hp, 1 + g // 3, tile("w_gate", l, hp * 6 + g))
                    with sp.Fori(0, NBLK) as n:
                        load(l, "rwkv", 0, hp, n + 3, tile("w_side", l, hp * NBLK + n))
                        if l == 0:
                            for s in (1, 2):
                                load(l, "rwkv", s, hp, n + 3, tile("w_ada", 1, hp * (2 * NBLK) + n * 2 + (s - 1)))
                if l == 0:
                    with sp.Fori(0, HP) as hp:
                        for k in range(2):
                            for s in range(4):
                                load(l, "late_ada", s, hp, k, tile("w_ada", l, hp * 8 + (2 * KD + 4 * k + s)))
                with sp.Fori(0, KD // 2) as i:
                    for b in range(2):
                        for n in range(3):
                            load(l, "merge", n, i, b, tile("w_up", l, i * 6 + (3 * b + n)), KM * P)
                with sp.Fori(0, 2) as i:
                    for s in range(4):
                        load(l, "out", s, i, 0, tile("w_out", l, i * 4 + s))
                with sp.Fori(0, NJ // 2) as i:
                    for s in range(4):
                        load(l, "ffn_in", s, i, 0, tile("w_ffn_in", l, i * 4 + s))
                with sp.Fori(0, KD) as i:
                    for s, (k0, k1) in enumerate(FFN_K):
                        load(l, "ffn_out", s, i, 0, a["w_ffn_out"][l, bass.ds(i, 1), :, k0 * P:k1 * P], (k1 - k0) * P)

        FFN_K = [(0, 8), (8, 16), (16, 22)]

        def ada_tile(s, out):
            for k in range(KD):
                last = nc.tensor.matmul(out, block(s, k), CIN[:, k, :], start=(k == 0), stop=(k == KD - 1))
            return last

        def add_bias(l, j, n, ps):
            return nc.vector.tensor_tensor(MOD[l][:, bass.ds(j, n), :], ps.rearrange("p (j s) -> p j s", s=2),
                                           bada[:, bass.ds(j + l * NADA, n)].unsqueeze(2).to_broadcast([P, n, 2]), ALU.add)

        def ada_pe(pe, l):
            pe.wait_ge(silu_done, 1)
            with pe.Fori(0, 4) as i:
                pe.wait_ge(ada_copy.sem, ada_copy.free(l, i))
                for s in range(4):
                    wait_slab(pe, l, "ada", s, i)
                    ada_tile(s, bank[0][:, 2 * s:2 * s + 2]).then_inc(slab_used[s], 1)
                nc.tensor.drain().then_inc(ada_prod.sem, 1)

        def ada_dve(dve, l):
            if l == 0:
                dve.sem_inc(ada_copy.sem, 1)
                with dve.Fori(0, 4) as i:
                    dve.wait_ge(ada_prod.sem, ada_prod.ready(l, i))
                    add_bias(l, i * 4, 4, bank[0][:, 0:8]).then_inc(ada_copy.sem, 1)
                dve.drain()
            dve.wait_ge(s_wload, 16 * (l + 1))
            scales(dve, l, range(1) if l == 0 else range(4))

        def scales(dve, l, which):
            for n in which:
                part, is_scale = [(1, True), (2, False), (4, True), (5, False)][n]
                g = vec[:, V_NG + n * KD:V_NG + (n + 1) * KD].unsqueeze(2).to_broadcast([P, KD, 2])
                nc.vector.scalar_tensor_tensor(out=DER[l][:, n], in0=MOD[l][:, part * KD:(part + 1) * KD, :], scalar=1.0 if is_scale else 0.0,
                                               in1=g, op0=ALU.add, op1=ALU.mult)
            dve.drain()

        def stats_act(act, use, src, segs):
            lo, hi = SEGS[segs[0]][0], T
            for k in range(KD):
                if k >= 2:
                    act.wait_ge(sq_used.sem, sq_used.ready(use, k - 2))
                nc.scalar.activation(NSQ[k % 2][:, lo:hi], src(k)[:, lo:hi], ACT.Square).then_inc(sq_made.sem, 1)
            act.wait_ge(sq_used.sem, sq_used.ready(use, KD - 1))
            for s in segs:
                nc.scalar.activation(NRS[:, SEGS[s][0]:SEGS[s][1]], pair(0)[s], ACT.Ln, bias=one[:, 0:1])
            act.drain()
            nc.scalar.activation(NRS[:, lo:hi], NRS[:, lo:hi], ACT.Exp, scale=-0.5).then_inc(rs_made, 1)

        def stats_pe(pe, use, segs):
            for k in range(KD):
                pe.wait_ge(sq_made.sem, sq_made.ready(use, k))
                for s in segs:
                    last = nc.tensor.matmul(pair(0)[s], MEAN_D, NSQ[k % 2][:, SEGS[s][0]:SEGS[s][1]], start=(k == 0), stop=(k == KD - 1))
                last.then_inc(sq_used.sem, 1)

        def norm_dve(dve, use, half, segs):
            lo = SEGS[segs[0]][0]
            dve.wait_ge(rs_made, 2 * use + 1)
            with dve.Fori(0, KD // 2) as i:
                for b in range(2):
                    dve.wait_ge(ap_shift.sem, ap_shift.free(use, i, b + 1))
                    nc.vector.tensor_tensor(NTMP[b][:, lo:T], RES[:, bass.ds(i * 2 + b, 1), lo:T].rearrange("p a t -> p (a t)"), NRS[:, lo:T], ALU.mult)\
                      .then_inc(ap_scaled.sem, 1)

        def norm_act(act, use, half, segs):
            act.sem_inc(ap_shift.sem, 2)
            with act.Fori(0, KD // 2) as i:
                for b in range(2):
                    act.wait_ge(ap_scaled.sem, ap_scaled.ready(use, i, b + 1))
                    for s in segs:
                        gain = ders[use // 2][:, bass.ds((i * 2 + b) * 2 + (half * 2 * KD * 2 + s), 1)]
                        shift = mods[use // 2][:, bass.ds((i * 2 + b) * 2 + (half * 3 * KD * 2 + s), 1)]
                        last = nc.scalar.activation(HX[:, bass.ds(i * 2 + b, 1), SEGS[s][0]:SEGS[s][1]].rearrange("p a t -> p (a t)"),
                                                    NTMP[b][:, SEGS[s][0]:SEGS[s][1]], ACT.Identity, bias=shift, scale=gain)
                    last.then_inc(ap_shift.sem, 1)

        def add_dve(dve, use, half, segs, Y):
            lo = SEGS[segs[0]][0]
            dve.wait_ge(rs_made, 2 * use + 2)
            with dve.Fori(0, KD) as k:
                nc.vector.tensor_tensor(NTMP[0][:, lo:T], Y[:, bass.ds(k, 1), lo:T].rearrange("p a t -> p (a t)"), NRS[:, lo:T], ALU.mult)
                dve.drain()
                for s in segs:
                    x = RES[:, bass.ds(k, 1), SEGS[s][0]:SEGS[s][1]].rearrange("p a t -> p (a t)")
                    nc.vector.scalar_tensor_tensor(out=x, in0=NTMP[0][:, SEGS[s][0]:SEGS[s][1]],
                                                   scalar=ders[use // 2][:, bass.ds(k * 2 + ((half * 2 + 1) * KD * 2 + s), 1)], in1=x, op0=ALU.mult, op1=ALU.add)
                dve.drain()

        side_loaded = sem("side_projections_loaded")
        side_copied = sem("side_gates_used")
        cw = Carve(WS0 + 2 * SEQ + 3 * 256 + 12 * T)
        CT = cw(3 * HP * T).rearrange("p (j t) -> p j t", j=3 * HP)
        ZP = cw(T + 3)
        CA = cw(T)
        ZSEG = [(1, 1 + CTX), (2 + CTX, 2 + T)]

        def conv_dve(dve, l):
            nc.vector.memset(ZP, 0.0)
            dve.drain()
            dve.wait_ge(side_loaded, 32 * l + 32)
            with dve.Fori(0, HP) as i:
                def tile(j, s):
                    return CT[:, bass.ds(i + j * HP, 1), SEGS[s][0]:SEGS[s][1]].rearrange("p a t -> p (a t)")

                for s in segs_of(l):
                    nc.vector.tensor_tensor(ZP[:, ZSEG[s][0]:ZSEG[s][1]], tile(1, s), tile(2, s), ALU.mult)
                dve.drain()
                w = [vec[:, bass.ds(i + (V_CW + j * HP), 1)] for j in range(3)]
                for s in segs_of(l):
                    (c0, c1), (z0, z1) = SEGS[s], ZSEG[s]
                    nc.vector.tensor_scalar(CA[:, c0:c1], ZP[:, z0:z1], w[1], None, ALU.mult)
                dve.drain()
                for j, off in ((0, -1), (2, 1)):
                    for s in segs_of(l):
                        (c0, c1), (z0, z1) = SEGS[s], ZSEG[s]
                        nc.vector.scalar_tensor_tensor(out=CA[:, c0:c1], in0=ZP[:, z0 + off:z1 + off], scalar=w[j], in1=CA[:, c0:c1], op0=ALU.mult, op1=ALU.add)
                    dve.drain()
                for s in segs_of(l):
                    c0, c1 = SEGS[s]
                    nc.vector.tensor_tensor(BR[:, 0, bass.ds(i, 1), c0:c1].rearrange("p a t -> p (a t)"), tile(0, s), CA[:, c0:c1], ALU.mult)
                dve.drain()

        rw = Carve(2 * HP * T)
        RC = rw(2 * 256 + 2 * 6 * P + 2 * T)
        GMASK = [RC[:, 0:256], RC[:, 256:512]]
        LOWER = [RC[:, 512 + j * P:512 + (j + 1) * P] for j in range(6)]
        UPPER = [RC[:, 512 + (6 + j) * P:512 + (7 + j) * P] for j in range(6)]
        KEEP = [RC[:, 512 + 12 * P:512 + 12 * P + T], RC[:, 512 + 12 * P + T:512 + 12 * P + 2 * T]]
        RW_N = 512 + 12 * P + 2 * T
        ZL = rw(T + 3)
        LD = rw(2 * T).rearrange("p (d t) -> p d t", d=2)
        SG, GT, BONUS = rw(T), rw(T), rw(T)
        DD = [rw(NBLK * 5 * P).rearrange("p (b o t) -> p b o t", b=NBLK, o=5) for _ in range(2)]
        YD = rw(2 * T).rearrange("p (d t) -> p d t", d=2)
        DC = rw(2 * 2 * NBLK).rearrange("p (d c) -> p d c", d=2)
        ARZ = [rw(512).rearrange("p (h o t) -> p h o t", h=2, o=2) for _ in range(2)]
        BKC = [rw(512).rearrange("p (c o t) -> p c o t", c=2, o=2) for _ in range(2)]
        alias = rw.at
        ZR = [rw(T + 3) for _ in range(3)]
        TMP = [rw(T) for _ in range(8)]
        end_a = rw.at
        rw.at = alias
        STG = [rw(640).rearrange("p (o t) -> p o t", o=5) for _ in range(2)]
        VT = [rw(P) for _ in range(2)]
        NAK = [[rw(512).rearrange("p (h o t) -> p h o t", h=2, o=2) for _ in range(2)] for _ in range(2)]
        XX = [rw(512).rearrange("p (x h t) -> p x h t", x=2, h=2) for _ in range(2)]
        T1 = [rw(256).rearrange("p (h t) -> p h t", h=2) for _ in range(2)]
        WR = [rw(256).rearrange("p (h o j) -> p h o j", h=2, o=2) for _ in range(2)]
        ZQ = [rw(256).rearrange("p (o h j) -> p o h j", o=2, h=2) for _ in range(2)]
        GS = [rw(P) for _ in range(2)]
        MH = [rw(256).rearrange("p (c t) -> p c t", c=2) for _ in range(2)]
        HDD = [rw(256).rearrange("p (c t) -> p c t", c=2) for _ in range(2)]
        ST = [rw(P) for _ in range(2)]
        DCS = [rw(2) for _ in range(2)]
        rw.at = max(end_a, rw.at)
        SPILL = rw(T)

        rw_tables = sem("rwkv_tables_loaded")
        lora_prod = sem("lora_products")
        lora_copy = sem("lora_copied")
        lora_mix = sem("lora_mixed")
        lora_act = sem("lora_activated")
        hp_prod = Count(sem("head_products"), HP, 4)
        hp_copy = Count(sem("head_copied"), HP, 2)
        pre_prod = Count(sem("prep_products"), HP, 2 * 3)
        pre_act = Count(sem("prep_activations"), HP, 2 * 4)
        pre_dve = Count(sem("prep_vector"), HP, 2 * 4)
        NPE, NDV, NAC = 16, 15, 5
        blk_pe = [Count(sem(f"block_products_{n}"), HP * NBLK, NPE) for n in ("fwd", "bwd")]
        blk_dve = [Count(sem(f"block_vector_{n}"), HP * NBLK, NDV, primed=1) for n in ("fwd", "bwd")]
        blk_act = [Count(sem(f"block_copies_{n}"), HP * NBLK, NAC) for n in ("fwd", "bwd")]
        post_dve = Count(sem("readout_vector"), HP, 2)
        post_pe = Count(sem("readout_products"), HP, 2)
        post_act = Count(sem("readout_activations"), HP, 2)

        def lora_pe(pe, l):
            wait_slab(pe, l, "lora", 0, 0)
            products(pair(0), slot_blocks(0), hx_rhs, [0, 1]).then_inc(lora_prod, 1)
            wait_slab(pe, l, "lora", 1, 0)
            products(pair(2), slot_blocks(1), hx_rhs, [0, 1], slab_used[0]).then_inc(lora_prod, 1)
            nc.tensor.drain().then_inc(slab_used[1], 1)

        def lora_act_(act, l):
            act.wait_ge(lora_mix, 3 * l + 1)
            act.wait_ge(lora_prod, 2 * l + 1)
            for s in range(2):
                nc.scalar.activation(ZL[:, ZSEG[s][0]:ZSEG[s][1]], pair(0)[s], ACT.Copy)
            act.drain().then_inc(lora_copy, 1)
            act.wait_ge(lora_prod, 2 * l + 2)
            for s in range(2):
                nc.scalar.activation(SG[:, SEGS[s][0]:SEGS[s][1]], pair(2)[s], ACT.Sigmoid)
            for d in range(2):
                act.wait_ge(lora_mix, 3 * l + 2 + d)
                last = nc.scalar.activation(LD[0:64, d, :], LD[0:64, d, :], ACT.Tanh)
            last.then_inc(lora_act, 1)

        def mix_ops(dve, Z, mu, d, out):
            off = -1 if d == 0 else 1
            for s in range(2):
                (z0, z1), (o0, o1) = ZSEG[s], DSEG[d][s]
                nc.vector.tensor_tensor(out[:, o0:o1], Z[:, z0 + off:z1 + off], Z[:, z0:z1], ALU.subtract)
            dve.drain()
            for s in range(2):
                (z0, z1), (o0, o1) = ZSEG[s], DSEG[d][s]
                last = nc.vector.scalar_tensor_tensor(out=out[:, o0:o1], in0=out[:, o0:o1], scalar=mu, in1=Z[:, z0:z1], op0=ALU.mult, op1=ALU.add)
            return last

        def lora_dve(dve, l):
            for z in [ZL] + ARZ_FLAT:
                nc.vector.memset(z, 0.0)
            dve.drain().then_inc(lora_mix, 1)
            dve.wait_ge(lora_copy, l + 1)
            for d in range(2):
                mix_ops(dve, ZL, vec[:, V_MUL + d:V_MUL + d + 1], d, LD[:, d, :]).then_inc(lora_mix, 1)
            nc.vector.tensor_scalar(OMKA, vec[:, V_KA:V_KA + HP], -1.0, 1.0, ALU.mult, ALU.add)

        ARZ_FLAT = [x.rearrange("p h o t -> p (h o t)") for x in ARZ + BKC]
        omka = sb("omka", HP)
        OMKA = omka[:, :]

        def blocked(x):
            return x.rearrange("p (b t) -> p b t", b=NBLK)

        tile_copied = Count(sem("side_tiles_copied"), HP, 6 + NBLK)
        spilled = Count(sem("side_tiles_in_dram"), HP, 16 * (6 + NBLK))
        spill_free = Count(sem("side_buffer_free"), HP, 6 + NBLK, primed=1)

        def heads_pe(pe, l, hp):
            for t in range(3):
                wait_slab(pe, l, "rwkv", t, hp)
                products(pair(2 * t), slot_blocks(t), hx_rhs, [0, 1], slab_used[t - 1] if t else None).then_inc(hp_prod.sem, 1)
            wait_slab(pe, l, "rwkv", 3, hp)
            products(pair(6), [block(3, 2)], lambda k, s: SG[:, SEGS[s][0]:SEGS[s][1]], [0, 1], slab_used[2]).then_inc(hp_prod.sem, 1)
            pe.wait_ge(hp_copy.sem, hp_copy.ready(l, hp, 2))

            def gate_tile(g):
                wait_slab(pe, l, "rwkv", g % 3, hp, 1 + g // 3)
                if g >= 2:
                    pe.wait_ge(tile_copied.sem, tile_copied.ready(l, hp, g - 1))
                products(pair(4 + 2 * (g % 2)), slot_blocks(g % 3), hx_rhs, segs_of(l)).then_inc(gate_prod.sem, 1)

            for d in range(2):
                if d == 1:
                    pe.wait_ge(pre_dve.sem, pre_dve.ready(l, hp, 4))
                for rows, b in ((slice(0, 64), 0), (slice(64, 128), 2)):
                    for s in range(2):
                        o0, o1 = DSEG[d][s]
                        last = nc.tensor.matmul(pair(b)[s], block(3, d)[rows], LD[rows, d, o0:o1], start=True, stop=True)
                last.then_inc(pre_prod.sem, 1)
                gate_tile(3 * d)
                pe.wait_ge(pre_act.sem, pre_act.ready(l, hp, 4 * d + 2))
                for s in range(2):
                    o0, o1 = DSEG[d][s]
                    last = nc.tensor.matmul(pair(0)[s], SAME, TMP[6][:, o0:o1], start=True, stop=True)
                last.then_inc(pre_prod.sem, 1)
                nc.tensor.drain().then_inc(slab_used[0], 1)
                gate_tile(3 * d + 1)
                pe.wait_ge(pre_dve.sem, pre_dve.ready(l, hp, 4 * d + 3))
                for s in range(2):
                    o0, o1 = DSEG[d][s]
                    last = nc.tensor.matmul(pair(2)[s], SAME, TMP[6][:, o0:o1], start=True, stop=True)
                last.then_inc(pre_prod.sem, 1)
                nc.tensor.drain().then_inc(slab_used[1], 1)
                gate_tile(3 * d + 2)
                nc.tensor.drain().then_inc(slab_used[2], 1)
            nc.tensor.drain().then_inc(slab_used[3], 1)

        gate_prod = Count(sem("gate_tile_products"), HP, 6)

        def copy_tile(act, l, hp, k, ps, segs, done):
            act.wait_ge(spill_free.sem, spill_free.free(l, hp, k))
            for s in segs:
                last = nc.scalar.activation(SPILL[:, SEGS[s][0]:SEGS[s][1]], ps[s], ACT.Copy)
            last.then_inc(done, 1)

        def spill_pool(pool, l):
            pool.sem_inc(spill_free.sem, 1)
            lo = 0 if l == 0 else CTX
            with pool.Fori(0, HP) as hp:
                for g in range(6):
                    pool.wait_ge(tile_copied.sem, tile_copied.ready(l, hp, g + 1))
                    pool.dma_start(gates_dram[bass.ds(hp * 6 + g, 1), :, lo:T].rearrange("a p t -> p (a t)"), SPILL[:, lo:T]).then_inc(spilled.sem, 16)
                    pool.wait_ge(spilled.sem, spilled.ready(l, hp, 16 * (g + 1)))
                    pool.sem_inc(spill_free.sem, 1)
                with pool.Fori(0, NBLK) as n:
                    pool.wait_ge(tile_copied.sem, tile_copied.ready(l, hp, 7) + n)
                    pool.dma_start(side_dram[bass.ds(hp * NBLK + n, 1), :, :].rearrange("a p t -> p (a t)"), SPILL).then_inc(spilled.sem, 16)
                    pool.wait_ge(spilled.sem, spilled.ready(l, hp, 16 * 7) + n * 16)
                    pool.sem_inc(spill_free.sem, 1)

        def heads_act(act, l, hp):
            act.wait_ge(zr_clear.sem, zr_clear.ready(l, hp))
            for t in range(3):
                act.wait_ge(hp_prod.sem, hp_prod.ready(l, hp, t + 1))
                for s in range(2):
                    nc.scalar.activation(ZR[t][:, ZSEG[s][0]:ZSEG[s][1]], pair(2 * t)[s], ACT.Copy)
            act.drain().then_inc(hp_copy.sem, 1)
            act.wait_ge(hp_prod.sem, hp_prod.ready(l, hp, 4))
            for s in range(2):
                nc.scalar.activation(GT[:, SEGS[s][0]:SEGS[s][1]], pair(6)[s], ACT.Copy)
            act.drain().then_inc(hp_copy.sem, 1)
            def gate_copy(g):
                act.wait_ge(gate_prod.sem, gate_prod.ready(l, hp, g + 1))
                copy_tile(act, l, hp, g + 1, pair(4 + 2 * (g % 2)), segs_of(l), tile_copied.sem)

            for d in range(2):
                act.wait_ge(pre_prod.sem, pre_prod.ready(l, hp, 3 * d + 1))
                if d == 1:
                    act.wait_ge(pre_dve.sem, pre_dve.ready(l, hp, 4))
                for s in range(2):
                    o0, o1 = DSEG[d][s]
                    nc.scalar.activation(TMP[3][:, o0:o1], pair(0)[s], ACT.Sigmoid, bias=vec[:, bass.ds(hp + (V_W0 + d * HP), 1)])
                    nc.scalar.activation(TMP[5][:, o0:o1], pair(2)[s], ACT.Sigmoid, bias=vec[:, bass.ds(hp + (V_A0 + d * HP), 1)])
                act.drain().then_inc(pre_act.sem, 1)
                act.wait_ge(pre_dve.sem, pre_dve.ready(l, hp, 4 * d + 1))
                nc.scalar.activation(TMP[6], TMP[7], ACT.Square).then_inc(pre_act.sem, 1)
                gate_copy(3 * d)
                act.wait_ge(pre_dve.sem, pre_dve.ready(l, hp, 4 * d + 2))
                nc.scalar.activation(TMP[6], TMP[6], ACT.Ln)
                act.drain()
                nc.scalar.activation(TMP[6], TMP[6], ACT.Exp, scale=-0.5)
                nc.scalar.activation(E3, E3, ACT.Exp, scale=-DECAY)
                nc.scalar.activation(E2, TMP[4], ACT.Exp, scale=DECAY)
                act.drain()
                nc.scalar.activation(TMP[4], TMP[4], ACT.Exp, scale=-DECAY).then_inc(pre_act.sem, 1)
                act.drain()
                last_tok = TMP[4].rearrange("p (c t) -> p c t", t=CHUNK)[:, :, CHUNK - 1 if d == 0 else 0]
                nc.scalar.activation(DC[:, d, :], last_tok, ACT.Copy).then_inc(pre_act.sem, 1)
                gate_copy(3 * d + 1)
                gate_copy(3 * d + 2)

        E2, E3 = YD[:, 0, :], YD[:, 1, :]
        zr_clear = Count(sem("head_pads_cleared"), HP, 1)

        def heads_dve(dve, l, hp):
            mu = lambda d, o: vec[:, bass.ds(hp + (V_MU + (d * 3 + o) * HP), 1)]
            for z in ZR:
                nc.vector.memset(z, 0.0)
            dve.drain().then_inc(zr_clear.sem, 1)
            dve.wait_ge(hp_copy.sem, hp_copy.ready(l, hp, 1))
            for d in range(2):
                if d == 1:
                    dve.wait_ge(pre_act.sem, pre_act.ready(l, hp, 4))
                for o in range(3):
                    mix_ops(dve, ZR[o], mu(d, o), d, TMP[o])
                dve.drain()
                nc.vector.tensor_scalar(TMP[7], TMP[1], vec[:, bass.ds(hp + V_KK, 1)], None, ALU.mult).then_inc(pre_dve.sem, 1)
                nc.vector.tensor_copy(DD[d][:, :, 4, :], blocked(TMP[2]))
                dve.wait_ge(pre_act.sem, pre_act.ready(l, hp, 4 * d + 1))
                sl = slice(None) if d == 0 else slice(None, None, -1)
                nc.vector.tensor_tensor_scan(TMP[4][:, sl], KEEP[d][:, sl], TMP[3][:, sl], 0.0, ALU.mult, ALU.add)
                dve.drain()
                nc.vector.tensor_tensor(E3, TMP[4], TMP[3], ALU.subtract)
                dve.wait_ge(pre_prod.sem, pre_prod.ready(l, hp, 3 * d + 2))
                for s in range(2):
                    o0, o1 = DSEG[d][s]
                    nc.vector.tensor_scalar(TMP[6][:, o0:o1], pair(0)[s], 1e-24, None, ALU.max)
                dve.drain().then_inc(pre_dve.sem, 1)
                nc.vector.tensor_scalar(TMP[3], TMP[5], vec[:, bass.ds(hp + V_KA, 1)], omka[:, bass.ds(hp, 1)], ALU.mult, ALU.add)
                dve.drain()
                nc.vector.tensor_tensor(TMP[1], TMP[1], TMP[3], ALU.mult)
                dve.wait_ge(pre_act.sem, pre_act.ready(l, hp, 4 * d + 3))
                nc.vector.tensor_tensor(TMP[7], TMP[7], TMP[6], ALU.mult)
                dve.drain()
                nc.vector.scalar_tensor_tensor(out=TMP[6], in0=TMP[0], scalar=vec[:, bass.ds(hp + V_RK, 1)], in1=TMP[1], op0=ALU.mult, op1=ALU.mult)\
                  .then_inc(pre_dve.sem, 1)
                nc.vector.tensor_tensor(DD[d][:, :, 3, :], blocked(TMP[1]), blocked(E2), ALU.mult)
                nc.vector.tensor_tensor(DD[d][:, :, 1, :], blocked(TMP[0]), blocked(TMP[4]), ALU.mult)
                nc.vector.scalar_tensor_tensor(out=DD[d][:, :, 0, :], in0=blocked(TMP[7]), scalar=-1.0, in1=blocked(E3), op0=ALU.mult, op1=ALU.mult)
                nc.vector.tensor_tensor(TMP[5], TMP[7], TMP[5], ALU.mult)
                dve.drain()
                nc.vector.tensor_tensor(DD[d][:, :, 2, :], blocked(TMP[5]), blocked(E2), ALU.mult)
                dve.wait_ge(pre_prod.sem, pre_prod.ready(l, hp, 3 * d + 3))
                for s in range(2):
                    (o0, o1), (c0, c1) = DSEG[d][s], SEGS[s]
                    dst = BONUS[:, c0:c1] if d == 0 else TMP[6][:, c0:c1]
                    nc.vector.tensor_tensor(dst, pair(2)[s], TMP[2][:, o0:o1], ALU.mult)
                dve.drain()
                if d == 1:
                    nc.vector.tensor_tensor(BONUS, BONUS, TMP[6], ALU.add)
                dve.drain().then_inc(pre_dve.sem, 1)
            for d in range(2):
                nc.vector.memset(ST[d], 0.0)

        def at_block(d, n):
            return n if d == 0 else (NBLK - 1) - n

        def block_pe(pe, l, hp, n):
            it = hp * NBLK + n
            b = lambda d, j: bank[3 * d + j]

            def side(j):
                k, s = divmod(j, 2)
                if j == 0:
                    wait_slab(pe, l, "rwkv", 0, hp, n + 3)
                    pe.wait_ge(tile_copied.sem, tile_copied.ready(l, hp, 6) + n)
                last = nc.tensor.matmul(pair(6)[s], block(0, k), hx_rhs(k, s), start=(k == 0), stop=(k == KD - 1))
                if j == 15:
                    last.then_inc(side_prod.sem, 1)

            def step(d, last, k):
                last.then_inc(blk_pe[d].sem, 1)

            def on_dve(d, k):
                pe.wait_ge(blk_dve[d].sem, blk_dve[d].ready(l, it, k))

            def on_act(d, k):
                pe.wait_ge(blk_act[d].sem, blk_act[d].ready(l, it, k))

            for d in range(2):
                on_act(d, 1)
                on_dve(d, 0)
                for j, o in enumerate((0, 2, 3, 4)):
                    nc.tensor.transpose(b(d, 0)[:, j * P:(j + 1) * P], STG[d][:, o, :], IDENT)
                rhs = ARZ[d].rearrange("p h o t -> p (h o t)")
                nc.tensor.matmul(b(d, 1)[:, :], STG[d][:, 2, :], rhs, start=True, stop=True)
                step(d, nc.tensor.matmul(b(d, 2)[:, :], STG[d][:, 3, :], rhs, start=True, stop=True), 1)
            side(0)
            for d in range(2):
                on_dve(d, 1)
                on_act(d, 2)
                for h in range(2):
                    nc.tensor.matmul(b(d, 0)[:, h * P:(h + 1) * P], NAK[d][0][:, h, 0, :], IDENT, start=True, stop=True)
                    last = nc.tensor.matmul(b(d, 2)[:, h * P:(h + 1) * P], NAK[d][1][:, h, 0, :], VT[d], start=True, stop=True)
                step(d, last, 2)
            side(1)
            for m in range(1, 6):
                for d in range(2):
                    on_dve(d, 2 * m)
                    for h in range(2):
                        last = nc.tensor.matmul(b(d, 1)[:, h * P:(h + 1) * P], NAK[d][0][:, h, 0, :], XX[d][:, 0, h, :], start=True, stop=True)
                    step(d, last, 2 * m + 1)
                side(2 * m)
                for d in range(2):
                    on_dve(d, 2 * m + 1)
                    if m == 1:
                        on_act(d, 3)
                    for h in range(2):
                        if m < 5:
                            nc.tensor.matmul(b(d, 2)[:, h * P:(h + 1) * P], XX[d][:, 1, h, :], T1[d][:, h, :], start=True, stop=True)
                        last = nc.tensor.matmul(b(d, 2)[:, (2 + h) * P:(3 + h) * P], T1[d][:, h, :], XX[d][:, 1, h, :], start=True, stop=True)
                    step(d, last, 2 * m + 2)
                side(2 * m + 1)
            for d in range(2):
                on_dve(d, 12)
                for h in range(2):
                    last = nc.tensor.matmul(b(d, 0)[:, h * P:(h + 1) * P], XX[d][:, 1, h, :], WR[d][:, h].rearrange("p o j -> p (o j)"), start=True, stop=True)
                step(d, last, 13)
            side(12)
            for d in range(2):
                on_act(d, 4)
                for h in range(2):
                    rows = slice(h * HD, (h + 1) * HD)
                    nc.tensor.matmul(b(d, 0)[rows, 0:P], ZQ[d][:, 0, h, :], NAK[d][0][:, h, 1, :], start=True, stop=True)
                    nc.tensor.matmul(b(d, 1)[rows, 0:P], ZQ[d][:, 1, h, :], NAK[d][0][:, h, 1, :], start=True, stop=False, skip_group_check=True)
                    nc.tensor.matmul(b(d, 1)[rows, 0:P], VT[d][:, rows], NAK[d][1][:, h, 1, :], start=False, stop=False, skip_group_check=True)
                z = ZQ[d][:, 0].rearrange("p h j -> p (h j)")
                q = ZQ[d][:, 1].rearrange("p h j -> p (h j)")
                for c in range(2):
                    nc.tensor.matmul(b(d, 2)[:, c * P:(c + 1) * P], z, BKC[d][:, c, 0, :], start=True, stop=True)
                for c in range(2):
                    nc.tensor.matmul(b(d, 0)[:, (c + 1) * P:(c + 2) * P], BKC[d][:, c, 0, :], q, start=True, stop=False)
                    last = nc.tensor.matmul(b(d, 0)[:, (c + 1) * P:(c + 2) * P], BKC[d][:, c, 1, :], VT[d], start=False, stop=True)
                step(d, last, 14)
            side(13)
            for j in range(2):
                for d in range(2):
                    if j == 1 and d == 1 and l == 0:
                        on_dve(d, 13)
                        for s in (1, 2):
                            wait_slab(pe, l, "rwkv", s, hp, n + 3)
                            ada_tile(s, b(1, 0)[:, 2 * s - 2:2 * s]).then_inc(slab_used[s], 1)
                    c = j if d == 0 else 1 - j
                    cols = slice(c * CHUNK, (c + 1) * CHUNK)
                    on_dve(d, 13 + j)
                    nc.tensor.matmul(b(d, 1)[:, cols], ST[d], GS[d][:, cols], start=False, stop=(j == 1), skip_group_check=True)
                    step(d, nc.tensor.matmul(b(d, 2)[:, j * P:(j + 1) * P], MH[d][:, c, :], ST[d], start=True, stop=True), 15 + j)
                side(14 + j)

        side_prod = Count(sem("side_products"), HP * NBLK)

        def block_act(act, l, hp, n):
            it = hp * NBLK + n
            b = lambda d, j: bank[3 * d + j]
            for d in range(2):
                blk = at_block(d, n)
                act.wait_ge(blk_dve[d].sem, blk_dve[d].ready(l, it, 0))
                nc.scalar.activation(DCS[d], DC[:, d, bass.ds(blk * 2, 2)], ACT.Copy)
                nc.scalar.activation(STG[d].rearrange("p o t -> p (o t)"), DD[d][:, bass.ds(blk, 1)].rearrange("p a o t -> p (a o t)"), ACT.Copy)
                act.drain()
                for h in range(2):
                    rows = slice(h * HD, (h + 1) * HD)
                    nc.scalar.activation(ARZ[d][rows, h].rearrange("p o t -> p (o t)"), STG[d][rows, 0:2, :].rearrange("p o t -> p (o t)"), ACT.Copy)
                act.drain().then_inc(blk_act[d].sem, 1)
            for d in range(2):
                act.wait_ge(blk_pe[d].sem, blk_pe[d].ready(l, it, 1))
                nc.scalar.activation(WR[d][:, :, 0, :], b(d, 0)[:, 0:P].rearrange("p (h j) -> p h j", h=2), ACT.Copy)
                nc.scalar.activation(VT[d], b(d, 0)[:, 3 * P:4 * P], ACT.Copy)
                for c in range(2):
                    rows = slice(c * CHUNK, (c + 1) * CHUNK)
                    last = nc.scalar.activation(BKC[d][rows, c].rearrange("p o t -> p (o t)"), b(d, 0)[rows, P:3 * P], ACT.Copy)
                last.then_inc(blk_act[d].sem, 1)
            for d in range(2):
                act.wait_ge(blk_pe[d].sem, blk_pe[d].ready(l, it, 2))
                for h in range(2):
                    last = nc.scalar.activation(WR[d][:, h, 1, :], b(d, 2)[:, h * (P + HD):h * (P + HD) + HD], ACT.Copy)
                last.then_inc(blk_act[d].sem, 1)
            for d in range(2):
                act.wait_ge(blk_pe[d].sem, blk_pe[d].ready(l, it, 13))
                nc.scalar.activation(ZQ[d].rearrange("p o h j -> p h o j"), b(d, 0)[:, 0:256].rearrange("p (h o j) -> p h o j", h=2, o=2), ACT.Copy)\
                  .then_inc(blk_act[d].sem, 1)
            for d in range(2):
                act.wait_ge(blk_pe[d].sem, blk_pe[d].ready(l, it, 16))
                nc.scalar.activation(YD[:, d, bass.ds(at_block(d, n) * P, P)], b(d, 1)[:, 0:P], ACT.Copy).then_inc(blk_act[d].sem, 1)
            act.wait_ge(side_prod.sem, side_prod.ready(l, it))
            act.wait_ge(spill_free.sem, spill_free.free(l, hp, 7) + n)
            nc.scalar.activation(SPILL[:, 0:CTX], pair(6)[0], ACT.Copy).then_inc(slab_used[0], 1)
            nc.scalar.activation(SPILL[:, CTX:T], pair(6)[1], ACT.Copy).then_inc(tile_copied.sem, 1)

        def block_dve(dve, l, hp, n):
            it = hp * NBLK + n
            b = lambda d, j: bank[3 * d + j]

            def bc(x, n):
                return x.unsqueeze(1).to_broadcast([P, n] + list(x.shape[1:]))

            def on_pe(d, k):
                dve.wait_ge(blk_pe[d].sem, blk_pe[d].ready(l, it, k))

            for d in range(2):
                on_pe(d, 1)
                for j in range(2):
                    last = nc.vector.tensor_tensor(NAK[d][j].rearrange("p h o t -> p h (o t)"), b(d, 1 + j)[:, :].rearrange("p (h t) -> p h t", h=2), bc(GMASK[d], 2), ALU.mult)
                last.then_inc(blk_dve[d].sem, 1)
            for d in range(2):
                on_pe(d, 2)
                low, up = (LOWER, UPPER) if d == 0 else (UPPER, LOWER)
                nc.vector.tensor_tensor(XX[d][:, 0], b(d, 0)[:, 0:256].rearrange("p (h t) -> p h t", h=2), bc(low[0], 2), ALU.mult)
                nc.vector.tensor_tensor(XX[d][:, 1], NAK[d][0][:, :, 0, :], bc(up[0], 2), ALU.mult)
                dve.drain()
                xx = XX[d].rearrange("p x h t -> p (x h) t")
                nc.vector.tensor_tensor(xx, xx, bc(IDENT, 4), ALU.add).then_inc(blk_dve[d].sem, 1)
            for m in range(1, 6):
                for d in range(2):
                    on_pe(d, 2 * m + 1)
                    low = LOWER if d == 0 else UPPER
                    nc.vector.tensor_tensor(T1[d], b(d, 1)[:, 0:256].rearrange("p (h t) -> p h t", h=2), bc(low[m], 2), ALU.mult).then_inc(blk_dve[d].sem, 1)
                for d in range(2):
                    on_pe(d, 2 * m + 2)
                    if m < 5:
                        x, ps = XX[d].rearrange("p x h t -> p (x h t)"), b(d, 2)[:, :]
                    else:
                        x, ps = XX[d][:, 1].rearrange("p h t -> p (h t)"), b(d, 2)[:, 256:512]
                    nc.vector.tensor_tensor(x, x, ps, ALU.add).then_inc(blk_dve[d].sem, 1)
            for d in range(2):
                on_pe(d, 14)
                nc.vector.tensor_tensor(GS[d], STG[d][:, 1, :], b(d, 0)[:, 0:P], ALU.add)
                nc.vector.tensor_tensor(MH[d], b(d, 2)[:, 0:256].rearrange("p (c t) -> p c t", c=2), bc(SAME, 2), ALU.mult)
                for c in range(2):
                    nc.vector.scalar_tensor_tensor(out=HDD[d][:, c, :], in0=b(d, 0)[:, (c + 1) * P:(c + 2) * P], scalar=DCS[d][:, c:c + 1], in1=SAME, op0=ALU.mult, op1=ALU.mult)
                dve.drain()
                nc.vector.tensor_tensor(MH[d], MH[d], bc(IDENT, 2), ALU.add).then_inc(blk_dve[d].sem, 1)
            for j in range(2):
                for d in range(2):
                    c = j if d == 0 else 1 - j
                    on_pe(d, 15 + j)
                    if j == 1 and d == 1 and l == 0:
                        add_bias(1, hp * (2 * NBLK) + n * 2, 2, b(1, 0)[:, 0:4])
                    nc.vector.scalar_tensor_tensor(out=ST[d], in0=b(d, 2)[:, j * P:(j + 1) * P], scalar=DCS[d][:, c:c + 1], in1=HDD[d][:, c, :], op0=ALU.mult, op1=ALU.add)\
                      .then_inc(blk_dve[d].sem, 1)

        def readout_pe(pe, l, hp):
            for j, src in enumerate((TMP[0], TMP[2])):
                pe.wait_ge(*( (post_dve.sem, post_dve.ready(l, hp, 1)) if j == 0 else (post_act.sem, post_act.ready(l, hp, 1)) ))
                for s in range(2):
                    last = nc.tensor.matmul(pair(2 * j)[s], SAME, src[:, SEGS[s][0]:SEGS[s][1]], start=True, stop=True)
                last.then_inc(post_pe.sem, 1)

        def readout_act(act, l, hp):
            act.wait_ge(post_dve.sem, post_dve.ready(l, hp, 2))
            nc.scalar.activation(TMP[2], TMP[1], ACT.Square).then_inc(post_act.sem, 1)
            act.wait_ge(post_pe.sem, post_pe.ready(l, hp, 2))
            for s in range(2):
                nc.scalar.activation(TMP[3][:, SEGS[s][0]:SEGS[s][1]], pair(2)[s], ACT.Ln, scale=1.0 / HD, bias=one[:, 1:2])
            act.drain()
            nc.scalar.activation(TMP[3], TMP[3], ACT.Exp, scale=-0.5).then_inc(post_act.sem, 1)

        def readout_dve(dve, l, hp, it_last):
            for d in range(2):
                dve.wait_ge(blk_act[d].sem, blk_act[d].ready(l, it_last, NAC))
            for s in range(2):
                (c0, c1), (o0, o1) = SEGS[s], DSEG[1][s]
                nc.vector.tensor_tensor(TMP[0][:, c0:c1], YD[:, 0, c0:c1], YD[:, 1, o0:o1], ALU.add)
            dve.drain().then_inc(post_dve.sem, 1)
            dve.wait_ge(post_pe.sem, post_pe.ready(l, hp, 1))
            for s in range(2):
                c0, c1 = SEGS[s]
                nc.vector.scalar_tensor_tensor(out=TMP[1][:, c0:c1], in0=pair(0)[s], scalar=-1.0 / HD, in1=TMP[0][:, c0:c1], op0=ALU.mult, op1=ALU.add)
            dve.drain().then_inc(post_dve.sem, 1)
            dve.wait_ge(post_act.sem, post_act.ready(l, hp, 2))
            nc.vector.tensor_tensor(TMP[1], TMP[1], TMP[3], ALU.mult)
            dve.drain()
            nc.vector.tensor_scalar(TMP[1], TMP[1], vec[:, bass.ds(hp + V_LG, 1)], vec[:, bass.ds(hp + V_LB, 1)], ALU.mult, ALU.add)
            dve.drain()
            nc.vector.tensor_tensor(TMP[1], TMP[1], BONUS, ALU.add)
            dve.drain()
            nc.vector.tensor_tensor(BR[:, 1, bass.ds(hp, 1), :].rearrange("p a t -> p (a t)"), TMP[1], GT, ALU.mult)
            dve.drain()

        def rwkv_pe(pe, l):
            lora_pe(pe, l)
            pe.wait_ge(lora_act, l + 1)
            pe.wait_ge(rw_tables, 16 * (l + 1))
            with pe.Fori(0, HP) as hp:
                heads_pe(pe, l, hp)
                phase_barrier_in(pe, l, hp, 0)
                with pe.Fori(0, NBLK) as n:
                    block_pe(pe, l, hp, n)
                phase_barrier_in(pe, l, hp, 1)
                readout_pe(pe, l, hp)
                phase_barrier_in(pe, l, hp, 2)

        def rwkv_act(act, l):
            lora_act_(act, l)
            with act.Fori(0, HP) as hp:
                heads_act(act, l, hp)
                phase_barrier_in(act, l, hp, 0)
                with act.Fori(0, NBLK) as n:
                    block_act(act, l, hp, n)
                phase_barrier_in(act, l, hp, 1)
                readout_act(act, l, hp)
                phase_barrier_in(act, l, hp, 2)

        def rwkv_dve(dve, l):
            lora_dve(dve, l)
            for d in range(2):
                dve.sem_inc(blk_dve[d].sem, 1)
            dve.wait_ge(rw_tables, 16 * (l + 1))
            with dve.Fori(0, HP) as hp:
                heads_dve(dve, l, hp)
                phase_barrier_in(dve, l, hp, 0)
                with dve.Fori(0, NBLK) as n:
                    block_dve(dve, l, hp, n)
                phase_barrier_in(dve, l, hp, 1)
                readout_dve(dve, l, hp, hp * NBLK + (NBLK - 1))
                phase_barrier_in(dve, l, hp, 2)

        head_stage = Count(sem("engines_at_head_stage"), HP, 9)

        stages_entered = sem("head_stages_entered")

        def phase_barrier_in(e, l, hp, j):
            e.drain().then_inc(head_stage.sem, 1)
            e.wait_ge(head_stage.sem, head_stage.ready(l, hp, 3 * (j + 1)))
            e.sem_inc(stages_entered, 1)

        at = Carve(WS0)
        AC = at(2 * SEQ + 3 * 256)
        COS, SIN = AC[:, 0:SEQ], AC[:, SEQ:2 * SEQ]
        NEG = [AC[:, 2 * SEQ + j * 256:2 * SEQ + (j + 1) * 256] for j in range(3)]
        QKV = at(12 * T).rearrange("p (j t) -> p j t", j=12)
        QZ = at(2 * 2 * SEQ).rearrange("p (e o q) -> p e o q", e=2, o=2)
        QC = at(2 * CTX).rearrange("p (e q) -> p e q", e=2)
        KR = at(SEQ)
        VS = at(T)
        VA = at(9 * P).rearrange("p (j c) -> p j c", j=9)
        RT = [at(SEQ), at(SEQ)]
        BIAS = at(2 * GR * BX).rearrange("p (e r x) -> p e r x", e=2, r=GR)
        BN = at(2 * 3 * 256).rearrange("p (e v c r) -> p e v c r", e=2, v=3, c=KCOLS)
        SX = [at(512) for _ in range(2)]
        PX = [at(512) for _ in range(2)]
        PT = [at(512) for _ in range(2)]
        SM = [at(4) for _ in range(2)]

        at_tables = sem("attention_tables_loaded")
        bias_load = sem("bias_loaded")
        a_clear = sem("attention_cleared")
        a_bias = Count(sem("bias_masked"), HP, 1)
        a_biased = Count(sem("bias_used"), HP, 1, primed=1)
        a_stage = Count(sem("attention_staged"), HP, 1)
        a_swap = Count(sem("attention_swapped"), HP, 3)
        a_rot = Count(sem("attention_rotated"), HP, 3)

        def units(l):
            u = [(g, e, True) for g in range(4) for e in range(2)]
            if l == 0:
                u += [(g, e, False) for g in range(2) for e in range(2)]
            return u

        NU = [12, 8]
        u_score = [Count(sem(f"scores_{l}"), HP, NU[l]) for l in range(2)]
        u_prob = [Count(sem(f"probabilities_{l}"), HP, NU[l]) for l in range(2)]
        u_tr = [Count(sem(f"transposed_{l}"), HP, NU[l]) for l in range(2)]
        u_trc = [Count(sem(f"transposed_copied_{l}"), HP, NU[l]) for l in range(2)]
        u_out = [Count(sem(f"attended_{l}"), HP, NU[l]) for l in range(2)]
        u_ctx = [Count(sem(f"context_scores_copied_{l}"), HP, NU[l]) for l in range(2)]
        u_max = [Count(sem(f"maximum_{l}"), HP, NU[l]) for l in range(2)]
        u_exp = [Count(sem(f"exponentials_{l}"), HP, NU[l]) for l in range(2)]
        u_oc = [Count(sem(f"attended_copied_{l}"), HP, NU[l] // 2) for l in range(2)]

        def col_major(x, reverse=False):
            if reverse:
                x = x[:, ::-1]
            return x.rearrange("p (c r) -> p r c", r=GR)

        def tokens(x):
            return x.rearrange("p (r c) -> p r c", r=GR)

        def q_of(j0, hp, s=1):
            return QKV[:, bass.ds(hp + j0 * HP, 1), SEGS[s][0]:SEGS[s][1]].rearrange("p a t -> p (a t)")

        SB = [4, 5, 6, 7]

        def attn_pe(pe, l):
            pe.wait_ge(at_tables, 16 * (l + 1))
            pe.wait_ge(side_loaded, 32 * l + 32)
            with pe.Fori(0, HP) as hp:
                pe.wait_ge(a_biased.sem, a_biased.free(l, hp))
                for j in range(2):
                    nc.tensor.matmul(bank[j][:, :], PERM, q_of(j, hp), start=True, stop=True).then_inc(a_swap.sem, 1)
                pe.wait_ge(a_stage.sem, a_stage.ready(l, hp))
                for j in range(9):
                    src = VS[:, (j - 7) * P:(j - 6) * P] if j >= 7 else VS[:, CTX + VCOL0[j] * GR:CTX + VCOL0[j] * GR + P]
                    last = nc.tensor.transpose(bank[2 + j // 4][:, (j % 4) * P:(j % 4 + 1) * P], src, IDENT)
                last.then_inc(a_swap.sem, 1)
                pe.wait_ge(a_rot.sem, a_rot.ready(l, hp, 3))
                us = units(l)

                def scores(u):
                    g, e, lat = us[u]
                    sc = bank[u % 2]
                    if u >= 2:
                        pe.wait_ge(u_prob[l].sem, u_prob[l].ready(0, hp, u - 1))
                    if lat:
                        k0 = KEY0[3 - g] * GR
                        nc.tensor.matmul(sc[:, 0:256], QZ[:, e, 0, g * P:(g + 1) * P], KR[:, k0:k0 + 256], start=True, stop=True)
                        last = nc.tensor.matmul(sc[:, 256:512], QZ[:, e, 1, g * P:(g + 1) * P], q_of(1, hp, 0), start=True, stop=True)
                    else:
                        last = nc.tensor.matmul(sc[:, 256:512], QC[:, e, g * P:(g + 1) * P], q_of(1, hp, 0), start=True, stop=True)
                    last.then_inc(u_score[l].sem, 1)

                scores(0)
                scores(1)
                for u, (g, e, lat) in enumerate(us):
                    pe.wait_ge(u_prob[l].sem, u_prob[l].ready(0, hp, u + 1))
                    tb = bank[2 + u % 2]
                    if u >= 2:
                        pe.wait_ge(u_trc[l].sem, u_trc[l].ready(0, hp, u - 1))
                    kts = range(4) if lat else range(2, 4)
                    for kt in kts:
                        last = nc.tensor.transpose(tb[:, kt * P:(kt + 1) * P], PX[u % 2][:, kt * P:(kt + 1) * P], IDENT)
                    last.then_inc(u_tr[l].sem, 1)
                    if u + 2 < len(us):
                        scores(u + 2)
                    pe.wait_ge(u_trc[l].sem, u_trc[l].ready(0, hp, u + 1))
                    if e == 0 and u >= 4:
                        pe.wait_ge(u_oc[l].sem, u_oc[l].ready(0, hp, u // 2 - 1))
                    ob = bank[4 + (u // 2) % 2]
                    rows = slice(e * HD, (e + 1) * HD)
                    k0 = KEY0[3 - g] if lat else 0
                    for kt in kts:
                        v = VA[:, 5 + kt, rows] if kt >= 2 else VA[:, VCOL0.index(k0 + 16 * kt), rows]
                        last = nc.tensor.matmul(ob[rows, 0:P], v, PT[u % 2][:, kt * P:(kt + 1) * P], start=(kt == kts[0]), stop=(kt == 3))
                    last.then_inc(u_out[l].sem, 1)
                    if l == 0 and u in (3, 7):
                        pe.wait_ge(late_copy.sem, late_copy.free(0, hp, u // 4 + 1))
                        for s in range(4):
                            wait_slab(pe, l, "late_ada", s, hp, u // 4)
                            ada_tile(s, bank[7][:, 2 * s:2 * s + 2]).then_inc(slab_used[s], 1)
                        nc.tensor.drain().then_inc(late_prod.sem, 1)
                nc.tensor.drain()

        def attn_act(act, l):
            act.wait_ge(a_clear, l + 1)
            act.wait_ge(side_loaded, 32 * l + 32)
            with act.Fori(0, HP) as hp:
                nc.scalar.activation(VS[:, 0:CTX], q_of(2, hp, 0), ACT.Copy)
                nc.scalar.activation(col_major(VS[:, CTX:T]), tokens(q_of(2, hp)), ACT.Copy)
                for e in range(2):
                    rows = slice(e * HD, (e + 1) * HD)
                    nc.scalar.activation(col_major(QZ[rows, e, 1, :], True), tokens(q_of(0, hp)[rows]), ACT.Copy)
                    if l == 0:
                        nc.scalar.activation(QC[rows, e, :], q_of(0, hp, 0)[rows], ACT.Copy)
                act.drain().then_inc(a_stage.sem, 1)
                us = units(l)

                def probabilities(u):
                    g, e, lat = us[u]
                    act.wait_ge(u_score[l].sem, u_score[l].ready(0, hp, u + 1))
                    if u >= 2:
                        act.wait_ge(u_prob[l].sem, u_prob[l].ready(0, hp, u - 1))
                    nc.scalar.activation(SX[u % 2][:, 256:512], bank[u % 2][:, 256:512], ACT.Copy, scale=HD ** -0.5).then_inc(u_ctx[l].sem, 1)
                    act.wait_ge(u_max[l].sem, u_max[l].ready(0, hp, u + 1))
                    lo = 0 if lat else 256
                    nc.scalar.activation(SX[u % 2][:, lo:512], SX[u % 2][:, lo:512], ACT.Exp, bias=SM[u % 2][:, 0:1], accum_out=SM[u % 2][:, 1:2])\
                      .then_inc(u_exp[l].sem, 1)

                probabilities(0)
                for u, (g, e, lat) in enumerate(us):
                    if u + 1 < len(us):
                        probabilities(u + 1)
                    act.wait_ge(u_tr[l].sem, u_tr[l].ready(0, hp, u + 1))
                    if u >= 2:
                        act.wait_ge(u_out[l].sem, u_out[l].ready(0, hp, u - 1))
                    lo = 0 if lat else 256
                    nc.scalar.activation(PT[u % 2][:, lo:512], bank[2 + u % 2][:, lo:512], ACT.Copy).then_inc(u_trc[l].sem, 1)
                act.drain()

        def attn_dve(dve, l):
            for z in (QZ.rearrange("p e o q -> p (e o q)"), QC.rearrange("p e q -> p (e q)")):
                nc.vector.memset(z, 0.0)
            dve.drain().then_inc(a_clear, 1)
            dve.wait_ge(at_tables, 16 * (l + 1))
            dve.sem_inc(a_biased.sem, 1)
            if l == 0:
                dve.sem_inc(late_copy.sem, 1)
            with dve.Fori(0, HP) as hp:
                for j in range(2):
                    nc.vector.tensor_tensor(RT[0], q_of(j, hp), COS, ALU.mult)
                    dve.wait_ge(a_swap.sem, a_swap.ready(l, hp, j + 1))
                    nc.vector.tensor_tensor(RT[1], bank[j][:, :], SIN, ALU.mult)
                    dve.drain()
                    if j == 0:
                        for e in range(2):
                            rows = slice(e * HD, (e + 1) * HD)
                            nc.vector.tensor_tensor(col_major(QZ[rows, e, 0, :], True), tokens(RT[0][rows]), tokens(RT[1][rows]), ALU.add)
                    else:
                        nc.vector.tensor_tensor(col_major(KR), tokens(RT[0]), tokens(RT[1]), ALU.add)
                    dve.drain().then_inc(a_rot.sem, 1)
                dve.wait_ge(a_swap.sem, a_swap.ready(l, hp, 3))
                for j in range(3):
                    n = min(4, 9 - 4 * j)
                    last = nc.vector.tensor_copy(VA[:, 4 * j:4 * j + n, :].rearrange("p j c -> p (j c)"), bank[2 + j][:, 0:n * P])
                last.then_inc(a_rot.sem, 1)
                dve.wait_ge(a_bias.sem, a_bias.ready(l, hp))
                us = units(l)
                for u, (g, e, lat) in enumerate(us):
                    x = SX[u % 2]
                    lo = 0 if lat else 256
                    dve.wait_ge(u_ctx[l].sem, u_ctx[l].ready(0, hp, u + 1))
                    if lat:
                        nc.vector.scalar_tensor_tensor(out=x[:, 0:256], in0=bank[u % 2][:, 0:256], scalar=HD ** -0.5,
                                                       in1=BN[:, e, VARIANT[3 - g]].rearrange("p c r -> p (c r)"), op0=ALU.mult, op1=ALU.add)
                        dve.drain()
                    nc.vector.reduce_max(SM[u % 2][:, 2:3], x[:, lo:512], AX)
                    dve.drain()
                    nc.vector.tensor_scalar(SM[u % 2][:, 0:1], SM[u % 2][:, 2:3], -1.0, None, ALU.mult).then_inc(u_max[l].sem, 1)
                    if u >= 1:
                        finish(dve, l, hp, us, u - 1)
                    if l == 0 and u in (5, 9):
                        dve.wait_ge(late_prod.sem, late_prod.ready(0, hp, u // 4))
                        add_bias(l, hp * 8 + (2 * KD + 4 * (u // 4 - 1)), 4, bank[7][:, 0:8]).then_inc(late_copy.sem, 1)
                finish(dve, l, hp, us, len(us) - 1)
                dve.drain().then_inc(a_biased.sem, 1)

        def finish(dve, l, hp, us, u):
            g, e, lat = us[u]
            lo = 0 if lat else 256
            dve.wait_ge(u_exp[l].sem, u_exp[l].ready(0, hp, u + 1))
            nc.vector.reciprocal(SM[u % 2][:, 3:4], SM[u % 2][:, 1:2])
            dve.drain()
            if u >= 2:
                dve.wait_ge(u_tr[l].sem, u_tr[l].ready(0, hp, u - 1))
            nc.vector.tensor_scalar(PX[u % 2][:, lo:512], SX[u % 2][:, lo:512], SM[u % 2][:, 3:4], None, ALU.mult).then_inc(u_prob[l].sem, 1)
            if u % 2 == 1 and u >= 3:
                copy_out(dve, l, hp, us, u - 2)
            if u == len(us) - 1:
                copy_out(dve, l, hp, us, u)

        def copy_out(dve, l, hp, us, u):
            g, e, lat = us[u]
            dve.wait_ge(u_out[l].sem, u_out[l].ready(0, hp, u + 1))
            ob = bank[4 + (u // 2) % 2][:, 0:P]
            if lat:
                g0 = 3 - g
                dst = BR[:, 2, bass.ds(hp, 1), CTX:T].rearrange("p a (r c) -> p (a r) c", r=GR)[:, :, g0 * QCOLS:(g0 + 1) * QCOLS]
                src = ob[:, ::-1].rearrange("p (c r) -> p r c", r=GR)
            else:
                dst = BR[:, 2, bass.ds(hp, 1), g * P:(g + 1) * P].rearrange("p a t -> p (a t)")
                src = ob
            nc.vector.tensor_copy(dst, src).then_inc(u_oc[l].sem, 1)

        def load_bias(pool, l, hp):
            for e in range(2):
                for x in range(QCOLS):
                    off = a["rpb"][l, bass.ds(hp * (2 * RPB) + (RPB_PAD - 16 + e * RPB + x), 31 * (2 * GR - 1) + 17)]
                    pool.dma_start(BIAS[x * GR:(x + 1) * GR, e], bias_window(off)).then_inc(bias_load, 16)

        def attn_pool(pool, l):
            per = 2 * QCOLS * 16
            with pool.Fori(0, HP) as hp:
                pool.wait_ge(bias_load, hp * per + (l * (HP + 1) + 1) * per)
                pool.wait_ge(a_biased.sem, a_biased.free(l, hp))
                for e in range(2):
                    for v, shift in enumerate((16, 8, 0)):
                        nc.gpsimd.tensor_tensor(BN[:, e, v], BIAS[:, e, :, shift:shift + KCOLS].rearrange("p r x -> p x r"),
                                                NEG[v].rearrange("p (c r) -> p c r", c=KCOLS), ALU.add)
                pool.drain().then_inc(a_bias.sem, 1)
                load_bias(pool, l, next_pair(hp))
            pool.wait_ge(bias_load, (l + 1) * (HP + 1) * per)

        def next_pair(hp):
            return hp + 1

        def bias_window(ap):
            rows = ap[0:31 * (2 * GR - 1) + 17]
            return bass.AP(tensor=rows.tensor, offset=rows.offset, ap=[[31, GR], [31, GR], [1, BX]])

        mg = Carve(WS0)
        MG = mg(KD * T).rearrange("p (k t) -> p k t", k=KD)
        GATE = [mg(3 * T).rearrange("p (n t) -> p n t", n=3) for _ in range(2)]
        MT = mg(T)
        NM = 6
        m_prod = Count(sem("merge_products"), KD // 2, NM)
        m_load = [Count(sem(f"merge_gates_loaded_{b}"), KD // 2, 16) for b in range(2)]
        m_gate = Count(sem("merge_gates"), KD // 2, 2)
        m_used = Count(sem("merge_used"), KD // 2, NM, primed=NM)

        def merge_pe(pe, l):
            with pe.Fori(0, KD // 2) as i:
                for u in range(NM):
                    b, n = divmod(u, 3)
                    wait_slab(pe, l, "merge", n, i, b)
                    if u >= 4:
                        pe.wait_ge(m_used.sem, m_used.ready(l, i, u - 3))
                    else:
                        pe.wait_ge(m_used.sem, m_used.free(l, i, u + 5 if u < 2 else u + 1))
                    products(pair(2 * (u % 4)), slot_blocks(n, KM), lambda k, s: BR[:, n, k, SEGS[s][0]:SEGS[s][1]], segs_of(l),
                             slab_used[n - 1] if n else (slab_used[2] if b else None)).then_inc(m_prod.sem, 1)
                nc.tensor.drain().then_inc(slab_used[2], 1)

        def merge_pool(pool, l):
            lo = 0 if l == 0 else CTX
            with pool.Fori(0, KD // 2) as i:
                for b in range(2):
                    pool.wait_ge(m_used.sem, m_used.free(l, i, 3 * b + 3))
                    pool.dma_start(GATE[b][:, :, lo:T], gates_dram.rearrange("(n k) p t -> p n k t", n=3)[:, :, bass.ds(i * 2 + b, 1), lo:T]
                                   .rearrange("p n a t -> p n (a t)")).then_inc(m_load[b].sem, 16)

        def merge_act(act, l):
            lo = 0 if l == 0 else CTX
            with act.Fori(0, KD // 2) as i:
                for b in range(2):
                    act.wait_ge(m_load[b].sem, m_load[b].ready(l, i, 16))
                    nc.scalar.activation(GATE[b][:, :, lo:T], GATE[b][:, :, lo:T], ACT.Sigmoid).then_inc(m_gate.sem, 1)

        def merge_dve(dve, l):
            dve.sem_inc(m_used.sem, NM)
            with dve.Fori(0, KD // 2) as i:
                for u in range(NM):
                    b, n = divmod(u, 3)
                    if n == 0:
                        dve.wait_ge(m_gate.sem, m_gate.ready(l, i, b + 1))
                    dve.wait_ge(m_prod.sem, m_prod.ready(l, i, u + 1))
                    dst = [MG[:, bass.ds(i * 2 + b, 1), c0:c1].rearrange("p a t -> p (a t)") for c0, c1 in SEGS]
                    for s in segs_of(l):
                        c0, c1 = SEGS[s]
                        last = nc.vector.tensor_tensor(dst[s] if n == 0 else MT[:, c0:c1], pair(2 * (u % 4))[s], GATE[b][:, n, c0:c1], ALU.mult)
                    last.then_inc(m_used.sem, 1)
                    if n:
                        dve.drain()
                        for s in segs_of(l):
                            c0, c1 = SEGS[s]
                            nc.vector.tensor_tensor(dst[s], dst[s], MT[:, c0:c1], ALU.add)
                        dve.drain()

        Y = arena[:, 0:KD * T].rearrange("p (k t) -> p k t", k=KD)
        o_prod = Count(sem("out_products"), 2, 4)
        o_copy = Count(sem("out_copied"), 2, 4, primed=4)

        def out_pe(pe, l):
            with pe.Fori(0, 2) as i:
                for t in range(4):
                    wait_slab(pe, l, "out", t, i)
                    pe.wait_ge(o_copy.sem, o_copy.free(l, i, t + 1))
                    products(pair(2 * t), slot_blocks(t), lambda k, s: MG[:, k, SEGS[s][0]:SEGS[s][1]], segs_of(l), slab_used[t - 1] if t else None)\
                        .then_inc(o_prod.sem, 1)
                nc.tensor.drain().then_inc(slab_used[3], 1)

        def out_act(act, l):
            act.sem_inc(o_copy.sem, 4)
            with act.Fori(0, 2) as i:
                for t in range(4):
                    act.wait_ge(o_prod.sem, o_prod.ready(l, i, t + 1))
                    for s in segs_of(l):
                        last = nc.scalar.activation(Y[:, bass.ds(i * 4 + t, 1), SEGS[s][0]:SEGS[s][1]].rearrange("p a t -> p (a t)"), pair(2 * t)[s], ACT.Copy)
                    last.then_inc(o_copy.sem, 1)

        MID = arena[:, KD * T:KD * T + NJ * T].rearrange("p (j t) -> p j t", j=NJ)
        SL = [NSQ[0], NSQ[1]]
        f_prod = Count(sem("ffn_products"), NJ // 2, 2)
        f_silu = Count(sem("ffn_silu"), NJ // 2, 2)
        f_mid = Count(sem("ffn_mid"), NJ // 2, 2, primed=2)
        g_prod = Count(sem("ffn_out_products"), KD // 2, 2)
        g_copy = Count(sem("ffn_out_copied"), KD // 2, 2, primed=2)

        def ffn_pe(pe, l):
            segs = segs_of(l)
            with pe.Fori(0, NJ // 2) as i:
                for t in range(2):
                    pe.wait_ge(f_mid.sem, f_mid.free(l, i, t + 1))
                    wait_slab(pe, l, "ffn_in", 2 * t, i)
                    products(pair(4 * t), slot_blocks(2 * t), hx_rhs, segs, slab_used[1] if t else None)
                    wait_slab(pe, l, "ffn_in", 2 * t + 1, i)
                    products(pair(4 * t + 2), slot_blocks(2 * t + 1), hx_rhs, segs, slab_used[2 * t]).then_inc(f_prod.sem, 1)
                nc.tensor.drain().then_inc(slab_used[3], 1)
            pe.wait_ge(f_mid.sem, f_mid.ready(l, NJ // 2 - 1, 2))
            pe.sem_inc(ffn_turn, 1)
            with pe.Fori(0, KD // 2) as i:
                for b in range(2):
                    pe.wait_ge(g_copy.sem, g_copy.free(l, i, b + 1))
                    for s, (k0, k1) in enumerate(FFN_K):
                        wait_slab(pe, l, "ffn_out", s, i * 2 + b)
                        for k in range(k0, k1):
                            for seg in segs:
                                last = nc.tensor.matmul(pair(2 * b)[seg], block(s, k - k0), MID[:, k, SEGS[seg][0]:SEGS[seg][1]], start=(k == 0), stop=(k == NJ - 1))
                            if s and k == k0:
                                last.then_inc(slab_used[s - 1], 1)
                    last.then_inc(g_prod.sem, 1)
                    nc.tensor.drain().then_inc(slab_used[2], 1)

        ffn_turn = sem("ffn_second_half")

        def ffn_act(act, l):
            with act.Fori(0, NJ // 2) as i:
                for t in range(2):
                    act.wait_ge(f_prod.sem, f_prod.ready(l, i, t + 1))
                    act.wait_ge(f_mid.sem, f_mid.free(l, i, t + 1))
                    for s in segs_of(l):
                        last = nc.scalar.activation(SL[t][:, SEGS[s][0]:SEGS[s][1]], pair(4 * t)[s], ACT.Silu)
                    last.then_inc(f_silu.sem, 1)
            act.sem_inc(g_copy.sem, 2)
            with act.Fori(0, KD // 2) as i:
                for b in range(2):
                    act.wait_ge(g_prod.sem, g_prod.ready(l, i, b + 1))
                    for s in segs_of(l):
                        last = nc.scalar.activation(Y[:, bass.ds(i * 2 + b, 1), SEGS[s][0]:SEGS[s][1]].rearrange("p a t -> p (a t)"), pair(2 * b)[s], ACT.Copy)
                    last.then_inc(g_copy.sem, 1)

        def ffn_dve(dve, l):
            dve.sem_inc(f_mid.sem, 2)
            with dve.Fori(0, NJ // 2) as i:
                for t in range(2):
                    dve.wait_ge(f_silu.sem, f_silu.ready(l, i, t + 1))
                    for s in segs_of(l):
                        c0, c1 = SEGS[s]
                        last = nc.vector.tensor_tensor(MID[:, bass.ds(i * 2 + t, 1), c0:c1].rearrange("p a t -> p (a t)"), pair(4 * t + 2)[s], SL[t][:, c0:c1], ALU.mult)
                    last.then_inc(f_mid.sem, 1)

        LOADS = 4
        blk = ctx.enter_context(nc.Block())
        res_src = lambda k: RES[:, k, :]
        y_src = lambda k: Y[:, k, :]

        @blk.sync
        def _(sp):
            sync_program(sp)
            sp.wait_ge(phase_end, 4 * TOTAL_BARRIERS)
            sp.dma_start(a["out"].rearrange("p (k t) -> p k t", k=KD), RES[:, :, CTX:T]).then_inc(s_out, 16)
            sp.wait_ge(s_out, 16)

        @blk.tensor
        def _(pe):
            for s in range(4):
                pe.sem_inc(slab_used[s], 1)
            pe.wait_ge(s_load, 16 * LOADS)
            for l in range(DEPTH):
                if l == 0:
                    ada_pe(pe, l)
                phase_barrier(pe, "pe")
                stats_pe(pe, 4 * l, [0, 1]); phase_barrier(pe, "pe")
                rwkv_pe(pe, l); phase_barrier(pe, "pe")
                phase_barrier(pe, "pe")
                attn_pe(pe, l); phase_barrier(pe, "pe")
                merge_pe(pe, l); phase_barrier(pe, "pe")
                out_pe(pe, l)
                pe.wait_ge(o_copy.sem, o_copy.ready(l, 1, 4))
                stats_pe(pe, 4 * l + 1, segs_of(l)); phase_barrier(pe, "pe")
                stats_pe(pe, 4 * l + 2, segs_of(l)); phase_barrier(pe, "pe")
                ffn_pe(pe, l)
                pe.wait_ge(g_copy.sem, g_copy.ready(l, KD // 2 - 1, 2))
                stats_pe(pe, 4 * l + 3, segs_of(l)); phase_barrier(pe, "pe")

        @blk.scalar
        def _(act):
            act.wait_ge(s_load, 16 * LOADS)
            nc.scalar.activation(cin[:, :], cin[:, :], ACT.Silu).then_inc(silu_done, 1)
            for l in range(DEPTH):
                phase_barrier(act, "act")
                stats_act(act, 4 * l, res_src, [0, 1])
                norm_act(act, 2 * l, 0, [0, 1]); phase_barrier(act, "act")
                rwkv_act(act, l); phase_barrier(act, "act")
                phase_barrier(act, "act")
                attn_act(act, l); phase_barrier(act, "act")
                merge_act(act, l); phase_barrier(act, "act")
                out_act(act, l)
                act.drain()
                stats_act(act, 4 * l + 1, y_src, segs_of(l)); phase_barrier(act, "act")
                stats_act(act, 4 * l + 2, res_src, segs_of(l))
                norm_act(act, 2 * l + 1, 1, segs_of(l)); phase_barrier(act, "act")
                ffn_act(act, l)
                act.drain()
                stats_act(act, 4 * l + 3, y_src, segs_of(l)); phase_barrier(act, "act")

        @blk.vector
        def _(dve):
            nc.vector.memset(one[:, 0:1], EPS)
            nc.vector.memset(one[:, 1:4], LN_EPS)
            dve.wait_ge(s_load, 16 * LOADS)
            for l in range(DEPTH):
                ada_dve(dve, l); phase_barrier(dve, "dve")
                norm_dve(dve, 2 * l, 0, [0, 1]); phase_barrier(dve, "dve")
                rwkv_dve(dve, l); phase_barrier(dve, "dve")
                conv_dve(dve, l); phase_barrier(dve, "dve")
                attn_dve(dve, l)
                if l == 0:
                    dve.drain()
                    scales(dve, l, range(1, 4))
                phase_barrier(dve, "dve")
                merge_dve(dve, l); phase_barrier(dve, "dve")
                add_dve(dve, 2 * l, 0, segs_of(l), Y); phase_barrier(dve, "dve")
                norm_dve(dve, 2 * l + 1, 1, segs_of(l)); phase_barrier(dve, "dve")
                ffn_dve(dve, l)
                add_dve(dve, 2 * l + 1, 1, segs_of(l), Y); phase_barrier(dve, "dve")

        @blk.gpsimd
        def _(pool):
            for dst, name in ((glob, "glob"), (cin, "cin"), (resid, "x"), (bada, "b_ada")):
                pool.dma_start(dst[:, :], a[name]).then_inc(s_load, 16)
            for l in range(DEPTH):
                pool.dma_start(vec[:, :], a["vec"][l, :, :]).then_inc(s_wload, 16)
                for k in range(2):
                    phase_barrier(pool, "pool")
                pool.dma_start(RC, a["rwkv_tables"]).then_inc(rw_tables, 16)
                spill_pool(pool, l)
                phase_barrier(pool, "pool")
                pool.dma_start(CT, side_dram[0:3 * HP].rearrange("j p t -> p j t")).then_inc(side_loaded, 16)
                pool.dma_start(QKV, side_dram[3 * HP:6 * HP].rearrange("j p t -> p j t")).then_inc(side_loaded, 16)
                pool.dma_start(AC, a["attn_tables"]).then_inc(at_tables, 16)
                phase_barrier(pool, "pool")
                load_bias(pool, l, 0)
                pool.wait_ge(at_tables, 16 * (l + 1))
                attn_pool(pool, l)
                phase_barrier(pool, "pool")
                merge_pool(pool, l)
                for k in range(4):
                    phase_barrier(pool, "pool")


def arrays():
    return {
        "glob": (P, 4 * P), "rwkv_tables": (P, 512 + 12 * P + 2 * T), "attn_tables": (P, 2 * SEQ + 768),
        "x": (P, KD * T), "cin": (P, KD * 2), "b_ada": (P, DEPTH * NADA), "vec": (DEPTH, P, NV), "rpb": (DEPTH, 2 * RPB_PAD + 10 * RPB),
        "w_ada": (DEPTH, NADA, P, 8 * P), "w_lora": (DEPTH, 2, P, 8 * P), "w_heads": (DEPTH, 4 * HP, P, 8 * P),
        "w_gate": (DEPTH, 3 * KD, P, 8 * P), "w_side": (DEPTH, 6 * HP, P, 8 * P), "w_up": (DEPTH, 3 * KD, P, KM * P),
        "w_out": (DEPTH, KD, P, 8 * P), "w_ffn_in": (DEPTH, 2 * NJ, P, 8 * P), "w_ffn_out": (DEPTH, KD, P, NJ * P),
    }


def layout(x, c, ctx, c_ctx, w_ada, b_ada, norm_g, w_in, conv_w, rwkv_mu, rwkv_w0, rwkv_w2, rwkv_a0, rwkv_a2,
           rwkv_kk, rwkv_ka, rwkv_rk, rwkv_g2, lnx_g, lnx_b, na_rpb, w_up, w_o, w_ffn_in, w_ffn_out):
    out = dict(zip(("glob", "rwkv_tables", "attn_tables"), constants()))

    def chan(v):
        v = np.asarray(v)
        return np.moveaxis(v.reshape(v.shape[:-1] + (-1, P)), -1, 0).reshape(P, -1)

    tok = np.concatenate([ctx[0], x[0]], 0)
    out["x"] = np.ascontiguousarray(tok.T.reshape(KD, P, T).transpose(1, 0, 2)).reshape(P, KD * T)
    out["cin"] = np.stack([c_ctx.reshape(KD, P).T, c[0].reshape(KD, P).T], 2).reshape(P, KD * 2)
    zero = np.zeros((P, P), np.float32)
    vecs, rpbs = [], []
    streams = {k: [] for k in arrays() if k.startswith("w_")}
    for l in range(DEPTH):
        mu = rwkv_mu[l]
        vecs.append(np.concatenate([
            chan(norm_g[l]), chan(conv_w[l]), chan(mu[:, 0:3 * MIX].reshape(2, 3, MIX)), chan(mu[:, 3 * MIX:]),
            chan(rwkv_w0[l]), chan(rwkv_a0[l]), chan(rwkv_kk[l]), chan(rwkv_ka[l]), chan(rwkv_rk[l].reshape(MIX)),
            chan(lnx_g[l]), chan(lnx_b[l])], 1))
        rpbs.append(np.pad(na_rpb[l].reshape(-1), (RPB_PAD, RPB_PAD + 2 * RPB)))

        def blocks(w):
            k, n = w.shape
            return w.reshape(k // P, P, n // P, P).transpose(2, 0, 1, 3)

        def slabs(name, bl):
            n, cols = arrays()[name][1], arrays()[name][3] // P
            bl = np.asarray(bl).reshape(n, cols, P, P)
            streams[name].append(bl.transpose(0, 2, 1, 3).reshape(n, P, cols * P))

        ada, win = blocks(w_ada[l]), blocks(w_in[l])
        cv, rk, lo, lg, qt, gt = win[0:12], win[12:24], win[24:25], win[25:26], win[26:38], win[38:62]
        slabs("w_ada", ada)
        slabs("w_lora", [lo[0], lg[0]])
        w2a2 = np.concatenate([rwkv_w2[l], rwkv_a2[l]], 1)
        heads = []
        for i in range(HP):
            cs = slice(i * P, (i + 1) * P)
            heads += [b for t in range(3) for b in rk[t * HP + i]]
            heads += [w2a2[0][:, cs], w2a2[1][:, cs], rwkv_g2[l][:, cs]] + [zero] * 5
        slabs("w_heads", heads)
        slabs("w_gate", gt)
        slabs("w_side", [t for part in (cv, qt) for t in part])
        up = [blocks(w_up[l, n]) for n in range(3)]
        slabs("w_up", [up[n][i] for i in range(KD) for n in range(3)])
        slabs("w_out", blocks(w_o[l]))
        fi = blocks(w_ffn_in[l])
        slabs("w_ffn_in", [fi[t] for j in range(NJ) for t in (j, NJ + j)])
        slabs("w_ffn_out", blocks(w_ffn_out[l]))
    out["b_ada"] = chan(b_ada)
    out["vec"] = np.stack(vecs)
    out["rpb"] = np.stack(rpbs)
    for k, v in streams.items():
        out[k] = np.stack(v)
    for k, shape in arrays().items():
        assert out[k].shape == shape, (k, out[k].shape, shape)
        out[k] = np.ascontiguousarray(out[k])
    return out


def build(nc):
    F = mybir.dt.float32
    a = {}
    for name, shape in arrays().items():
        a[name] = nc.dram_tensor("in_" + name, list(shape), F, kind="ExternalInput").ap()
    a["side_dram"] = nc.dram_tensor("side_projections", [6 * HP, P, T], F, kind="Internal").ap()
    a["gates_dram"] = nc.dram_tensor("gate_projections", [3 * KD, P, T], F, kind="Internal").ap()
    a["out"] = nc.dram_tensor("out", [P, KD * SEQ], F, kind="ExternalOutput").ap()
    return a


def kernel(**inputs):
    import concourse.bacc as bacc
    from concourse.bass_utils import run_bass_kernel_spmd

    nc = bacc.Bacc("TRN2", target_bir_lowering=False, num_devices=1)
    a = build(nc)
    program(nc, a)
    got = run_bass_kernel_spmd(nc, [{"in_" + k: v for k, v in layout(**{k: np.asarray(v) for k, v in inputs.items()}).items()}], core_ids=[0])
    y = got.results[0]["out"].reshape(P, KD, SEQ)
    return np.ascontiguousarray(y.transpose(2, 1, 0).reshape(1, SEQ, D))
```

```python
import math
from contextlib import ExitStack

import numpy as np
import concourse.bass as bass
from concourse import mybir

D, SEQ, CTX, DEPTH, MIX, HD, FF = 1024, 512, 256, 2, 512, 64, 2816
P = 128
T = CTX + SEQ
GW, GR = 64, SEQ // 64
NROW, NCOL = 8, 16
KD, KM, NJ = D // P, MIX // P, FF // P
HP = MIX // P
CHUNK = 64
NBLK = T // P
SEGS = [(0, CTX), (CTX, T)]
DSEG = [[(0, CTX), (CTX, T)], [(SEQ, T), (0, SEQ)]]
QCOLS = 16
KCOLS = 32
KEY0 = [0, 8, 24, 32]
VCOL0 = [0, 16, 8, 24, 40, 32, 48]
VARIANT = [0, 1, 1, 2]
RPB = (2 * NROW - 1) * (2 * NCOL - 1)
RPB_PAD = 16
BX = 48
DECAY = math.exp(-0.5)
EPS, LN_EPS = 1e-6, 64e-5
V_NG, V_CW, V_MU, V_MUL, V_W0, V_A0 = 0, 32, 44, 68, 70, 78
V_KK, V_KA, V_RK, V_LG, V_LB = 86, 90, 94, 98, 102
NV = V_LB + HP
NADA = 6 * KD


def constants():
    i = np.arange(P)
    same = (i[:, None] // HD == i[None, :] // HD)
    eye = np.eye(P, dtype=np.float32)
    perm = np.zeros((P, P), np.float32)
    perm[i, (i // 32) * 32 + (i + 16) % 32] = 1.0
    glob = np.concatenate([eye, np.full((P, P), 1.0 / D), same, perm], 1).astype(np.float32)
    s, t = i[:, None], i[None, :]
    chunk = s // CHUNK == t // CHUNK
    gram = [np.concatenate([chunk & (s < t), chunk & (s <= t)], 1), np.concatenate([chunk & (s > t), chunk & (s >= t)], 1)]
    merge = []
    for m in (1, 2, 4, 8, 16, 32):
        low = (s // (2 * m) == t // (2 * m)) & (s // m > t // m)
        merge.append(low)
    lows = np.concatenate(merge, 1)
    ups = np.concatenate([x.T for x in merge], 1)
    tok = np.arange(T)
    resets = [np.broadcast_to(tok % CHUNK != 0, (P, T)), np.broadcast_to(tok % CHUNK != CHUNK - 1, (P, T))]
    rwkv = np.concatenate(gram + [lows, ups] + resets, 1).astype(np.float32)
    tt = np.arange(SEQ)
    freq = 10000.0 ** (-np.arange(16, dtype=np.float32) / 16)
    pos = np.where((i % HD < 32)[:, None], (tt // GW)[None, :], (tt % GW)[None, :]).astype(np.float32)
    ang = pos * freq[i % 16][:, None].astype(np.float32)
    sign = np.where(i % 32 < 16, -1.0, 1.0)[:, None]
    neg = []
    for g in (0, 1, 3):
        qc = QCOLS * g + 15 - i // GR
        kc = KEY0[g] + np.arange(KCOLS * GR) // GR
        start = np.clip(qc - NCOL // 2, 0, GW - NCOL)
        win = (kc[None, :] >= start[:, None]) & (kc[None, :] < start[:, None] + NCOL)
        neg.append(np.where(win, 0.0, -1e30))
    attn = np.concatenate([np.cos(ang), np.sin(ang) * sign] + neg, 1).astype(np.float32)
    return glob, rwkv, attn


class Count:

    def __init__(self, sem, passes=1, per=1, primed=0):
        self.sem, self.passes, self.per, self.primed = sem, passes, per, primed
        self.total = primed + passes * per

    def ready(self, use, i, k=1):
        return i * self.per + (use * self.total + self.primed + k)

    def free(self, use, i, k=1):
        return i * self.per + (use * self.total + k)


def program(nc, a, debug=None):
    F = mybir.dt.float32
    R = mybir.dt.float32r
    ALU = mybir.AluOpType
    ACT = mybir.ActivationFunctionType
    AX = mybir.AxisListType.X
    ctx = ExitStack()
    with ctx:
        def sb(name, n):
            return ctx.enter_context(nc.sbuf_tensor(name, [P, n], F))

        def sem(name):
            return ctx.enter_context(nc.semaphore(name))

        side_dram, gates_dram = a["side_dram"], a["gates_dram"]

        glob = sb("glob", 4 * P)
        IDENT, MEAN_D, SAME, PERM = [glob[:, j * P:(j + 1) * P] for j in range(4)]
        vec = sb("vec", NV)
        cin = sb("cin", KD * 2)
        bada = sb("bada", DEPTH * NADA)
        padded = sb("mod1", NADA * 2 + 4)
        mods = [sb("mod0", NADA * 2), padded[:, 4:]]
        ders = [sb(f"der{l}", 4 * KD * 2) for l in range(DEPTH)]
        one = sb("one", 4)

        def both(name, n):
            with nc.sbuf_tensor(name, [P, n], F) as whole:
                pass
            return whole, ctx.enter_context(nc.sbuf_tensor(name + "_rounded", [P, n], R))

        resid, resid_r = both("resid", KD * T)
        hx, hx_r = both("hx", KD * T)
        slots, slots_r = zip(*[both(f"slot{s}", 8 * P) for s in range(4)])
        NA_ = 9216 + 25984
        with nc.sbuf_tensor("arena", [P, NA_], F) as arena:
            pass
        with nc.sbuf_tensor("branches_low", [P, 3 * HP * T], R) as br_lo, nc.sbuf_tensor("branches_high", [P, 3 * HP * T], R) as br_hi:
            pass
        win_hi = ctx.enter_context(nc.sbuf_tensor("branch_weights_high", [P, 3 * 8 * P], R))
        sb("arena_low", NJ * T - 3 * 8 * P)
        hx_hi, hx_lo, w_parts = [ctx.enter_context(nc.sbuf_tensor(name, [P, n], R))
                                 for name, n in (("hx_high", KD * T), ("hx_low", KD * T), ("weight_parts", 4 * 8 * P))]
        sb("arena_high", NA_ - NJ * T - 2 * KD * T - 4 * 8 * P)
        bank = [ctx.enter_context(nc.psum_tensor(f"bank{i}", [P, 512], F)) for i in range(8)]

        RES = resid[:, :].rearrange("p (k t) -> p k t", k=KD)
        HX = hx[:, :].rearrange("p (k t) -> p k t", k=KD)
        CIN = cin[:, :].rearrange("p (k s) -> p k s", s=2)
        MOD = [x[:, :].rearrange("p (j s) -> p j s", s=2) for x in mods]
        DER = [x[:, :].rearrange("p (n k s) -> p n k s", n=4, s=2) for x in ders]

        class Carve:

            def __init__(self, at):
                self.at = at

            def __call__(self, n):
                self.at += n
                assert self.at <= NA_, self.at
                return arena[:, self.at - n:self.at]

        BR = arena[:, 0:3 * HP * T].rearrange("p (n k t) -> p n k t", n=3, k=HP)
        WS0 = 3 * HP * T

        norm_ws = Carve(NA_ - 5 * T)
        NSQ = [norm_ws(T), norm_ws(T)]
        NRS = norm_ws(T)
        NTMP = [norm_ws(T), norm_ws(T)]

        s_load = sem("loaded_constants")
        s_wload = sem("loaded_layer_tables")
        s_out = sem("output_stored")
        phase_end = sem("engines_at_phase_end")
        slab_full = [sem(f"slab_full_{s}") for s in range(4)]
        slab_used = [sem(f"slab_used_{s}") for s in range(4)]
        silu_done = sem("silu_done")
        ada_prod = Count(sem("ada_products"), 4)
        ada_copy = Count(sem("ada_copied"), 4, primed=1)
        late_prod = Count(sem("late_ada_products"), HP, 4)
        late_copy = Count(sem("late_ada_copied"), HP, 4, primed=1)
        sq_made = Count(sem("squares_made"), 8)
        sq_used = Count(sem("squares_used"), 8)
        rs_made = sem("rms_made")
        added = Count(sem("residual_tiles_added"), KD)
        resid_kept = sem("residual_in_dram")
        resid_back = sem("residual_loaded_again")
        ap_scaled = Count(sem("norm_scaled"), 4, 2)
        ap_shift = Count(sem("norm_shifted"), 4, 2, primed=2)

        segs_of = lambda l, all_tokens=False: [0, 1] if (l == 0 or all_tokens) else [1]
        nbar = {}
        PHASES = 8
        TOTAL_BARRIERS = PHASES * DEPTH

        def phase_barrier(e, name):
            nbar[name] = nbar.get(name, 0) + 1
            e.drain().then_inc(phase_end, 1)
            e.wait_ge(phase_end, 4 * nbar[name])

        STREAM = []
        for l in range(DEPTH):
            if l == 0:
                STREAM.append(((l, "ada"), 4, (1, 1, 1, 1)))
            STREAM.append(((l, "lora"), 1, (1, 1, 0, 0)))
            STREAM.append(((l, "rwkv"), HP, (3, 3 + NBLK, 3 + NBLK, 1 + NBLK) if l == 0 else (3, 3, 3, 1 + NBLK)))
            if l == 0:
                STREAM.append(((l, "late_ada"), HP, (2, 2, 2, 2)))
            STREAM.append(((l, "merge"), KD // 2, (2, 2, 2, 0)))
            STREAM.append(((l, "out"), 2, (1, 1, 1, 1)))
            STREAM.append(((l, "ffn_in"), NJ // 2, (1, 1, 1, 1)))
            STREAM.append(((l, "ffn_out"), 2, (1, 5, 5, 0)))
        before, sofar = {}, [0] * 4
        for key, passes, uses in STREAM:
            before[key] = (list(sofar), uses)
            sofar = [n + passes * u for n, u in zip(sofar, uses)]

        def nth(l, phase, s, i, k):
            base, uses = before[l, phase]
            return i * uses[s] + (base[s] + k)

        def wait_slab(pe, l, phase, s, i, k=0):
            pe.wait_ge(slab_full[s], nth(l, phase, s, i, k) * 16 + 16)

        def block(s, j):
            return slots[s][:, j * P:(j + 1) * P]

        def products(outs, blocks, rhs, segs, done_before=None):
            for s in segs:
                for k, w in enumerate(blocks):
                    last = nc.tensor.matmul(outs[s], w, rhs(k, s), start=(k == 0), stop=(k == len(blocks) - 1))
                    if done_before is not None:
                        last.then_inc(done_before, 1)
                        done_before = None
            return last

        def slot_blocks(s, n=KD):
            return [block(s, k) for k in range(n)]

        def split_products(out, w_hi, w_lo, x_hi, x_lo, start, stop):
            first = nc.tensor.matmul(out, w_hi, x_hi, start=start, stop=False)
            nc.tensor.matmul(out, w_hi, x_lo, start=False, stop=False)
            return first, nc.tensor.matmul(out, w_lo, x_hi, start=False, stop=stop)

        MIX_HI, MIX_LO = [x[:, :].rearrange("p (k t) -> p k t", k=KD) for x in (hx_r, resid_r)]
        WIN_HI = [win_hi[:, s * 8 * P:(s + 1) * 8 * P] for s in range(3)]
        side_turn = sem("side_slabs_turn")
        slab_split = [sem(f"slab_split_{s}") for s in range(3)]

        def splits(l, s, hp=None, k=0):
            each, lora = 3, 1 if s < 2 else 0
            return l * (lora + HP * each) + k + (0 if hp is None else hp * each + lora)

        def wait_split(pe, l, s, hp=None, k=0):
            pe.wait_ge(slab_split[s], splits(l, s, hp, k) + 1)

        def hx_product(out, high, low, k, s):
            c0, c1 = SEGS[s]
            w = slice(k * P, (k + 1) * P)
            return split_products(out, high[:, w], low[:, w], MIX_HI[:, k, c0:c1], MIX_LO[:, k, c0:c1], k == 0, k == KD - 1)

        def hx_products(outs, slot, segs, done_before=None):
            for s in segs:
                for k in range(KD):
                    first, last = hx_product(outs[s], WIN_HI[slot], slots_r[slot], k, s)
                    if done_before is not None:
                        first.then_inc(done_before, 1)
                        done_before = None
            return last

        def split_pool(pool, l):
            def rounded(high, whole):
                nc.gpsimd.tensor_tensor(high, whole, one[:, 2:3].to_broadcast(list(whole.shape)), ALU.mult)

            def split(phase, s, i, k):
                wait_slab(pool, l, phase, s, i, k)
                rounded(WIN_HI[s], slots[s][:, :])
                pool.drain()
                nc.gpsimd.tensor_tensor(slots_r[s][:, :], slots[s][:, :], WIN_HI[s], ALU.subtract).then_inc(slab_split[s], 1)

            for s in range(2):
                split("lora", s, 0, 0)
            with pool.Fori(0, HP) as hp:
                for s in range(3):
                    if s == 1:
                        pool.wait_ge(side_prod.sem, side_prod.free(l, hp * NBLK, 2))
                    split("rwkv", s, hp, 0)
                for g in range(6):
                    split("rwkv", g % 3, hp, 1 + g // 3)
                pool.wait_ge(gate_prod.sem, gate_prod.ready(l, hp, 6))
                pool.sem_inc(side_turn, 1)
                with pool.Fori(0, NBLK) as n:
                    for q in range(2):
                        half = slice(q * 4 * P, (q + 1) * 4 * P)
                        if q == 0:
                            wait_slab(pool, l, "rwkv", 3, hp, n + 1)
                        pool.wait_ge(side_prod.sem, side_prod.free(l, hp * NBLK + n, q + 1))
                        rounded(WIN_HI[1][:, half], slots[3][:, half])
                        pool.drain()
                        nc.gpsimd.tensor_tensor(WIN_HI[2][:, half], slots[3][:, half], WIN_HI[1][:, half], ALU.subtract).then_inc(side_split.sem, 1)
                    pool.drain().then_inc(slab_used[3], 1)

        def pair(i, width=(CTX, SEQ)):
            return [bank[i][:, 0:width[0]], bank[i + 1][:, 0:width[1]]]

        def sync_program(sp):
            def load(l, phase, s, i, k, src, cols=8 * P):
                sp.wait_ge(slab_used[s], nth(l, phase, s, i, k) + 1)
                sp.dma_start(slots[s][:, 0:cols], src.rearrange("a p n -> p (a n)")).then_inc(slab_full[s], 16)

            def tile(name, l, j):
                return a[name][l, bass.ds(j, 1), :, :]

            for l in range(DEPTH):
                if l == 0:
                    with sp.Fori(0, 4) as i:
                        for s in range(4):
                            load(l, "ada", s, i, 0, tile("w_ada", l, i * 4 + s))
                for s in range(2):
                    load(l, "lora", s, 0, 0, a["w_lora"][l, s:s + 1, :, :])
                with sp.Fori(0, HP) as hp:
                    for s in range(4):
                        load(l, "rwkv", s, hp, 0, tile("w_heads", l, hp * 4 + s))
                    for g in range(6):
                        load(l, "rwkv", g % 3, hp, 1 + g // 3, tile("w_gate", l, hp * 6 + g))
                    with sp.Fori(0, NBLK) as n:
                        load(l, "rwkv", 3, hp, n + 1, tile("w_side", l, hp * NBLK + n))
                        if l == 0:
                            for s in (1, 2):
                                load(l, "rwkv", s, hp, n + 3, tile("w_ada", 1, hp * (2 * NBLK) + n * 2 + (s - 1)))
                sp.wait_ge(phase_end, 4 * (PHASES * l + 3))
                load_bias(sp, l, 0)
                with sp.Fori(0, HP) as hp:
                    for k in range(2):
                        if l == 0:
                            for s in range(4):
                                load(l, "late_ada", s, hp, k, tile("w_ada", l, hp * 8 + (2 * KD + 4 * k + s)))
                        if k == 0:
                            sp.wait_ge(a_bias.sem, a_bias.ready(l, hp))
                            load_bias(sp, l, hp + 1)
                sp.wait_ge(phase_end, 4 * (PHASES * l + 4))
                with sp.Fori(0, KD // 2) as i:
                    for b in range(2):
                        load_gates(sp, l, i, b)
                        for n in range(3):
                            load(l, "merge", n, i, b, tile("w_up", l, i * 6 + (3 * b + n)), KM * P)
                with sp.Fori(0, 2) as i:
                    for s in range(4):
                        load(l, "out", s, i, 0, tile("w_out", l, i * 4 + s))
                with sp.Fori(0, NJ // 2) as i:
                    for s in range(4):
                        load(l, "ffn_in", s, i, 0, tile("w_ffn_in", l, i * 4 + s))
                def out_slab(h, m, s, idx):
                    load(l, "ffn_out", s, h, idx, tile("w_ffn_out", l, m + h * (NJ // 2)))

                for h in range(2):
                    each_out_slab(sp, h, out_slab)

        def each_out_slab(e, h, body, after_first=None):
            body(h, 0, 0, 0)
            if after_first is not None:
                after_first()
            with e.Fori(0, NJ // 4 - 1) as i:
                body(h, i * 2 + 1, 1, i)
                body(h, i * 2 + 2, 2, i)
            for m in (NJ // 2 - 2, NJ // 2 - 1):
                body(h, m, 2 - m % 2, NJ // 4 - 1)

        def ada_tile(s, out):
            for k in range(KD):
                last = nc.tensor.matmul(out, block(s, k), CIN[:, k, :], start=(k == 0), stop=(k == KD - 1))
            return last

        def ada_rows(s, out):
            for k in range(KD):
                last = nc.tensor.matmul(out, CIN[:, k, :], block(s, k), start=(k == 0), stop=(k == KD - 1))
            return last

        def ada_columns(rows, n, out):
            for j in range(n):
                last = nc.tensor.matmul(out[:, 2 * j:2 * j + 2], rows[0:2, j * P:(j + 1) * P], IDENT[0:2, 0:2], start=True, stop=True)
            return last

        def add_bias(l, j, n, ps):
            return nc.vector.tensor_tensor(MOD[l][:, bass.ds(j, n), :], ps.rearrange("p (j s) -> p j s", s=2),
                                           bada[:, bass.ds(j + l * NADA, n)].unsqueeze(2).to_broadcast([P, n, 2]), ALU.add)

        def ada_pe(pe, l):
            pe.wait_ge(silu_done, 1)
            with pe.Fori(0, 4) as i:
                pe.wait_ge(ada_copy.sem, ada_copy.free(l, i))
                for s in range(4):
                    wait_slab(pe, l, "ada", s, i)
                    ada_tile(s, bank[0][:, 2 * s:2 * s + 2]).then_inc(slab_used[s], 1)
                nc.tensor.drain().then_inc(ada_prod.sem, 1)

        def ada_dve(dve, l):
            if l == 0:
                dve.sem_inc(ada_copy.sem, 1)
                with dve.Fori(0, 4) as i:
                    dve.wait_ge(ada_prod.sem, ada_prod.ready(l, i))
                    add_bias(l, i * 4, 4, bank[0][:, 0:8]).then_inc(ada_copy.sem, 1)
                dve.drain()
            dve.wait_ge(s_wload, 16 * (l + 1))
            scales(dve, l, range(1) if l == 0 else range(4))

        def scales(dve, l, which):
            for n in which:
                part, is_scale = [(1, True), (2, False), (4, True), (5, False)][n]
                g = vec[:, V_NG + n * KD:V_NG + (n + 1) * KD].unsqueeze(2).to_broadcast([P, KD, 2])
                nc.vector.scalar_tensor_tensor(out=DER[l][:, n], in0=MOD[l][:, part * KD:(part + 1) * KD, :], scalar=1.0 if is_scale else 0.0,
                                               in1=g, op0=ALU.add, op1=ALU.mult)
            dve.drain()

        def stats_act(act, use, src, segs, after=None):
            lo, hi = SEGS[segs[0]][0], T
            for k in range(KD):
                if after is not None:
                    act.wait_ge(added.sem, added.ready(after, k))
                if k >= 2:
                    act.wait_ge(sq_used.sem, sq_used.ready(use, k - 2))
                nc.scalar.activation(NSQ[k % 2][:, lo:hi], src(k)[:, lo:hi], ACT.Square).then_inc(sq_made.sem, 1)
            act.wait_ge(sq_used.sem, sq_used.ready(use, KD - 1))
            for s in segs:
                nc.scalar.activation(NRS[:, SEGS[s][0]:SEGS[s][1]], pair(0)[s], ACT.Ln, bias=one[:, 0:1])
            act.drain()
            nc.scalar.activation(NRS[:, lo:hi], NRS[:, lo:hi], ACT.Exp, scale=-0.5).then_inc(rs_made, 1)

        def stats_pe(pe, use, segs):
            for k in range(KD):
                pe.wait_ge(sq_made.sem, sq_made.ready(use, k))
                for s in segs:
                    last = nc.tensor.matmul(pair(0)[s], MEAN_D, NSQ[k % 2][:, SEGS[s][0]:SEGS[s][1]], start=(k == 0), stop=(k == KD - 1))
                last.then_inc(sq_used.sem, 1)

        def norm_dve(dve, use, half, segs):
            lo = SEGS[segs[0]][0]
            dve.wait_ge(rs_made, 2 * use + 1)
            with dve.Fori(0, KD // 2) as i:
                for b in range(2):
                    dve.wait_ge(ap_shift.sem, ap_shift.free(use, i, b + 1))
                    nc.vector.tensor_tensor(NTMP[b][:, lo:T], RES[:, bass.ds(i * 2 + b, 1), lo:T].rearrange("p a t -> p (a t)"), NRS[:, lo:T], ALU.mult)\
                      .then_inc(ap_scaled.sem, 1)

        def of_norm(half):
            return (arena[:, 0:KD * T].rearrange("p (k t) -> p k t", k=KD), MIX_HI, MIX_LO) if half == 0 else (HX, HX_HI, HX_LO)

        def norm_act(act, use, half, segs):
            act.sem_inc(ap_shift.sem, 2)
            with act.Fori(0, KD // 2) as i:
                for b in range(2):
                    act.wait_ge(ap_scaled.sem, ap_scaled.ready(use, i, b + 1))
                    for s in segs:
                        gain = ders[use // 2][:, bass.ds((i * 2 + b) * 2 + (half * 2 * KD * 2 + s), 1)]
                        shift = mods[use // 2][:, bass.ds((i * 2 + b) * 2 + (half * 3 * KD * 2 + s), 1)]
                        for dst in of_norm(half)[:2]:
                            last = nc.scalar.activation(dst[:, bass.ds(i * 2 + b, 1), SEGS[s][0]:SEGS[s][1]].rearrange("p a t -> p (a t)"),
                                                        NTMP[b][:, SEGS[s][0]:SEGS[s][1]], ACT.Identity, bias=shift, scale=gain)
                    last.then_inc(ap_shift.sem, 1)

        def norm_pool(pool, use, half, segs):
            lo = SEGS[segs[0]][0]
            with pool.Fori(0, KD // 2) as i:
                for b in range(2):
                    pool.wait_ge(ap_shift.sem, ap_shift.ready(use, i, b + 1))
                    whole, high, rest = [x[:, bass.ds(i * 2 + b, 1), lo:T].rearrange("p a t -> p (a t)") for x in of_norm(half)]
                    nc.gpsimd.tensor_tensor(rest, whole, high, ALU.subtract)

        def add_dve(dve, use, half, segs, Y):
            lo = SEGS[segs[0]][0]
            dve.wait_ge(rs_made, 2 * use + 2)
            if half == 0:
                dve.wait_ge(resid_back, 16 * (use // 2 + 1))
            with dve.Fori(0, KD) as k:
                nc.vector.tensor_tensor(NTMP[0][:, lo:T], Y[:, bass.ds(k, 1), lo:T].rearrange("p a t -> p (a t)"), NRS[:, lo:T], ALU.mult)
                dve.drain()
                for s in segs:
                    x = RES[:, bass.ds(k, 1), SEGS[s][0]:SEGS[s][1]].rearrange("p a t -> p (a t)")
                    nc.vector.scalar_tensor_tensor(out=x, in0=NTMP[0][:, SEGS[s][0]:SEGS[s][1]],
                                                   scalar=ders[use // 2][:, bass.ds(k * 2 + ((half * 2 + 1) * KD * 2 + s), 1)], in1=x, op0=ALU.mult, op1=ALU.add)
                dve.drain().then_inc(added.sem, 1)

        ZSEG = [(1, 1 + CTX), (2 + CTX, 2 + T)]

        def conv_step(dve, l, i, j):
            def tile(k, s):
                return CT[:, k, SEGS[s][0]:SEGS[s][1]]

            dve.drain()
            if j == 0:
                dve.wait_ge(conv_loaded.sem, conv_loaded.ready(l, i, 16))
            for s in segs_of(l):
                (c0, c1), (z0, z1) = SEGS[s], ZSEG[s]
                w = [vec[:, bass.ds(i + (V_CW + k * HP), 1)] for k in range(3)]
                if j == 0:
                    nc.vector.tensor_tensor(ZP[:, z0:z1], tile(1, s), tile(2, s), ALU.mult)
                elif j == 1:
                    nc.vector.tensor_scalar(CA[:, c0:c1], ZP[:, z0:z1], w[1], None, ALU.mult)
                elif j < 4:
                    off, wk = ((-1, w[0]), (1, w[2]))[j - 2]
                    nc.vector.scalar_tensor_tensor(out=CA[:, c0:c1], in0=ZP[:, z0 + off:z1 + off], scalar=wk, in1=CA[:, c0:c1], op0=ALU.mult, op1=ALU.add)
                else:
                    last = nc.vector.tensor_tensor(BR[:, 0, bass.ds(i, 1), c0:c1].rearrange("p a t -> p (a t)"), tile(0, s), CA[:, c0:c1], ALU.mult)
            if j == 4:
                last.then_inc(conv_used.sem, 1)

        rw = Carve(2 * HP * T)
        RC = rw(2 * 256 + 2 * 6 * P + 2 * T)
        GMASK = [RC[:, 0:256], RC[:, 256:512]]
        LOWER = [RC[:, 512 + j * P:512 + (j + 1) * P] for j in range(6)]
        UPPER = [RC[:, 512 + (6 + j) * P:512 + (7 + j) * P] for j in range(6)]
        KEEP = [RC[:, 512 + 12 * P:512 + 12 * P + T], RC[:, 512 + 12 * P + T:512 + 12 * P + 2 * T]]
        RW_N = 512 + 12 * P + 2 * T
        ZL = rw(T + 3)
        LD = rw(2 * T).rearrange("p (d t) -> p d t", d=2)
        SG, GT, BONUS = rw(T), rw(T), rw(T)
        DD = [rw(NBLK * 5 * P).rearrange("p (b o t) -> p b o t", b=NBLK, o=5) for _ in range(2)]
        YD = rw(2 * T).rearrange("p (d t) -> p d t", d=2)
        DC = rw(2 * 2 * NBLK).rearrange("p (d c) -> p d c", d=2)
        ARZ = [rw(512).rearrange("p (h o t) -> p h o t", h=2, o=2) for _ in range(2)]
        BKC = [rw(512).rearrange("p (c o t) -> p c o t", c=2, o=2) for _ in range(2)]
        alias = rw.at
        ZR = [rw(T + 3) for _ in range(3)]
        TMP = [rw(T) for _ in range(8)]
        end_a = rw.at
        rw.at = alias
        STG = [rw(640).rearrange("p (o t) -> p o t", o=5) for _ in range(2)]
        VT = [rw(P) for _ in range(2)]
        NAK = [[rw(512).rearrange("p (h o t) -> p h o t", h=2, o=2) for _ in range(2)] for _ in range(2)]
        XX = [rw(512).rearrange("p (x h t) -> p x h t", x=2, h=2) for _ in range(2)]
        T1 = [rw(256).rearrange("p (h t) -> p h t", h=2) for _ in range(2)]
        WR = [rw(256).rearrange("p (h o j) -> p h o j", h=2, o=2) for _ in range(2)]
        ZQ = [rw(256).rearrange("p (o h j) -> p o h j", o=2, h=2) for _ in range(2)]
        GS = [rw(P) for _ in range(2)]
        MH = [rw(256).rearrange("p (c t) -> p c t", c=2) for _ in range(2)]
        HDD = [rw(256).rearrange("p (c t) -> p c t", c=2) for _ in range(2)]
        ST = [rw(P) for _ in range(2)]
        rw.at = max(end_a, rw.at)
        BROW = rw(256)
        SPILL = rw(T)

        rw_tables = sem("rwkv_tables_loaded")
        lora_prod = sem("lora_products")
        lora_copy = sem("lora_copied")
        lora_mix = sem("lora_mixed")
        lora_act = sem("lora_activated")
        hp_prod = Count(sem("head_products"), HP, 4)
        hp_copy = Count(sem("head_copied"), HP, 2)
        pre_prod = Count(sem("prep_products"), HP, 2 * 3)
        pre_act = Count(sem("prep_activations"), HP, 2 * 4)
        pre_dve = Count(sem("prep_vector"), HP, 2 * 4)
        NPE, NDV, NAC = 16, 15, 4
        blk_pe = [Count(sem(f"block_products_{n}"), HP * NBLK, NPE) for n in ("fwd", "bwd")]
        blk_dve = [Count(sem(f"block_vector_{n}"), HP * NBLK, NDV, primed=1) for n in ("fwd", "bwd")]
        blk_act = [Count(sem(f"block_copies_{n}"), HP * NBLK, NAC, primed=1) for n in ("fwd", "bwd")]
        blk_stage = [Count(sem(f"block_staged_{n}"), HP * NBLK) for n in ("fwd", "bwd")]
        post_dve = Count(sem("readout_vector"), HP, 2)
        post_pe = Count(sem("readout_products"), HP, 2)
        post_act = Count(sem("readout_activations"), HP, 2)

        def lora_pe(pe, l):
            wait_split(pe, l, 0)
            hx_products(pair(0), 0, [0, 1]).then_inc(lora_prod, 1)
            wait_split(pe, l, 1)
            hx_products(pair(2), 1, [0, 1], slab_used[0]).then_inc(lora_prod, 1)
            nc.tensor.drain().then_inc(slab_used[1], 1)

        def lora_act_(act, l):
            act.wait_ge(lora_mix, 3 * l + 1)
            act.wait_ge(lora_prod, 2 * l + 1)
            for s in range(2):
                nc.scalar.activation(ZL[:, ZSEG[s][0]:ZSEG[s][1]], pair(0)[s], ACT.Copy)
            act.drain().then_inc(lora_copy, 1)
            act.wait_ge(lora_prod, 2 * l + 2)
            for s in range(2):
                nc.scalar.activation(SG[:, SEGS[s][0]:SEGS[s][1]], pair(2)[s], ACT.Sigmoid)
            for d in range(2):
                act.wait_ge(lora_mix, 3 * l + 2 + d)
                last = nc.scalar.activation(LD[0:64, d, :], LD[0:64, d, :], ACT.Tanh)
            last.then_inc(lora_act, 1)

        def mix_ops(dve, Z, mu, d, out):
            off = -1 if d == 0 else 1
            for s in range(2):
                (z0, z1), (o0, o1) = ZSEG[s], DSEG[d][s]
                nc.vector.tensor_tensor(out[:, o0:o1], Z[:, z0 + off:z1 + off], Z[:, z0:z1], ALU.subtract)
            dve.drain()
            for s in range(2):
                (z0, z1), (o0, o1) = ZSEG[s], DSEG[d][s]
                last = nc.vector.scalar_tensor_tensor(out=out[:, o0:o1], in0=out[:, o0:o1], scalar=mu, in1=Z[:, z0:z1], op0=ALU.mult, op1=ALU.add)
            return last

        def lora_dve(dve, l):
            for z in [ZL] + ARZ_FLAT:
                nc.vector.memset(z, 0.0)
            dve.drain().then_inc(lora_mix, 1)
            dve.wait_ge(lora_copy, l + 1)
            for d in range(2):
                mix_ops(dve, ZL, vec[:, V_MUL + d:V_MUL + d + 1], d, LD[:, d, :]).then_inc(lora_mix, 1)
            nc.vector.tensor_scalar(OMKA, vec[:, V_KA:V_KA + HP], -1.0, 1.0, ALU.mult, ALU.add)

        ARZ_FLAT = [x.rearrange("p h o t -> p (h o t)") for x in ARZ + BKC]
        omka = sb("omka", HP)
        OMKA = omka[:, :]

        def blocked(x):
            return x.rearrange("p (b t) -> p b t", b=NBLK)

        tile_copied = Count(sem("side_tiles_copied"), HP, 6 + NBLK)
        spilled = Count(sem("side_tiles_in_dram"), HP, 16 * (6 + NBLK), primed=16)

        def heads_pe(pe, l, hp):
            for t in range(3):
                wait_split(pe, l, t, hp)
                hx_products(pair(2 * t), t, [0, 1], slab_used[t - 1] if t else None).then_inc(hp_prod.sem, 1)
            wait_slab(pe, l, "rwkv", 3, hp)
            products(pair(6), [block(3, 2)], lambda k, s: SG[:, SEGS[s][0]:SEGS[s][1]], [0, 1], slab_used[2]).then_inc(hp_prod.sem, 1)
            pe.wait_ge(hp_copy.sem, hp_copy.ready(l, hp, 2))

            def gate_tile(g):
                wait_split(pe, l, g % 3, hp, 1 + g // 3)
                if g >= 2:
                    pe.wait_ge(tile_copied.sem, tile_copied.ready(l, hp, g - 1))
                hx_products(pair(4 + 2 * (g % 2)), g % 3, segs_of(l)).then_inc(gate_prod.sem, 1)

            for d in range(2):
                if d == 1:
                    pe.wait_ge(pre_dve.sem, pre_dve.ready(l, hp, 4))
                for rows, b in ((slice(0, 64), 0), (slice(64, 128), 2)):
                    for s in range(2):
                        o0, o1 = DSEG[d][s]
                        last = nc.tensor.matmul(pair(b)[s], block(3, d)[rows], LD[rows, d, o0:o1], start=True, stop=True)
                last.then_inc(pre_prod.sem, 1)
                gate_tile(3 * d)
                pe.wait_ge(pre_act.sem, pre_act.ready(l, hp, 4 * d + 2))
                for s in range(2):
                    o0, o1 = DSEG[d][s]
                    last = nc.tensor.matmul(pair(0)[s], SAME, TMP[6][:, o0:o1], start=True, stop=True)
                last.then_inc(pre_prod.sem, 1)
                nc.tensor.drain().then_inc(slab_used[0], 1)
                gate_tile(3 * d + 1)
                pe.wait_ge(pre_dve.sem, pre_dve.ready(l, hp, 4 * d + 3))
                for s in range(2):
                    o0, o1 = DSEG[d][s]
                    last = nc.tensor.matmul(pair(2)[s], SAME, TMP[6][:, o0:o1], start=True, stop=True)
                last.then_inc(pre_prod.sem, 1)
                nc.tensor.drain().then_inc(slab_used[1], 1)
                gate_tile(3 * d + 2)
                nc.tensor.drain().then_inc(slab_used[2], 1)
            nc.tensor.drain().then_inc(slab_used[3], 1)

        gate_prod = Count(sem("gate_tile_products"), HP, 6)

        def spill(act, l, hp, k, ps, segs, dst):
            act.wait_ge(spilled.sem, spilled.free(l, hp, 0) + k * 16 + 16)
            for s in segs:
                last = nc.scalar.activation(SPILL[:, SEGS[s][0]:SEGS[s][1]], ps[s], ACT.Copy)
            last.then_inc(tile_copied.sem, 1)
            act.wait_ge(tile_copied.sem, tile_copied.ready(l, hp, 1) + k)
            lo = SEGS[segs[0]][0]
            act.dma_start(dst[:, :, lo:T].rearrange("a p t -> p (a t)"), SPILL[:, lo:T]).then_inc(spilled.sem, 16)

        def heads_act(act, l, hp):
            act.wait_ge(zr_clear.sem, zr_clear.ready(l, hp))
            for t in range(3):
                act.wait_ge(hp_prod.sem, hp_prod.ready(l, hp, t + 1))
                for s in range(2):
                    nc.scalar.activation(ZR[t][:, ZSEG[s][0]:ZSEG[s][1]], pair(2 * t)[s], ACT.Copy)
            act.drain().then_inc(hp_copy.sem, 1)
            act.wait_ge(hp_prod.sem, hp_prod.ready(l, hp, 4))
            for s in range(2):
                nc.scalar.activation(GT[:, SEGS[s][0]:SEGS[s][1]], pair(6)[s], ACT.Copy)
            act.drain().then_inc(hp_copy.sem, 1)
            def gate_copy(g):
                act.wait_ge(gate_prod.sem, gate_prod.ready(l, hp, g + 1))
                spill(act, l, hp, g, pair(4 + 2 * (g % 2)), segs_of(l), gates_dram[bass.ds(hp * 6 + g, 1)])

            for d in range(2):
                act.wait_ge(pre_prod.sem, pre_prod.ready(l, hp, 3 * d + 1))
                if d == 1:
                    act.wait_ge(pre_dve.sem, pre_dve.ready(l, hp, 4))
                for s in range(2):
                    o0, o1 = DSEG[d][s]
                    nc.scalar.activation(TMP[3][:, o0:o1], pair(0)[s], ACT.Sigmoid, bias=vec[:, bass.ds(hp + (V_W0 + d * HP), 1)])
                    nc.scalar.activation(TMP[5][:, o0:o1], pair(2)[s], ACT.Sigmoid, bias=vec[:, bass.ds(hp + (V_A0 + d * HP), 1)])
                act.drain().then_inc(pre_act.sem, 1)
                act.wait_ge(pre_dve.sem, pre_dve.ready(l, hp, 4 * d + 1))
                nc.scalar.activation(TMP[6], TMP[7], ACT.Square).then_inc(pre_act.sem, 1)
                gate_copy(3 * d)
                act.wait_ge(pre_dve.sem, pre_dve.ready(l, hp, 4 * d + 2))
                nc.scalar.activation(TMP[6], TMP[6], ACT.Ln)
                act.drain()
                nc.scalar.activation(TMP[6], TMP[6], ACT.Exp, scale=-0.5)
                nc.scalar.activation(E3, E3, ACT.Exp, scale=-DECAY)
                nc.scalar.activation(E2, TMP[4], ACT.Exp, scale=DECAY)
                act.drain()
                nc.scalar.activation(TMP[4], TMP[4], ACT.Exp, scale=-DECAY).then_inc(pre_act.sem, 1)
                act.drain()
                last_tok = TMP[4].rearrange("p (c t) -> p c t", t=CHUNK)[:, :, CHUNK - 1 if d == 0 else 0]
                nc.scalar.activation(DC[:, d, :], last_tok, ACT.Copy).then_inc(pre_act.sem, 1)
                gate_copy(3 * d + 1)
                gate_copy(3 * d + 2)

        E2, E3 = YD[:, 0, :], YD[:, 1, :]
        zr_clear = Count(sem("head_pads_cleared"), HP, 1)

        def heads_dve(dve, l, hp):
            mu = lambda d, o: vec[:, bass.ds(hp + (V_MU + (d * 3 + o) * HP), 1)]
            for z in ZR:
                nc.vector.memset(z, 0.0)
            dve.drain().then_inc(zr_clear.sem, 1)
            dve.wait_ge(hp_copy.sem, hp_copy.ready(l, hp, 1))
            for d in range(2):
                if d == 1:
                    dve.wait_ge(pre_act.sem, pre_act.ready(l, hp, 4))
                for o in range(3):
                    mix_ops(dve, ZR[o], mu(d, o), d, TMP[o])
                dve.drain()
                nc.vector.tensor_scalar(TMP[7], TMP[1], vec[:, bass.ds(hp + V_KK, 1)], None, ALU.mult).then_inc(pre_dve.sem, 1)
                nc.vector.tensor_copy(DD[d][:, :, 4, :], blocked(TMP[2]))
                dve.wait_ge(pre_act.sem, pre_act.ready(l, hp, 4 * d + 1))
                sl = slice(None) if d == 0 else slice(None, None, -1)
                nc.vector.tensor_tensor_scan(TMP[4][:, sl], KEEP[d][:, sl], TMP[3][:, sl], 0.0, ALU.mult, ALU.add)
                dve.drain()
                nc.vector.tensor_tensor(E3, TMP[4], TMP[3], ALU.subtract)
                dve.wait_ge(pre_prod.sem, pre_prod.ready(l, hp, 3 * d + 2))
                for s in range(2):
                    o0, o1 = DSEG[d][s]
                    nc.vector.tensor_scalar(TMP[6][:, o0:o1], pair(0)[s], 1e-24, None, ALU.max)
                dve.drain().then_inc(pre_dve.sem, 1)
                nc.vector.tensor_scalar(TMP[3], TMP[5], vec[:, bass.ds(hp + V_KA, 1)], omka[:, bass.ds(hp, 1)], ALU.mult, ALU.add)
                dve.drain()
                nc.vector.tensor_tensor(TMP[1], TMP[1], TMP[3], ALU.mult)
                dve.wait_ge(pre_act.sem, pre_act.ready(l, hp, 4 * d + 3))
                nc.vector.tensor_tensor(TMP[7], TMP[7], TMP[6], ALU.mult)
                dve.drain()
                nc.vector.scalar_tensor_tensor(out=TMP[6], in0=TMP[0], scalar=vec[:, bass.ds(hp + V_RK, 1)], in1=TMP[1], op0=ALU.mult, op1=ALU.mult)\
                  .then_inc(pre_dve.sem, 1)
                nc.vector.tensor_tensor(DD[d][:, :, 3, :], blocked(TMP[1]), blocked(E2), ALU.mult)
                nc.vector.tensor_tensor(DD[d][:, :, 1, :], blocked(TMP[0]), blocked(TMP[4]), ALU.mult)
                nc.vector.scalar_tensor_tensor(out=DD[d][:, :, 0, :], in0=blocked(TMP[7]), scalar=-1.0, in1=blocked(E3), op0=ALU.mult, op1=ALU.mult)
                nc.vector.tensor_tensor(TMP[5], TMP[7], TMP[5], ALU.mult)
                dve.drain()
                nc.vector.tensor_tensor(DD[d][:, :, 2, :], blocked(TMP[5]), blocked(E2), ALU.mult)
                dve.wait_ge(pre_prod.sem, pre_prod.ready(l, hp, 3 * d + 3))
                for s in range(2):
                    (o0, o1), (c0, c1) = DSEG[d][s], SEGS[s]
                    dst = BONUS[:, c0:c1] if d == 0 else TMP[6][:, c0:c1]
                    nc.vector.tensor_tensor(dst, pair(2)[s], TMP[2][:, o0:o1], ALU.mult)
                dve.drain()
                if d == 1:
                    nc.vector.tensor_tensor(BONUS, BONUS, TMP[6], ALU.add)
                dve.drain().then_inc(pre_dve.sem, 1)
            for d in range(2):
                nc.vector.memset(ST[d], 0.0)

        def at_block(d, n):
            return n if d == 0 else (NBLK - 1) - n

        def block_pe(pe, l, hp, n):
            it = hp * NBLK + n
            b = lambda d, j: bank[3 * d + j]

            def side(j):
                k, s = divmod(j, 2)
                if j % 8 == 0:
                    pe.wait_ge(side_split.sem, side_split.ready(l, it, j // 8 + 1))
                if j == 0:
                    pe.wait_ge(tile_copied.sem, tile_copied.ready(l, hp, 6) + n)
                _, last = hx_product(pair(6)[s], WIN_HI[1], WIN_HI[2], k, s)
                if j % 8 == 7:
                    last.then_inc(side_prod.sem, 1)

            def step(d, last, k):
                last.then_inc(blk_pe[d].sem, 1)

            def on_dve(d, k):
                pe.wait_ge(blk_dve[d].sem, blk_dve[d].ready(l, it, k))

            def on_act(d, k):
                pe.wait_ge(blk_act[d].sem, blk_act[d].ready(l, it, k))

            for d in range(2):
                pe.wait_ge(blk_stage[d].sem, blk_stage[d].ready(l, it))
                if l == 0 and d == 1:
                    on_dve(d, 0)
                for j, o in enumerate((0, 2, 3, 4)):
                    nc.tensor.transpose(b(d, 0)[:, j * P:(j + 1) * P], STG[d][:, o, :], IDENT)
                on_act(d, 0)
                on_dve(d, 0)
                rhs = ARZ[d].rearrange("p h o t -> p (h o t)")
                nc.tensor.matmul(b(d, 1)[:, :], STG[d][:, 2, :], rhs, start=True, stop=True)
                step(d, nc.tensor.matmul(b(d, 2)[:, :], STG[d][:, 3, :], rhs, start=True, stop=True), 1)
            side(0)
            for d in range(2):
                on_dve(d, 1)
                on_act(d, 1)
                for h in range(2):
                    nc.tensor.matmul(b(d, 0)[:, h * P:(h + 1) * P], NAK[d][0][:, h, 0, :], IDENT, start=True, stop=True)
                    last = nc.tensor.matmul(b(d, 2)[:, h * P:(h + 1) * P], NAK[d][1][:, h, 0, :], VT[d], start=True, stop=True)
                step(d, last, 2)
            side(1)
            for m in range(1, 6):
                for d in range(2):
                    on_dve(d, 2 * m)
                    for h in range(2):
                        last = nc.tensor.matmul(b(d, 1)[:, h * P:(h + 1) * P], NAK[d][0][:, h, 0, :], XX[d][:, 0, h, :], start=True, stop=True)
                    step(d, last, 2 * m + 1)
                side(2 * m)
                for d in range(2):
                    on_dve(d, 2 * m + 1)
                    if m == 1:
                        on_act(d, 2)
                    for h in range(2):
                        if m < 5:
                            nc.tensor.matmul(b(d, 2)[:, h * P:(h + 1) * P], XX[d][:, 1, h, :], T1[d][:, h, :], start=True, stop=True)
                        last = nc.tensor.matmul(b(d, 2)[:, (2 + h) * P:(3 + h) * P], T1[d][:, h, :], XX[d][:, 1, h, :], start=True, stop=True)
                    step(d, last, 2 * m + 2)
                side(2 * m + 1)
            for d in range(2):
                on_dve(d, 12)
                for h in range(2):
                    last = nc.tensor.matmul(b(d, 0)[:, h * P:(h + 1) * P], XX[d][:, 1, h, :], WR[d][:, h].rearrange("p o j -> p (o j)"), start=True, stop=True)
                step(d, last, 13)
            side(12)
            for d in range(2):
                on_act(d, 3)
                for h in range(2):
                    rows = slice(h * HD, (h + 1) * HD)
                    nc.tensor.matmul(b(d, 0)[rows, 0:P], ZQ[d][:, 0, h, :], NAK[d][0][:, h, 1, :], start=True, stop=True)
                    nc.tensor.matmul(b(d, 1)[rows, 0:P], ZQ[d][:, 1, h, :], NAK[d][0][:, h, 1, :], start=True, stop=False, skip_group_check=True)
                    nc.tensor.matmul(b(d, 1)[rows, 0:P], VT[d][:, rows], NAK[d][1][:, h, 1, :], start=False, stop=False, skip_group_check=True)
                z = ZQ[d][:, 0].rearrange("p h j -> p (h j)")
                q = ZQ[d][:, 1].rearrange("p h j -> p (h j)")
                for c in range(2):
                    nc.tensor.matmul(b(d, 2)[:, c * P:(c + 1) * P], z, BKC[d][:, c, 0, :], start=True, stop=True)
                for c in range(2):
                    nc.tensor.matmul(b(d, 0)[:, (c + 1) * P:(c + 2) * P], BKC[d][:, c, 0, :], q, start=True, stop=False)
                    last = nc.tensor.matmul(b(d, 0)[:, (c + 1) * P:(c + 2) * P], BKC[d][:, c, 1, :], VT[d], start=False, stop=True)
                step(d, last, 14)
            side(13)
            for j in range(2):
                for d in range(2):
                    if j == 1 and d == 1 and l == 0:
                        on_dve(d, 13)
                        ada_columns(BROW, 2, b(1, 0)[:, 256:260])
                        for s in (1, 2):
                            wait_slab(pe, l, "rwkv", s, hp, n + 3)
                            ada_rows(s, b(1, 0)[0:2, (s - 1) * P:s * P]).then_inc(slab_used[s], 1)
                    c = j if d == 0 else 1 - j
                    cols = slice(c * CHUNK, (c + 1) * CHUNK)
                    on_dve(d, 13 + j)
                    nc.tensor.matmul(b(d, 1)[:, cols], ST[d], GS[d][:, cols], start=False, stop=(j == 1), skip_group_check=True)
                    step(d, nc.tensor.matmul(b(d, 2)[:, j * P:(j + 1) * P], MH[d][:, c, :], ST[d], start=True, stop=True), 15 + j)
                side(14 + j)

        side_prod = Count(sem("side_products"), HP * NBLK, 2, primed=2)
        side_split = Count(sem("side_slab_halves_split"), HP * NBLK, 2)

        def stage_block(act, l, hp, n, d):
            blk = at_block(d, n)
            nc.scalar.activation(STG[d].rearrange("p o t -> p (o t)"), DD[d][:, bass.ds(blk, 1)].rearrange("p a o t -> p (a o t)"), ACT.Copy)
            act.drain()
            for h in range(2):
                rows = slice(h * HD, (h + 1) * HD)
                nc.scalar.activation(ARZ[d][rows, h].rearrange("p o t -> p (o t)"), STG[d][rows, 0:2, :].rearrange("p o t -> p (o t)"), ACT.Copy)
            act.drain().then_inc(blk_stage[d].sem, 1)

        def block_act(act, l, hp, n, more):
            it = hp * NBLK + n
            b = lambda d, j: bank[3 * d + j]
            for d in range(2):
                act.wait_ge(blk_pe[d].sem, blk_pe[d].ready(l, it, 1))
                nc.scalar.activation(WR[d][:, :, 0, :], b(d, 0)[:, 0:P].rearrange("p (h j) -> p h j", h=2), ACT.Copy)
                nc.scalar.activation(VT[d], b(d, 0)[:, 3 * P:4 * P], ACT.Copy)
                for c in range(2):
                    rows = slice(c * CHUNK, (c + 1) * CHUNK)
                    last = nc.scalar.activation(BKC[d][rows, c].rearrange("p o t -> p (o t)"), b(d, 0)[rows, P:3 * P], ACT.Copy)
                last.then_inc(blk_act[d].sem, 1)
            for d in range(2):
                act.wait_ge(blk_pe[d].sem, blk_pe[d].ready(l, it, 2))
                for h in range(2):
                    last = nc.scalar.activation(WR[d][:, h, 1, :], b(d, 2)[:, h * (P + HD):h * (P + HD) + HD], ACT.Copy)
                last.then_inc(blk_act[d].sem, 1)
            for d in range(2):
                act.wait_ge(blk_pe[d].sem, blk_pe[d].ready(l, it, 13))
                nc.scalar.activation(ZQ[d].rearrange("p o h j -> p h o j"), b(d, 0)[:, 0:256].rearrange("p (h o j) -> p h o j", h=2, o=2), ACT.Copy)\
                  .then_inc(blk_act[d].sem, 1)
            if more:
                for d in range(2):
                    act.wait_ge(blk_dve[d].sem, blk_dve[d].ready(l, it, 13))
                    stage_block(act, l, hp, n + 1, d)
            for d in range(2):
                act.wait_ge(blk_pe[d].sem, blk_pe[d].ready(l, it, 16))
                nc.scalar.activation(YD[:, d, bass.ds(at_block(d, n) * P, P)], b(d, 1)[:, 0:P], ACT.Copy).then_inc(blk_act[d].sem, 1)
            act.wait_ge(side_prod.sem, side_prod.ready(l, it, 2))
            spill(act, l, hp, n + 6, pair(6), [0, 1], side_dram[bass.ds(hp * NBLK + n, 1)])

        def add_block_tiles(it, ps):
            return nc.vector.tensor_tensor(padded[:, bass.ds(it * 4, 4)].rearrange("p (j s) -> p j s", s=2), ps.rearrange("p (j s) -> p j s", s=2),
                                           bada[:, bass.ds(it * 2 + (NADA - 2), 2)].unsqueeze(2).to_broadcast([P, 2, 2]), ALU.add)

        last_tiles = sem("last_modulation_tiles")

        def block_dve(dve, l, hp, n):
            it = hp * NBLK + n
            b = lambda d, j: bank[3 * d + j]

            def decay(d, c):
                return DC[:, d, bass.ds(at_block(d, n) * 2 + c, 1)]

            def bc(x, n):
                return x.unsqueeze(1).to_broadcast([P, n] + list(x.shape[1:]))

            def on_pe(d, k):
                dve.wait_ge(blk_pe[d].sem, blk_pe[d].ready(l, it, k))

            for d in range(2):
                on_pe(d, 1)
                for j in range(2):
                    last = nc.vector.tensor_tensor(NAK[d][j].rearrange("p h o t -> p h (o t)"), b(d, 1 + j)[:, :].rearrange("p (h t) -> p h t", h=2), bc(GMASK[d], 2), ALU.mult)
                last.then_inc(blk_dve[d].sem, 1)
            for d in range(2):
                on_pe(d, 2)
                low, up = (LOWER, UPPER) if d == 0 else (UPPER, LOWER)
                nc.vector.tensor_tensor(XX[d][:, 0], b(d, 0)[:, 0:256].rearrange("p (h t) -> p h t", h=2), bc(low[0], 2), ALU.mult)
                nc.vector.tensor_tensor(XX[d][:, 1], NAK[d][0][:, :, 0, :], bc(up[0], 2), ALU.mult)
                dve.drain()
                xx = XX[d].rearrange("p x h t -> p (x h) t")
                nc.vector.tensor_tensor(xx, xx, bc(IDENT, 4), ALU.add).then_inc(blk_dve[d].sem, 1)
            for m in range(1, 6):
                for d in range(2):
                    on_pe(d, 2 * m + 1)
                    low = LOWER if d == 0 else UPPER
                    nc.vector.tensor_tensor(T1[d], b(d, 1)[:, 0:256].rearrange("p (h t) -> p h t", h=2), bc(low[m], 2), ALU.mult).then_inc(blk_dve[d].sem, 1)
                for d in range(2):
                    on_pe(d, 2 * m + 2)
                    if m < 5:
                        x, ps = XX[d].rearrange("p x h t -> p (x h t)"), b(d, 2)[:, :]
                    else:
                        x, ps = XX[d][:, 1].rearrange("p h t -> p (h t)"), b(d, 2)[:, 256:512]
                    nc.vector.tensor_tensor(x, x, ps, ALU.add).then_inc(blk_dve[d].sem, 1)
            for d in range(2):
                on_pe(d, 14)
                nc.vector.tensor_tensor(GS[d], STG[d][:, 1, :], b(d, 0)[:, 0:P], ALU.add)
                nc.vector.tensor_tensor(MH[d], b(d, 2)[:, 0:256].rearrange("p (c t) -> p c t", c=2), bc(SAME, 2), ALU.mult)
                for c in range(2):
                    nc.vector.scalar_tensor_tensor(out=HDD[d][:, c, :], in0=b(d, 0)[:, (c + 1) * P:(c + 2) * P], scalar=decay(d, c), in1=SAME, op0=ALU.mult, op1=ALU.mult)
                dve.drain()
                nc.vector.tensor_tensor(MH[d], MH[d], bc(IDENT, 2), ALU.add).then_inc(blk_dve[d].sem, 1)
            for j in range(2):
                for d in range(2):
                    c = j if d == 0 else 1 - j
                    on_pe(d, 15 + j)
                    if j == 1 and d == 1 and l == 0:
                        add_block_tiles(it, b(1, 0)[:, 256:260])
                        nc.vector.tensor_copy(BROW[0:2, :], b(1, 0)[0:2, 0:256])
                    nc.vector.scalar_tensor_tensor(out=ST[d], in0=b(d, 2)[:, j * P:(j + 1) * P], scalar=decay(d, c), in1=HDD[d][:, c, :], op0=ALU.mult, op1=ALU.add)\
                      .then_inc(blk_dve[d].sem, 1)

        def readout_pe(pe, l, hp):
            for j, src in enumerate((TMP[0], TMP[2])):
                pe.wait_ge(*( (post_dve.sem, post_dve.ready(l, hp, 1)) if j == 0 else (post_act.sem, post_act.ready(l, hp, 1)) ))
                for s in range(2):
                    last = nc.tensor.matmul(pair(2 * j)[s], SAME, src[:, SEGS[s][0]:SEGS[s][1]], start=True, stop=True)
                last.then_inc(post_pe.sem, 1)

        def readout_act(act, l, hp):
            act.wait_ge(post_dve.sem, post_dve.ready(l, hp, 2))
            nc.scalar.activation(TMP[2], TMP[1], ACT.Square).then_inc(post_act.sem, 1)
            act.wait_ge(post_pe.sem, post_pe.ready(l, hp, 2))
            for s in range(2):
                nc.scalar.activation(TMP[3][:, SEGS[s][0]:SEGS[s][1]], pair(2)[s], ACT.Ln, scale=1.0 / HD, bias=one[:, 1:2])
            act.drain()
            nc.scalar.activation(TMP[3], TMP[3], ACT.Exp, scale=-0.5).then_inc(post_act.sem, 1)

        def readout_dve(dve, l, hp, it_last):
            for d in range(2):
                dve.wait_ge(blk_act[d].sem, blk_act[d].ready(l, it_last, NAC))
            for s in range(2):
                (c0, c1), (o0, o1) = SEGS[s], DSEG[1][s]
                nc.vector.tensor_tensor(TMP[0][:, c0:c1], YD[:, 0, c0:c1], YD[:, 1, o0:o1], ALU.add)
            dve.drain().then_inc(post_dve.sem, 1)
            dve.wait_ge(post_pe.sem, post_pe.ready(l, hp, 1))
            for s in range(2):
                c0, c1 = SEGS[s]
                nc.vector.scalar_tensor_tensor(out=TMP[1][:, c0:c1], in0=pair(0)[s], scalar=-1.0 / HD, in1=TMP[0][:, c0:c1], op0=ALU.mult, op1=ALU.add)
            dve.drain().then_inc(post_dve.sem, 1)
            dve.wait_ge(post_act.sem, post_act.ready(l, hp, 2))
            nc.vector.tensor_tensor(TMP[1], TMP[1], TMP[3], ALU.mult)
            dve.drain()
            nc.vector.tensor_scalar(TMP[1], TMP[1], vec[:, bass.ds(hp + V_LG, 1)], vec[:, bass.ds(hp + V_LB, 1)], ALU.mult, ALU.add)
            dve.drain()
            nc.vector.tensor_tensor(TMP[1], TMP[1], BONUS, ALU.add)
            dve.drain()
            nc.vector.tensor_tensor(BR[:, 1, bass.ds(hp, 1), :].rearrange("p a t -> p (a t)"), TMP[1], GT, ALU.mult)
            dve.drain()

        def rwkv_pe(pe, l):
            pe.sem_inc(side_prod.sem, 2)
            lora_pe(pe, l)
            pe.wait_ge(lora_act, l + 1)
            pe.wait_ge(rw_tables, 16 * (l + 1))
            with pe.Fori(0, HP) as hp:
                heads_pe(pe, l, hp)
                phase_barrier_in(pe, l, hp, 0)
                with pe.Fori(0, NBLK) as n:
                    block_pe(pe, l, hp, n)
                phase_barrier_in(pe, l, hp, 1)
                readout_pe(pe, l, hp)
                phase_barrier_in(pe, l, hp, 2)
            if l == 0:
                ada_columns(BROW, 2, bank[3][:, 256:260]).then_inc(last_tiles, 1)

        def rwkv_act(act, l):
            for d in range(2):
                act.sem_inc(blk_act[d].sem, 1)
            act.sem_inc(spilled.sem, 16)
            lora_act_(act, l)
            with act.Fori(0, HP) as hp:
                heads_act(act, l, hp)
                phase_barrier_in(act, l, hp, 0)
                for d in range(2):
                    stage_block(act, l, hp, 0, d)
                with act.Fori(0, NBLK - 1) as n:
                    block_act(act, l, hp, n, True)
                block_act(act, l, hp, NBLK - 1, False)
                phase_barrier_in(act, l, hp, 1)
                readout_act(act, l, hp)
                phase_barrier_in(act, l, hp, 2)

        def rwkv_dve(dve, l):
            if l == 0:
                nc.vector.memset(BROW, 0.0)
            lora_dve(dve, l)
            for d in range(2):
                dve.sem_inc(blk_dve[d].sem, 1)
            dve.wait_ge(rw_tables, 16 * (l + 1))
            with dve.Fori(0, HP) as hp:
                heads_dve(dve, l, hp)
                phase_barrier_in(dve, l, hp, 0)
                with dve.Fori(0, NBLK) as n:
                    block_dve(dve, l, hp, n)
                phase_barrier_in(dve, l, hp, 1)
                readout_dve(dve, l, hp, hp * NBLK + (NBLK - 1))
                phase_barrier_in(dve, l, hp, 2)
            if l == 0:
                dve.wait_ge(last_tiles, 1)
                add_block_tiles(HP * NBLK, bank[3][:, 256:260])

        head_stage = Count(sem("engines_at_head_stage"), HP, 9)

        stages_entered = sem("head_stages_entered")

        def phase_barrier_in(e, l, hp, j):
            e.drain().then_inc(head_stage.sem, 1)
            e.wait_ge(head_stage.sem, head_stage.ready(l, hp, 3 * (j + 1)))
            e.sem_inc(stages_entered, 1)

        at = Carve(WS0)
        AC = at(2 * SEQ + 3 * 256)
        COS, SIN = AC[:, 0:SEQ], AC[:, SEQ:2 * SEQ]
        NEG = [AC[:, 2 * SEQ + j * 256:2 * SEQ + (j + 1) * 256] for j in range(3)]
        QKV = at(12 * T).rearrange("p (j t) -> p j t", j=12)
        QZ = at(2 * 2 * SEQ).rearrange("p (e o q) -> p e o q", e=2, o=2)
        QC = at(2 * CTX).rearrange("p (e q) -> p e q", e=2)
        KR = at(SEQ)
        VS = at(T)
        VA = at(9 * P).rearrange("p (j c) -> p j c", j=9)
        RT = [at(SEQ), at(SEQ)]
        BIAS = at(2 * GR * BX).rearrange("p (e r x) -> p e r x", e=2, r=GR)
        BN = at(2 * 3 * 256).rearrange("p (e v c r) -> p e v c r", e=2, v=3, c=KCOLS)
        SX = [at(512) for _ in range(3)]
        PX = [at(512) for _ in range(2)]
        PT = [at(512) for _ in range(2)]
        SM = [at(4) for _ in range(3)]
        AROW = at(512)
        CT = hx[:, 0:3 * T].rearrange("p (j t) -> p j t", j=3)
        ZP = hx[:, 3 * T:4 * T + 3]
        CA = hx[:, 5 * T:6 * T]
        SIDE = side_dram.rearrange("(j h) p t -> h p j t", h=HP)
        qkv_loaded = Count(sem("qkv_loaded"), HP, 16)
        conv_loaded = Count(sem("conv_inputs_loaded"), HP, 16)
        conv_used = Count(sem("conv_inputs_used"), HP)

        at_tables = sem("attention_tables_loaded")
        bias_load = sem("bias_loaded")
        a_clear = sem("attention_cleared")
        a_bias = Count(sem("bias_masked"), HP, 1)
        a_biased = Count(sem("bias_used"), HP, 1, primed=1)
        a_stage = Count(sem("attention_staged"), HP, 1)
        a_swap = Count(sem("attention_swapped"), HP, 3)
        a_rot = Count(sem("attention_rotated"), HP, 3)

        def units(l):
            u = [(g, e, True) for g in range(4) for e in range(2)]
            if l == 0:
                u += [(g, e, False) for g in range(2) for e in range(2)]
            return u

        NU = [12, 8]
        u_score = [Count(sem(f"scores_{l}"), HP, NU[l]) for l in range(2)]
        u_prob = [Count(sem(f"probabilities_{l}"), HP, NU[l]) for l in range(2)]
        u_tr = [Count(sem(f"transposed_{l}"), HP, NU[l]) for l in range(2)]
        u_trc = [Count(sem(f"transposed_copied_{l}"), HP, NU[l]) for l in range(2)]
        u_out = [Count(sem(f"attended_{l}"), HP, NU[l]) for l in range(2)]
        u_max = [Count(sem(f"maximum_{l}"), HP, NU[l]) for l in range(2)]
        u_exp = [Count(sem(f"exponentials_{l}"), HP, NU[l]) for l in range(2)]
        u_oc = [Count(sem(f"attended_copied_{l}"), HP, NU[l] // 2) for l in range(2)]

        def col_major(x, reverse=False):
            if reverse:
                x = x[:, ::-1]
            return x.rearrange("p (c r) -> p r c", r=GR)

        def tokens(x):
            return x.rearrange("p (r c) -> p r c", r=GR)

        def q_of(j0, hp, s=1):
            return QKV[:, bass.ds(hp + j0 * HP, 1), SEGS[s][0]:SEGS[s][1]].rearrange("p a t -> p (a t)")

        SB = [0, 1, 6]

        def attn_pe(pe, l):
            pe.wait_ge(at_tables, 16 * (l + 1))
            with pe.Fori(0, HP) as hp:
                pe.wait_ge(qkv_loaded.sem, qkv_loaded.ready(l, hp, 16))
                pe.wait_ge(a_biased.sem, a_biased.free(l, hp))
                for j in range(2):
                    nc.tensor.matmul(bank[j][:, :], PERM, q_of(j, hp), start=True, stop=True).then_inc(a_swap.sem, 1)
                pe.wait_ge(a_stage.sem, a_stage.ready(l, hp))
                for j in range(9):
                    src = VS[:, (j - 7) * P:(j - 6) * P] if j >= 7 else VS[:, CTX + VCOL0[j] * GR:CTX + VCOL0[j] * GR + P]
                    last = nc.tensor.transpose(bank[2 + j // 4][:, (j % 4) * P:(j % 4 + 1) * P], src, IDENT)
                last.then_inc(a_swap.sem, 1)
                pe.wait_ge(a_rot.sem, a_rot.ready(l, hp, 3))
                us = units(l)

                def scores(u):
                    g, e, lat = us[u]
                    sc = bank[SB[u % 3]]
                    if u >= 3:
                        pe.wait_ge(u_exp[l].sem, u_exp[l].ready(0, hp, u - 2))
                    if lat:
                        k0 = KEY0[3 - g] * GR
                        nc.tensor.matmul(sc[:, 0:256], QZ[:, e, 0, g * P:(g + 1) * P], KR[:, k0:k0 + 256], start=True, stop=True)
                        last = nc.tensor.matmul(sc[:, 256:512], QZ[:, e, 1, g * P:(g + 1) * P], q_of(1, hp, 0), start=True, stop=True)
                    else:
                        last = nc.tensor.matmul(sc[:, 256:512], QC[:, e, g * P:(g + 1) * P], q_of(1, hp, 0), start=True, stop=True)
                    last.then_inc(u_score[l].sem, 1)

                def weighted(u):
                    g, e, lat = us[u]
                    pe.wait_ge(u_trc[l].sem, u_trc[l].ready(0, hp, u + 1))
                    if e == 0 and u >= 4:
                        pe.wait_ge(u_oc[l].sem, u_oc[l].ready(0, hp, u // 2 - 1))
                    ob = bank[4 + (u // 2) % 2]
                    rows = slice(e * HD, (e + 1) * HD)
                    k0 = KEY0[3 - g] if lat else 0
                    kts = range(4) if lat else range(2, 4)
                    for kt in kts:
                        v = VA[:, 5 + kt, rows] if kt >= 2 else VA[:, VCOL0.index(k0 + 16 * kt), rows]
                        last = nc.tensor.matmul(ob[rows, 0:P], v, PT[u % 2][:, kt * P:(kt + 1) * P], start=(kt == kts[0]), stop=(kt == 3))
                    last.then_inc(u_out[l].sem, 1)

                for u in range(3):
                    scores(u)
                for u, (g, e, lat) in enumerate(us):
                    pe.wait_ge(u_prob[l].sem, u_prob[l].ready(0, hp, u + 1))
                    tb = bank[2 + u % 2]
                    if u >= 2:
                        pe.wait_ge(u_trc[l].sem, u_trc[l].ready(0, hp, u - 1))
                    for kt in (range(4) if lat else range(2, 4)):
                        last = nc.tensor.transpose(tb[:, kt * P:(kt + 1) * P], PX[u % 2][:, kt * P:(kt + 1) * P], IDENT)
                    last.then_inc(u_tr[l].sem, 1)
                    if u + 3 < len(us):
                        scores(u + 3)
                    if u >= 1:
                        weighted(u - 1)
                    if u == len(us) - 1:
                        weighted(u)
                    if l == 0 and u in (3, 7):
                        pe.wait_ge(late_copy.sem, late_copy.free(0, hp, 1 if u == 3 else 3))
                        for s in range(4):
                            wait_slab(pe, l, "late_ada", s, hp, u // 4)
                            ada_rows(s, bank[7][0:2, s * P:(s + 1) * P]).then_inc(slab_used[s], 1)
                        nc.tensor.drain().then_inc(late_prod.sem, 1)
                    if l == 0 and u in (5, 9):
                        pe.wait_ge(late_copy.sem, late_copy.ready(0, hp, u // 2 - 1))
                        ada_columns(AROW, 4, bank[7]).then_inc(late_prod.sem, 1)
                nc.tensor.drain()

        SCALE = HD ** -0.5

        def attn_act(act, l):
            act.wait_ge(a_clear, l + 1)
            with act.Fori(0, HP) as hp:
                act.wait_ge(qkv_loaded.sem, qkv_loaded.ready(l, hp, 16))
                nc.scalar.activation(VS[:, 0:CTX], q_of(2, hp, 0), ACT.Copy)
                nc.scalar.activation(col_major(VS[:, CTX:T]), tokens(q_of(2, hp)), ACT.Copy)
                for e in range(2):
                    rows = slice(e * HD, (e + 1) * HD)
                    nc.scalar.activation(col_major(QZ[rows, e, 1, :], True), tokens(q_of(0, hp)[rows]), ACT.Copy, scale=SCALE)
                    if l == 0:
                        nc.scalar.activation(QC[rows, e, :], q_of(0, hp, 0)[rows], ACT.Copy, scale=SCALE)
                act.drain().then_inc(a_stage.sem, 1)
                us = units(l)

                def probabilities(u):
                    g, e, lat = us[u]
                    act.wait_ge(u_max[l].sem, u_max[l].ready(0, hp, u + 1))
                    if u >= 3:
                        act.wait_ge(u_prob[l].sem, u_prob[l].ready(0, hp, u - 2))
                    lo = 0 if lat else 256
                    nc.scalar.activation(SX[u % 3][:, lo:512], bank[SB[u % 3]][:, lo:512], ACT.Exp, bias=SM[u % 3][:, 0:1], accum_out=SM[u % 3][:, 1:2])\
                      .then_inc(u_exp[l].sem, 1)

                probabilities(0)
                probabilities(1)
                for u, (g, e, lat) in enumerate(us):
                    if u + 2 < len(us):
                        probabilities(u + 2)
                    act.wait_ge(u_tr[l].sem, u_tr[l].ready(0, hp, u + 1))
                    if u >= 2:
                        act.wait_ge(u_out[l].sem, u_out[l].ready(0, hp, u - 1))
                    lo = 0 if lat else 256
                    nc.scalar.activation(PT[u % 2][:, lo:512], bank[2 + u % 2][:, lo:512], ACT.Copy).then_inc(u_trc[l].sem, 1)
                act.drain()

        def attn_dve(dve, l):
            for z in (QZ.rearrange("p e o q -> p (e o q)"), QC.rearrange("p e q -> p (e q)"), ZP):
                nc.vector.memset(z, 0.0)
            dve.drain().then_inc(a_clear, 1)
            dve.wait_ge(at_tables, 16 * (l + 1))
            dve.sem_inc(a_biased.sem, 1)
            if l == 0:
                dve.sem_inc(late_copy.sem, 1)
            with dve.Fori(0, HP) as hp:
                dve.wait_ge(qkv_loaded.sem, qkv_loaded.ready(l, hp, 16))
                for j in range(2):
                    scale = SCALE if j == 0 else 1.0
                    nc.vector.scalar_tensor_tensor(out=RT[0], in0=q_of(j, hp), scalar=scale, in1=COS, op0=ALU.mult, op1=ALU.mult)
                    dve.wait_ge(a_swap.sem, a_swap.ready(l, hp, j + 1))
                    nc.vector.scalar_tensor_tensor(out=RT[1], in0=bank[j][:, :], scalar=scale, in1=SIN, op0=ALU.mult, op1=ALU.mult)
                    dve.drain()
                    if j == 0:
                        for e in range(2):
                            rows = slice(e * HD, (e + 1) * HD)
                            nc.vector.tensor_tensor(col_major(QZ[rows, e, 0, :], True), tokens(RT[0][rows]), tokens(RT[1][rows]), ALU.add)
                    else:
                        nc.vector.tensor_tensor(col_major(KR), tokens(RT[0]), tokens(RT[1]), ALU.add)
                    dve.drain().then_inc(a_rot.sem, 1)
                dve.wait_ge(a_swap.sem, a_swap.ready(l, hp, 3))
                for j in range(3):
                    n = min(4, 9 - 4 * j)
                    last = nc.vector.tensor_copy(VA[:, 4 * j:4 * j + n, :].rearrange("p j c -> p (j c)"), bank[2 + j][:, 0:n * P])
                last.then_inc(a_rot.sem, 1)
                dve.wait_ge(a_bias.sem, a_bias.ready(l, hp))
                us = units(l)

                def maximum(u):
                    g, e, lat = us[u]
                    sc = bank[SB[u % 3]]
                    dve.wait_ge(u_score[l].sem, u_score[l].ready(0, hp, u + 1))
                    if lat:
                        nc.vector.tensor_tensor(sc[:, 0:256], sc[:, 0:256], BN[:, e, VARIANT[3 - g]].rearrange("p c r -> p (c r)"), ALU.add)
                        dve.drain()
                    nc.vector.reduce_max(SM[u % 3][:, 0:1], sc[:, 0 if lat else 256:512], AX, negate=True).then_inc(u_max[l].sem, 1)

                maximum(0)
                maximum(1)
                for u in range(len(us)):
                    if u + 2 < len(us):
                        maximum(u + 2)
                    finish(dve, l, hp, us, u)
                    if 1 <= u <= 5:
                        conv_step(dve, l, hp, u - 1)
                    if l == 0 and u in (4, 8):
                        dve.wait_ge(late_prod.sem, late_prod.ready(0, hp, u // 2 - 1))
                        nc.vector.tensor_copy(AROW[0:2, :], bank[7][0:2, :]).then_inc(late_copy.sem, 1)
                    if l == 0 and u in (6, 10):
                        dve.wait_ge(late_prod.sem, late_prod.ready(0, hp, u // 2 - 1))
                        add_bias(l, hp * 8 + (2 * KD + 4 * (u // 8)), 4, bank[7][:, 0:8]).then_inc(late_copy.sem, 1)
                dve.drain().then_inc(a_biased.sem, 1)

        def finish(dve, l, hp, us, u):
            g, e, lat = us[u]
            lo = 0 if lat else 256
            dve.wait_ge(u_exp[l].sem, u_exp[l].ready(0, hp, u + 1))
            nc.vector.reciprocal(SM[u % 3][:, 3:4], SM[u % 3][:, 1:2])
            dve.drain()
            if u >= 2:
                dve.wait_ge(u_tr[l].sem, u_tr[l].ready(0, hp, u - 1))
            nc.vector.tensor_scalar(PX[u % 2][:, lo:512], SX[u % 3][:, lo:512], SM[u % 3][:, 3:4], None, ALU.mult).then_inc(u_prob[l].sem, 1)
            if u % 2 == 1 and u >= 3:
                copy_out(dve, l, hp, us, u - 2)
            if u == len(us) - 1:
                copy_out(dve, l, hp, us, u)

        def copy_out(dve, l, hp, us, u):
            g, e, lat = us[u]
            dve.wait_ge(u_out[l].sem, u_out[l].ready(0, hp, u + 1))
            ob = bank[4 + (u // 2) % 2][:, 0:P]
            if lat:
                g0 = 3 - g
                dst = BR[:, 2, bass.ds(hp, 1), CTX:T].rearrange("p a (r c) -> p (a r) c", r=GR)[:, :, g0 * QCOLS:(g0 + 1) * QCOLS]
                src = ob[:, ::-1].rearrange("p (c r) -> p r c", r=GR)
            else:
                dst = BR[:, 2, bass.ds(hp, 1), g * P:(g + 1) * P].rearrange("p a t -> p (a t)")
                src = ob
            nc.vector.tensor_copy(dst, src).then_inc(u_oc[l].sem, 1)

        def load_bias(pool, l, hp):
            for e in range(2):
                for x in range(QCOLS):
                    off = a["rpb"][l, bass.ds(hp * (2 * RPB) + (RPB_PAD - 16 + e * RPB + x), 31 * (2 * GR - 1) + 17)]
                    pool.dma_start(BIAS[x * GR:(x + 1) * GR, e], bias_window(off)).then_inc(bias_load, 16)

        def load_qkv(pool, hp):
            pool.dma_start(QKV.rearrange("p (j h) t -> p j h t", h=HP)[:, :, bass.ds(hp, 1)].rearrange("p j a t -> p j (a t)"),
                           SIDE[bass.ds(hp, 1), :, 3:6].rearrange("a p j t -> p (a j) t")).then_inc(qkv_loaded.sem, 16)

        def load_conv(pool, hp):
            pool.dma_start(CT, SIDE[bass.ds(hp, 1), :, 0:3].rearrange("a p j t -> p (a j) t")).then_inc(conv_loaded.sem, 16)

        def attn_pool(pool, l):
            per = 2 * QCOLS * 16

            def body(hp, more):
                pool.wait_ge(bias_load, hp * per + (l * (HP + 1) + 1) * per)
                pool.wait_ge(a_biased.sem, a_biased.free(l, hp))
                for e in range(2):
                    for v, shift in enumerate((16, 8, 0)):
                        nc.gpsimd.tensor_tensor(BN[:, e, v], BIAS[:, e, :, shift:shift + KCOLS].rearrange("p r x -> p x r"),
                                                NEG[v].rearrange("p (c r) -> p c r", c=KCOLS), ALU.add)
                pool.drain().then_inc(a_bias.sem, 1)
                if more:
                    pool.wait_ge(qkv_loaded.sem, qkv_loaded.ready(l, hp, 16))
                    load_qkv(pool, hp + 1)
                    pool.wait_ge(conv_used.sem, conv_used.ready(l, hp))
                    load_conv(pool, hp + 1)

            with pool.Fori(0, HP - 1) as hp:
                body(hp, True)
            body(HP - 1, False)
            pool.wait_ge(bias_load, (l + 1) * (HP + 1) * per)

        def bias_window(ap):
            rows = ap[0:31 * (2 * GR - 1) + 17]
            return bass.AP(tensor=rows.tensor, offset=rows.offset, ap=[[31, GR], [31, GR], [1, BX]])

        mg = Carve(2 * WS0)
        MG = HX
        MG_HI, MG_LO = [x[:, :].rearrange("p (k t) -> p k t", k=KD) for x in (hx_lo, hx_r)]
        BR_HI, BR_LO = [x[:, :].rearrange("p (n k t) -> p n k t", n=3, k=HP) for x in (br_hi, br_lo)]
        GATE = [mg(3 * T).rearrange("p (n t) -> p n t", n=3) for _ in range(2)]
        MT = NTMP[0]
        W_HI, W_LO = [[w_parts[:, (2 * n + b) * 8 * P:(2 * n + b + 1) * 8 * P] for b in range(2)] for n in range(2)]
        NM = 6
        br_high = sem("branch_outputs_rounded")
        br_low = sem("branch_output_rests")
        m_high = Count(sem("merge_weights_rounded"), KD // 2, NM)
        m_low = Count(sem("merge_weight_rests"), KD // 2, NM)
        m_prod = Count(sem("merge_products"), KD // 2, NM, primed=2)
        m_load = [Count(sem(f"merge_gates_loaded_{b}"), KD // 2, 16) for b in range(2)]
        m_gate = Count(sem("merge_gates"), KD // 2, 2)
        m_used = Count(sem("merge_used"), KD // 2, NM, primed=NM)

        def merge_pe(pe, l):
            pe.sem_inc(m_prod.sem, 2)
            with pe.Fori(0, KD // 2) as i:
                for u in range(NM):
                    b, n = divmod(u, 3)
                    pe.wait_ge(br_low, 3 * HP * l + HP * (n + 1))
                    pe.wait_ge(m_low.sem, m_low.ready(l, i, u + 1))
                    if u >= 4:
                        pe.wait_ge(m_used.sem, m_used.ready(l, i, u - 3))
                    else:
                        pe.wait_ge(m_used.sem, m_used.free(l, i, u + 5 if u < 2 else u + 1))
                    for s in segs_of(l):
                        c0, c1 = SEGS[s]
                        for k in range(KM):
                            w = slice(k * P, (k + 1) * P)
                            _, last = split_products(pair(2 * (u % 4))[s], W_HI[u % 2][:, w], W_LO[u % 2][:, w], BR_HI[:, n, k, c0:c1], BR_LO[:, n, k, c0:c1],
                                                     k == 0, k == KM - 1)
                    last.then_inc(m_prod.sem, 1)

        def load_gates(sp, l, i, b):
            sp.wait_ge(m_used.sem, m_used.free(l, i, 3 * b + 3))
            lo = 0 if l == 0 else CTX
            sp.dma_start(GATE[b][:, :, lo:T], gates_dram.rearrange("(n k) p t -> p n k t", n=3)[:, :, bass.ds(i * 2 + b, 1), lo:T]
                         .rearrange("p n a t -> p n (a t)")).then_inc(m_load[b].sem, 16)

        def merge_act(act, l):
            lo = 0 if l == 0 else CTX
            for n in range(3):
                for k in range(HP):
                    nc.scalar.activation(BR_HI[:, n, k, lo:T], BR[:, n, k, lo:T], ACT.Copy).then_inc(br_high, 1)
            with act.Fori(0, KD // 2) as i:
                for b in range(2):
                    for u in range(3 * b, 3 * b + 3):
                        wait_slab(act, l, "merge", u % 3, i, b)
                        act.wait_ge(m_prod.sem, m_prod.ready(l, i, u - 1))
                        nc.scalar.activation(W_HI[u % 2][:, 0:KM * P], slots[u % 3][:, 0:KM * P], ACT.Copy).then_inc(m_high.sem, 1)
                        if u % 3 == 0:
                            act.wait_ge(m_load[b].sem, m_load[b].ready(l, i, 16))
                            nc.scalar.activation(GATE[b][:, :, lo:T], GATE[b][:, :, lo:T], ACT.Sigmoid).then_inc(m_gate.sem, 1)

        def merge_pool(pool, l):
            with pool.Fori(0, KD // 2) as i:
                for u in range(NM):
                    pool.wait_ge(m_high.sem, m_high.ready(l, i, u + 1))
                    nc.gpsimd.tensor_tensor(W_LO[u % 2][:, 0:KM * P], slots[u % 3][:, 0:KM * P], W_HI[u % 2][:, 0:KM * P], ALU.subtract).then_inc(m_low.sem, 1)
                    pool.drain().then_inc(slab_used[u % 3], 1)

        def merge_dve(dve, l):
            lo = 0 if l == 0 else CTX
            dve.sem_inc(m_used.sem, NM)
            for n in range(3):
                for k in range(HP):
                    dve.wait_ge(br_high, 3 * HP * l + n * HP + k + 1)
                    nc.vector.tensor_tensor(BR_LO[:, n, k, lo:T], BR[:, n, k, lo:T], BR_HI[:, n, k, lo:T], ALU.subtract).then_inc(br_low, 1)
            with dve.Fori(0, KD // 2) as i:
                for u in range(NM):
                    b, n = divmod(u, 3)
                    if n == 0:
                        dve.wait_ge(m_gate.sem, m_gate.ready(l, i, b + 1))
                    dve.wait_ge(m_prod.sem, m_prod.ready(l, i, u + 1))
                    dst = [MG[:, bass.ds(i * 2 + b, 1), c0:c1].rearrange("p a t -> p (a t)") for c0, c1 in SEGS]
                    for s in segs_of(l):
                        c0, c1 = SEGS[s]
                        last = nc.vector.tensor_tensor(dst[s] if n == 0 else MT[:, c0:c1], pair(2 * (u % 4))[s], GATE[b][:, n, c0:c1], ALU.mult)
                    last.then_inc(m_used.sem, 1)
                    if n:
                        dve.drain()
                        for s in segs_of(l):
                            c0, c1 = SEGS[s]
                            nc.vector.tensor_tensor(dst[s], dst[s], MT[:, c0:c1], ALU.add)
                        dve.drain()
                    if n == 2:
                        whole, high, rest = [x[:, bass.ds(i * 2 + b, 1), lo:T].rearrange("p a t -> p (a t)") for x in (MG, MG_HI, MG_LO)]
                        nc.vector.tensor_copy(high, whole)
                        dve.drain()
                        nc.vector.tensor_tensor(rest, whole, high, ALU.subtract)

        Y = arena[:, 0:KD * T].rearrange("p (k t) -> p k t", k=KD)
        y_high = Count(sem("out_weights_rounded"), 2, 4)
        y_low = Count(sem("out_weight_rests"), 2, 4)
        o_prod = Count(sem("out_products"), 2, 4, primed=2)
        o_copy = Count(sem("out_copied"), 2, 4, primed=4)

        def out_pe(pe, l):
            pe.sem_inc(o_prod.sem, 2)
            with pe.Fori(0, 2) as i:
                for t in range(4):
                    pe.wait_ge(y_low.sem, y_low.ready(l, i, t + 1))
                    pe.wait_ge(o_copy.sem, o_copy.free(l, i, t + 1))
                    for s in segs_of(l):
                        c0, c1 = SEGS[s]
                        for k in range(KD):
                            w = slice(k * P, (k + 1) * P)
                            _, last = split_products(pair(2 * t)[s], W_HI[t % 2][:, w], W_LO[t % 2][:, w], MG_HI[:, k, c0:c1], MG_LO[:, k, c0:c1], k == 0, k == KD - 1)
                    last.then_inc(o_prod.sem, 1)

        def out_act(act, l):
            act.sem_inc(o_copy.sem, 4)
            with act.Fori(0, 2) as i:
                for t in range(5):
                    if t < 4:
                        wait_slab(act, l, "out", t, i)
                        act.wait_ge(o_prod.sem, o_prod.ready(l, i, t - 1))
                        nc.scalar.activation(W_HI[t % 2], slots[t][:, :], ACT.Copy).then_inc(y_high.sem, 1)
                    if t >= 1:
                        act.wait_ge(o_prod.sem, o_prod.ready(l, i, t))
                        for s in segs_of(l):
                            last = nc.scalar.activation(Y[:, bass.ds(i * 4 + t - 1, 1), SEGS[s][0]:SEGS[s][1]].rearrange("p a t -> p (a t)"), pair(2 * t - 2)[s], ACT.Copy)
                        last.then_inc(o_copy.sem, 1)

        def out_pool(pool, l):
            with pool.Fori(0, 2) as i:
                for t in range(4):
                    pool.wait_ge(y_high.sem, y_high.ready(l, i, t + 1))
                    nc.gpsimd.tensor_tensor(W_LO[t % 2], slots[t][:, :], W_HI[t % 2], ALU.subtract).then_inc(y_low.sem, 1)
                    pool.drain().then_inc(slab_used[t], 1)

        ff = Carve(0)
        MID = ff(NJ * T).rearrange("p (j t) -> p j t", j=NJ)
        ff(2 * KD * T)
        HX_HI, HX_LO = [x[:, :].rearrange("p (k t) -> p k t", k=KD) for x in (hx_hi, hx_lo)]
        MID_HI, MID_LO = [[x[:, b * 2 * T:(b + 1) * 2 * T].rearrange("p (k t) -> p k t", k=2) for b in range(2)] for x in (hx_hi, hx_lo)]
        ff(4 * 8 * P)
        SL = [ff(T) for _ in range(2)]
        YF = HX
        f_high = Count(sem("ffn_weights_rounded"), NJ // 2, 4)
        f_low = Count(sem("ffn_weight_rests"), NJ // 2, 4)
        f_prod = Count(sem("ffn_products"), NJ // 2, 4, primed=2)
        f_silu = Count(sem("ffn_silu"), NJ // 2, 2)
        f_mid = Count(sem("ffn_mid"), NJ // 2, 2, primed=2)
        NS = NJ // 2
        o_high = sem("ffn_out_weights_rounded")
        o_low = sem("ffn_out_weight_rests")
        o_mid = sem("ffn_out_mid_split")
        o_used = sem("ffn_out_slab_multiplied")
        g_prod = sem("ffn_out_products")
        g_copy = sem("ffn_out_copied")

        def slab_no(l, h, m):
            return m + (2 * l + h) * NS

        def part(h, s):
            return (h + (s == 1)) % 2

        def ffn_pe(pe, l):
            segs = segs_of(l)
            pe.sem_inc(f_prod.sem, 2)
            if l == 0:
                pe.sem_inc(o_used, 2)
            with pe.Fori(0, NJ // 2) as i:
                for u in range(4):
                    if u % 2 == 0:
                        pe.wait_ge(f_mid.sem, f_mid.free(l, i, u // 2 + 1))
                    pe.wait_ge(f_low.sem, f_low.ready(l, i, u + 1))
                    for s in segs:
                        for k in range(KD):
                            c0, c1 = SEGS[s]
                            _, last = split_products(pair(2 * u)[s], W_HI[u % 2][:, k * P:(k + 1) * P], W_LO[u % 2][:, k * P:(k + 1) * P],
                                                  HX_HI[:, k, c0:c1], HX_LO[:, k, c0:c1], k == 0, k == KD - 1)
                    last.then_inc(f_prod.sem, 1)
            pe.wait_ge(f_mid.sem, f_mid.ready(l, NJ // 2 - 1, 2))

            def slab(h, m, s, idx):
                b, first, end = part(h, s), s == 0, isinstance(m, int) and m == NS - 1
                pe.wait_ge(o_low, slab_no(l, h, m) + 1)
                pe.wait_ge(o_mid, slab_no(l, h, m) + 1)
                for t in range(4):
                    if first and h == 1:
                        pe.wait_ge(g_copy, 8 * l + t + 1)
                    for k in range(2):
                        w = slice((k * 4 + t) * P, (k * 4 + t + 1) * P)
                        for seg in segs:
                            c0, c1 = SEGS[seg]
                            _, last = split_products(pair(2 * t)[seg], W_HI[b][:, w], W_LO[b][:, w], MID_HI[b][:, k, c0:c1], MID_LO[b][:, k, c0:c1],
                                                  first and k == 0, end and k == 1)
                    if end:
                        last.then_inc(g_prod, 1)
                if end:
                    nc.tensor.drain().then_inc(o_used, 1)
                else:
                    last.then_inc(o_used, 1)

            for h in range(2):
                each_out_slab(pe, h, slab)

        def ffn_act(act, l):
            with act.Fori(0, NJ // 2) as i:
                for t in range(2):
                    for u in (2 * t, 2 * t + 1):
                        wait_slab(act, l, "ffn_in", u, i)
                        act.wait_ge(f_prod.sem, f_prod.ready(l, i, u - 1))
                        nc.scalar.activation(W_HI[u % 2], slots[u][:, :], ACT.Copy).then_inc(f_high.sem, 1)
                    act.wait_ge(f_prod.sem, f_prod.ready(l, i, 2 * t + 1))
                    act.wait_ge(f_mid.sem, f_mid.free(l, i, t + 1))
                    for s in segs_of(l):
                        last = nc.scalar.activation(SL[t][:, SEGS[s][0]:SEGS[s][1]], pair(4 * t)[s], ACT.Silu)
                    last.then_inc(f_silu.sem, 1)

            def slab(h, m, s, idx):
                wait_slab(act, l, "ffn_out", s, h, idx)
                if h == 0 and s == 0:
                    act.wait_ge(f_prod.sem, f_prod.ready(l, NJ // 2 - 1, 4))
                act.wait_ge(o_used, slab_no(l, h, m) + 1)
                nc.scalar.activation(W_HI[part(h, s)], slots[s][:, :], ACT.Copy).then_inc(o_high, 1)

            def copy_half(h):
                for t in range(4):
                    act.wait_ge(g_prod, 8 * l + 4 * h + t + 1)
                    for s in segs_of(l):
                        last = nc.scalar.activation(YF[:, 4 * h + t, SEGS[s][0]:SEGS[s][1]], pair(2 * t)[s], ACT.Copy)
                    last.then_inc(g_copy, 1)

            each_out_slab(act, 0, slab)
            each_out_slab(act, 1, slab, lambda: copy_half(0))
            copy_half(1)

        def ffn_pool(pool, l):
            with pool.Fori(0, NJ // 2) as i:
                for u in range(4):
                    pool.wait_ge(f_high.sem, f_high.ready(l, i, u + 1))
                    nc.gpsimd.tensor_tensor(W_LO[u % 2], slots[u][:, :], W_HI[u % 2], ALU.subtract).then_inc(f_low.sem, 1)
                    pool.drain().then_inc(slab_used[u], 1)

            def slab(h, m, s, idx):
                pool.wait_ge(o_high, slab_no(l, h, m) + 1)
                nc.gpsimd.tensor_tensor(W_LO[part(h, s)], slots[s][:, :], W_HI[part(h, s)], ALU.subtract).then_inc(o_low, 1)
                pool.drain().then_inc(slab_used[s], 1)

            for h in range(2):
                each_out_slab(pool, h, slab)

        def ffn_dve(dve, l):
            lo = SEGS[segs_of(l)[0]][0]
            dve.sem_inc(f_mid.sem, 2)
            with dve.Fori(0, NJ // 2) as i:
                for t in range(2):
                    dve.wait_ge(f_silu.sem, f_silu.ready(l, i, t + 1))
                    dve.wait_ge(f_prod.sem, f_prod.ready(l, i, 2 * t + 2))
                    for s in segs_of(l):
                        c0, c1 = SEGS[s]
                        last = nc.vector.tensor_tensor(MID[:, bass.ds(i * 2 + t, 1), c0:c1].rearrange("p a t -> p (a t)"), pair(4 * t + 2)[s], SL[t][:, c0:c1], ALU.mult)
                    last.then_inc(f_mid.sem, 1)
            dve.drain()

            def slab(h, m, s, idx):
                b = part(h, s)
                dve.wait_ge(o_used, slab_no(l, h, m) + 1)
                src = MID[:, bass.ds(m * 2, 2), lo:T]
                nc.vector.tensor_copy(MID_HI[b][:, :, lo:T], src)
                dve.drain()
                nc.vector.tensor_tensor(MID_LO[b][:, :, lo:T], src, MID_HI[b][:, :, lo:T], ALU.subtract).then_inc(o_mid, 1)

            for h in range(2):
                each_out_slab(dve, h, slab)

        LOADS = 4
        blk = ctx.enter_context(nc.Block())
        res_src = lambda k: RES[:, k, :]
        y_src = lambda k: Y[:, k, :]
        yf_src = lambda k: YF[:, k, :]

        @blk.sync
        def _(sp):
            sync_program(sp)
            sp.wait_ge(phase_end, 4 * TOTAL_BARRIERS)
            sp.dma_start(a["out"].rearrange("p (k t) -> p k t", k=KD), RES[:, :, CTX:T]).then_inc(s_out, 16)
            sp.wait_ge(s_out, 16)

        @blk.tensor
        def _(pe):
            for s in range(4):
                pe.sem_inc(slab_used[s], 1)
            pe.wait_ge(s_load, 16 * LOADS)
            for l in range(DEPTH):
                if l == 0:
                    ada_pe(pe, l)
                phase_barrier(pe, "pe")
                if l == 0:
                    stats_pe(pe, 0, [0, 1])
                phase_barrier(pe, "pe")
                rwkv_pe(pe, l); phase_barrier(pe, "pe")
                attn_pe(pe, l); phase_barrier(pe, "pe")
                merge_pe(pe, l); phase_barrier(pe, "pe")
                out_pe(pe, l)
                pe.wait_ge(o_copy.sem, o_copy.ready(l, 1, 4))
                stats_pe(pe, 4 * l + 1, segs_of(l))
                stats_pe(pe, 4 * l + 2, segs_of(l)); phase_barrier(pe, "pe")
                phase_barrier(pe, "pe")
                ffn_pe(pe, l)
                pe.wait_ge(g_copy, 8 * l + 8)
                stats_pe(pe, 4 * l + 3, segs_of(l))
                if l < DEPTH - 1:
                    stats_pe(pe, 4 * l + 4, [0, 1])
                phase_barrier(pe, "pe")

        @blk.scalar
        def _(act):
            act.wait_ge(s_load, 16 * LOADS)
            nc.scalar.activation(cin[:, :], cin[:, :], ACT.Silu).then_inc(silu_done, 1)
            for l in range(DEPTH):
                phase_barrier(act, "act")
                if l == 0:
                    stats_act(act, 0, res_src, [0, 1])
                norm_act(act, 2 * l, 0, [0, 1]); phase_barrier(act, "act")
                rwkv_act(act, l); phase_barrier(act, "act")
                attn_act(act, l); phase_barrier(act, "act")
                merge_act(act, l); phase_barrier(act, "act")
                out_act(act, l)
                act.drain()
                stats_act(act, 4 * l + 1, y_src, segs_of(l))
                stats_act(act, 4 * l + 2, res_src, segs_of(l), after=2 * l); phase_barrier(act, "act")
                norm_act(act, 2 * l + 1, 1, segs_of(l)); phase_barrier(act, "act")
                ffn_act(act, l)
                act.drain()
                stats_act(act, 4 * l + 3, yf_src, segs_of(l))
                if l < DEPTH - 1:
                    stats_act(act, 4 * l + 4, res_src, [0, 1], after=2 * l + 1)
                phase_barrier(act, "act")

        @blk.vector
        def _(dve):
            nc.vector.memset(one[:, 0:1], EPS)
            nc.vector.memset(one[:, 1:2], LN_EPS)
            nc.vector.memset(one[:, 2:4], 1.0)
            dve.wait_ge(s_load, 16 * LOADS)
            for l in range(DEPTH):
                ada_dve(dve, l); phase_barrier(dve, "dve")
                norm_dve(dve, 2 * l, 0, [0, 1]); phase_barrier(dve, "dve")
                rwkv_dve(dve, l); phase_barrier(dve, "dve")
                attn_dve(dve, l)
                if l == 0:
                    dve.drain()
                    scales(dve, l, range(1, 4))
                phase_barrier(dve, "dve")
                merge_dve(dve, l); phase_barrier(dve, "dve")
                add_dve(dve, 2 * l, 0, segs_of(l), Y); phase_barrier(dve, "dve")
                norm_dve(dve, 2 * l + 1, 1, segs_of(l)); phase_barrier(dve, "dve")
                ffn_dve(dve, l)
                add_dve(dve, 2 * l + 1, 1, segs_of(l), YF); phase_barrier(dve, "dve")

        @blk.gpsimd
        def _(pool):
            for dst, name in ((glob, "glob"), (cin, "cin"), (resid, "x"), (bada, "b_ada")):
                pool.dma_start(dst[:, :], a[name]).then_inc(s_load, 16)
            for l in range(DEPTH):
                pool.dma_start(vec[:, :], a["vec"][l, :, :]).then_inc(s_wload, 16)
                phase_barrier(pool, "pool")
                if l:
                    pool.dma_start(a["resid_dram"], resid[:, :]).then_inc(resid_kept, 16)
                    pool.wait_ge(resid_kept, 16)
                norm_pool(pool, 2 * l, 0, [0, 1]); phase_barrier(pool, "pool")
                pool.dma_start(RC, a["rwkv_tables"]).then_inc(rw_tables, 16)
                split_pool(pool, l)
                pool.wait_ge(spilled.sem, spilled.ready(l, HP, 0))
                phase_barrier(pool, "pool")
                load_qkv(pool, 0)
                pool.dma_start(AC, a["attn_tables"]).then_inc(at_tables, 16)
                pool.dma_start(resid[:, :], a["resid_dram"] if l else a["x"]).then_inc(resid_back, 16)
                load_conv(pool, 0)
                pool.wait_ge(at_tables, 16 * (l + 1))
                attn_pool(pool, l)
                phase_barrier(pool, "pool")
                merge_pool(pool, l); phase_barrier(pool, "pool")
                out_pool(pool, l); phase_barrier(pool, "pool")
                norm_pool(pool, 2 * l + 1, 1, segs_of(l)); phase_barrier(pool, "pool")
                ffn_pool(pool, l); phase_barrier(pool, "pool")


def arrays():
    return {
        "glob": (P, 4 * P), "rwkv_tables": (P, 512 + 12 * P + 2 * T), "attn_tables": (P, 2 * SEQ + 768),
        "x": (P, KD * T), "cin": (P, KD * 2), "b_ada": (P, DEPTH * NADA), "vec": (DEPTH, P, NV), "rpb": (DEPTH, 2 * RPB_PAD + 10 * RPB),
        "w_ada": (DEPTH, NADA, P, 8 * P), "w_lora": (DEPTH, 2, P, 8 * P), "w_heads": (DEPTH, 4 * HP, P, 8 * P),
        "w_gate": (DEPTH, 3 * KD, P, 8 * P), "w_side": (DEPTH, 6 * HP, P, 8 * P), "w_up": (DEPTH, 3 * KD, P, KM * P),
        "w_out": (DEPTH, KD, P, 8 * P), "w_ffn_in": (DEPTH, 2 * NJ, P, 8 * P), "w_ffn_out": (DEPTH, NJ, P, 8 * P),
    }


def layout(x, c, ctx, c_ctx, w_ada, b_ada, norm_g, w_in, conv_w, rwkv_mu, rwkv_w0, rwkv_w2, rwkv_a0, rwkv_a2,
           rwkv_kk, rwkv_ka, rwkv_rk, rwkv_g2, lnx_g, lnx_b, na_rpb, w_up, w_o, w_ffn_in, w_ffn_out):
    out = dict(zip(("glob", "rwkv_tables", "attn_tables"), constants()))

    def chan(v):
        v = np.asarray(v)
        return np.moveaxis(v.reshape(v.shape[:-1] + (-1, P)), -1, 0).reshape(P, -1)

    tok = np.concatenate([ctx[0], x[0]], 0)
    out["x"] = np.ascontiguousarray(tok.T.reshape(KD, P, T).transpose(1, 0, 2)).reshape(P, KD * T)
    out["cin"] = np.stack([c_ctx.reshape(KD, P).T, c[0].reshape(KD, P).T], 2).reshape(P, KD * 2)
    zero = np.zeros((P, P), np.float32)
    vecs, rpbs = [], []
    streams = {k: [] for k in arrays() if k.startswith("w_")}
    for l in range(DEPTH):
        mu = rwkv_mu[l]
        vecs.append(np.concatenate([
            chan(norm_g[l]), chan(conv_w[l]), chan(mu[:, 0:3 * MIX].reshape(2, 3, MIX)), chan(mu[:, 3 * MIX:]),
            chan(rwkv_w0[l]), chan(rwkv_a0[l]), chan(rwkv_kk[l]), chan(rwkv_ka[l]), chan(rwkv_rk[l].reshape(MIX)),
            chan(lnx_g[l]), chan(lnx_b[l])], 1))
        rpbs.append(np.pad(na_rpb[l].reshape(-1), (RPB_PAD, RPB_PAD + 2 * RPB)))

        def blocks(w):
            k, n = w.shape
            return w.reshape(k // P, P, n // P, P).transpose(2, 0, 1, 3)

        def slabs(name, bl):
            n, cols = arrays()[name][1], arrays()[name][3] // P
            bl = np.asarray(bl).reshape(n, cols, P, P)
            streams[name].append(bl.transpose(0, 2, 1, 3).reshape(n, P, cols * P))

        ada, win = blocks(w_ada[l]), blocks(w_in[l])
        cv, rk, lo, lg, qt, gt = win[0:12], win[12:24], win[24:25], win[25:26], win[26:38], win[38:62]
        slabs("w_ada", ada)
        slabs("w_lora", [lo[0], lg[0]])
        w2a2 = np.concatenate([rwkv_w2[l], rwkv_a2[l]], 1)
        heads = []
        for i in range(HP):
            cs = slice(i * P, (i + 1) * P)
            heads += [b for t in range(3) for b in rk[t * HP + i]]
            heads += [w2a2[0][:, cs], w2a2[1][:, cs], rwkv_g2[l][:, cs]] + [zero] * 5
        slabs("w_heads", heads)
        slabs("w_gate", gt)
        slabs("w_side", [t for part in (cv, qt) for t in part])
        up = [blocks(w_up[l, n]) for n in range(3)]
        slabs("w_up", [up[n][i] for i in range(KD) for n in range(3)])
        slabs("w_out", blocks(w_o[l]))
        fi = blocks(w_ffn_in[l])
        slabs("w_ffn_in", [fi[t] for j in range(NJ) for t in (j, NJ + j)])
        fo = blocks(w_ffn_out[l])
        slabs("w_ffn_out", [fo[4 * h + t][2 * m + k] for h in range(2) for m in range(NJ // 2) for k in range(2) for t in range(4)])
    out["b_ada"] = chan(b_ada)
    out["vec"] = np.stack(vecs)
    out["rpb"] = np.stack(rpbs)
    for k, v in streams.items():
        out[k] = np.stack(v)
    for k, shape in arrays().items():
        assert out[k].shape == shape, (k, out[k].shape, shape)
        out[k] = np.ascontiguousarray(out[k])
    return out


def build(nc):
    F = mybir.dt.float32
    a = {}
    for name, shape in arrays().items():
        a[name] = nc.dram_tensor("in_" + name, list(shape), F, kind="ExternalInput").ap()
    a["side_dram"] = nc.dram_tensor("side_projections", [6 * HP, P, T], F, kind="Internal").ap()
    a["gates_dram"] = nc.dram_tensor("gate_projections", [3 * KD, P, T], F, kind="Internal").ap()
    a["resid_dram"] = nc.dram_tensor("residual_kept", [P, KD * T], F, kind="Internal").ap()
    a["out"] = nc.dram_tensor("out", [P, KD * SEQ], F, kind="ExternalOutput").ap()
    return a


def kernel(**inputs):
    import concourse.bacc as bacc
    from concourse.bass_utils import run_bass_kernel_spmd

    nc = bacc.Bacc("TRN2", target_bir_lowering=False, num_devices=1)
    a = build(nc)
    program(nc, a)
    got = run_bass_kernel_spmd(nc, [{"in_" + k: v for k, v in layout(**{k: np.asarray(v) for k, v in inputs.items()}).items()}], core_ids=[0])
    y = got.results[0]["out"].reshape(P, KD, SEQ)
    return np.ascontiguousarray(y.transpose(2, 1, 0).reshape(1, SEQ, D))
```
